# Optimizing a Trainium2 kernel written in Bass

```python
import jax, jax.numpy as jnp
from jax import lax
import numpy as np
import math

D_MODEL = 1024
BATCH = 1
SEQ = 512
DEPTH = 2

CHUNK = 64
N_MIXERS = 2
HEAD_SIZE = 64
N_HEADS = D_MODEL // HEAD_SIZE
D_FF = 4 * D_MODEL
CONV_WIDTH = 3
D_DECAY_LORA = 64
D_AAA_LORA = 64
D_MV_LORA = 32
D_GATE_LORA = 160
N_CONV_LAYERS = (DEPTH + 1) // 2
N_RWKV_LAYERS = DEPTH // 2
N_VRES = max(N_RWKV_LAYERS - 1, 0)
N_MOD = 6
NORM_EPS = 1e-6
GN_EPS = 64e-5


def _rmsnorm(x, g):
    x32 = x.astype(jnp.float32)
    y = x32 * lax.rsqrt(jnp.mean(x32 * x32, axis=-1, keepdims=True) + NORM_EPS)
    return (y * g.astype(jnp.float32)).astype(x.dtype)

def _modulate(h, shift, scale):
    return h * (1 + scale[:, None, :]) + shift[:, None, :]

def _short_conv_mixer(h, w_in, conv_w, w_out):
    bch = h @ w_in
    b_gate, c_gate, hv = jnp.split(bch, 3, axis=-1)
    u = c_gate * hv
    conv = lax.conv_general_dilated(
        u, conv_w[:, None, :], window_strides=(1,),
        padding=[(CONV_WIDTH - 1, 0)],
        dimension_numbers=('NWC', 'WIO', 'NWC'),
        feature_group_count=D_MODEL)
    return (b_gate * conv) @ w_out

def _wkv7_scan(r, w, k, v, a, b):
    bsz, seq = r.shape[0], r.shape[1]

    def to_chunks(t):
        return t.transpose(1, 0, 2, 3).reshape(seq // CHUNK, CHUNK, bsz, N_HEADS, HEAD_SIZE)

    def frame_step(state, inp):
        r_t, w_t, k_t, v_t, a_t, b_t = inp
        sa = jnp.einsum('bhvk,bhk->bhv', state, a_t)
        state = (state * w_t[:, :, None, :]
                 + sa[..., None] * b_t[:, :, None, :]
                 + v_t[..., None] * k_t[:, :, None, :])
        y_t = jnp.einsum('bhvk,bhk->bhv', state, r_t)
        return state, y_t

    def chunk_step(state, inp_chunk):
        return lax.scan(frame_step, state, inp_chunk)

    s0 = jnp.zeros((bsz, N_HEADS, HEAD_SIZE, HEAD_SIZE), jnp.float32)
    inputs = (to_chunks(r), to_chunks(w), to_chunks(k), to_chunks(v), to_chunks(a), to_chunks(b))
    _, y = lax.scan(chunk_step, s0, inputs)
    return y.reshape(seq, bsz, N_HEADS, HEAD_SIZE).transpose(1, 0, 2, 3)

def _rwkv7_mixer(h, v_first, vres, mu, w_rkv, w_o, w0, w1, w2, a0, a1, a2,
                 g1, g2, k_k, k_a, r_k, ln_w, ln_b):
    bsz, seq, d = h.shape
    h_prev = jnp.pad(h, ((0, 0), (1, 0), (0, 0)))[:, :-1]
    xx = h_prev - h
    xr, xw, xk, xv, xa, xg = h[None] + xx[None] * mu[:, None, None, :]
    r, k, v = jnp.einsum('nbsd,nde->nbse', jnp.stack([xr, xk, xv]), w_rkv)
    w = -jax.nn.softplus(-(w0 + jnp.tanh(xw @ w1) @ w2)) - 0.5
    a = jax.nn.sigmoid(a0 + (xa @ a1) @ a2)
    g = jax.nn.sigmoid(xg @ g1) @ g2
    if vres is None:
        v_first = v
    else:
        v0, v1, v2 = vres
        v = v + (v_first - v) * jax.nn.sigmoid(v0 + (xv @ v1) @ v2)

    def heads(t):
        return t.reshape(bsz, seq, N_HEADS, HEAD_SIZE).astype(jnp.float32)

    kk = heads(k * k_k)
    kk = kk / jnp.maximum(jnp.sqrt(jnp.sum(kk * kk, axis=-1, keepdims=True)), 1e-12)
    k = k * (1 + (a - 1) * k_a)
    rh, kh, vh, ah = heads(r), heads(k), heads(v), heads(a)
    decay = jnp.exp(-jnp.exp(heads(w)))
    y = _wkv7_scan(rh, decay, kh, vh, -kk, kk * ah)
    mean = jnp.mean(y, axis=-1, keepdims=True)
    var = jnp.mean(jnp.square(y - mean), axis=-1, keepdims=True)
    y = (y - mean) * lax.rsqrt(var + GN_EPS)
    y = y * ln_w.reshape(N_HEADS, HEAD_SIZE) + ln_b.reshape(N_HEADS, HEAD_SIZE)
    bonus = jnp.sum(rh * kh * r_k, axis=-1, keepdims=True) * vh
    out = ((y + bonus).reshape(bsz, seq, d).astype(h.dtype) * g) @ w_o
    return out, v_first

def first_inputs(seed: int = 0) -> dict:
    key = jax.random.key(seed)
    ks = iter(jax.random.split(key, 40))
    D = D_MODEL
    nrm = lambda shape, s: jax.random.normal(next(ks), shape, jnp.float32) * s
    uni = lambda shape, lo, hi: jax.random.uniform(next(ks), shape, jnp.float32, lo, hi)
    NC, NR, NV = N_CONV_LAYERS, N_RWKV_LAYERS, N_VRES
    return {
        "x": nrm((BATCH, SEQ, D), 1.0),
        "c": nrm((BATCH, D), 1.0),
        "norm_g": 1.0 + nrm((DEPTH, 2, D), 0.05),
        "final_g": 1.0 + nrm((D,), 0.05),
        "ada_w": nrm((DEPTH, D, N_MOD * D), 0.5 * D ** -0.5),
        "ada_b": nrm((DEPTH, N_MOD * D), 0.02),
        "conv_w_in": nrm((NC, D, 3 * D), D ** -0.5),
        "conv_w": nrm((NC, CONV_WIDTH, D), CONV_WIDTH ** -0.5),
        "conv_w_out": nrm((NC, D, D), D ** -0.5),
        "rw_mu": uni((NR, 6, D), 0.0, 1.0),
        "rw_w_rkv": nrm((NR, 3, D, D), D ** -0.5),
        "rw_w_o": nrm((NR, D, D), D ** -0.5),
        "rw_w0": uni((NR, D), -6.5, -1.5),
        "rw_w1": nrm((NR, D, D_DECAY_LORA), D ** -0.5),
        "rw_w2": nrm((NR, D_DECAY_LORA, D), 0.1 * D_DECAY_LORA ** -0.5),
        "rw_a0": nrm((NR, D), 0.1),
        "rw_a1": nrm((NR, D, D_AAA_LORA), D ** -0.5),
        "rw_a2": nrm((NR, D_AAA_LORA, D), 0.1 * D_AAA_LORA ** -0.5),
        "rw_g1": nrm((NR, D, D_GATE_LORA), D ** -0.5),
        "rw_g2": nrm((NR, D_GATE_LORA, D), D_GATE_LORA ** -0.5),
        "rw_k_k": 0.85 + nrm((NR, D), 0.05),
        "rw_k_a": 1.0 + nrm((NR, D), 0.05),
        "rw_r_k": nrm((NR, N_HEADS, HEAD_SIZE), 0.1),
        "rw_ln_w": 1.0 + nrm((NR, D), 0.05),
        "rw_ln_b": nrm((NR, D), 0.02),
        "rw_v0": 1.0 + nrm((NV, D), 0.1),
        "rw_v1": nrm((NV, D, D_MV_LORA), D ** -0.5),
        "rw_v2": nrm((NV, D_MV_LORA, D), 0.1 * D_MV_LORA ** -0.5),
        "mlp_w1": nrm((DEPTH, D, D_FF), D ** -0.5),
        "mlp_w2": nrm((DEPTH, D_FF, D), D_FF ** -0.5),
    }

def first_block(x, c, norm_g, final_g, ada_w, ada_b, conv_w_in, conv_w, conv_w_out,
              rw_mu, rw_w_rkv, rw_w_o, rw_w0, rw_w1, rw_w2, rw_a0, rw_a1, rw_a2,
              rw_g1, rw_g2, rw_k_k, rw_k_a, rw_r_k, rw_ln_w, rw_ln_b,
              rw_v0, rw_v1, rw_v2, mlp_w1, mlp_w2):
    c_act = jax.nn.silu(c)
    v_first = None
    for i in range(DEPTH):
        mod = c_act @ ada_w[i] + ada_b[i]
        sh1, sc1, gt1, sh2, sc2, gt2 = jnp.split(mod, N_MOD, axis=-1)
        h = _modulate(_rmsnorm(x, norm_g[i, 0]), sh1, sc1)
        j = i // N_MIXERS
        if i % N_MIXERS == 0:
            y = _short_conv_mixer(h, conv_w_in[j], conv_w[j], conv_w_out[j])
        else:
            vres = None if v_first is None else (rw_v0[j - 1], rw_v1[j - 1], rw_v2[j - 1])
            y, v_first = _rwkv7_mixer(
                h, v_first, vres, rw_mu[j], rw_w_rkv[j], rw_w_o[j], rw_w0[j], rw_w1[j],
                rw_w2[j], rw_a0[j], rw_a1[j], rw_a2[j], rw_g1[j], rw_g2[j], rw_k_k[j],
                rw_k_a[j], rw_r_k[j], rw_ln_w[j], rw_ln_b[j])
        x = x + gt1[:, None, :] * y
        h = _modulate(_rmsnorm(x, norm_g[i, 1]), sh2, sc2)
        x = x + gt2[:, None, :] * (jnp.square(jax.nn.relu(h @ mlp_w1[i])) @ mlp_w2[i])
    return _rmsnorm(x, final_g)


DEPTH_2 = 1

N_MEM = 256
RET_HEADS = 4
RET_DV = D_MODEL // 2 // RET_HEADS
RET_DK = RET_DV // 2
RET_QK_W = RET_HEADS * RET_DK
RET_V_W = RET_HEADS * RET_DV
DIFF_HEADS = 4
DIFF_DH = D_MODEL // 2 // DIFF_HEADS // 2
DIFF_DV = 2 * DIFF_DH
DIFF_QK_W = DIFF_HEADS * 2 * DIFF_DH
DIFF_V_W = DIFF_HEADS * DIFF_DV
MIX_W = RET_V_W + DIFF_V_W
IN_COLS = 2 * RET_QK_W + 2 * RET_V_W + 2 * DIFF_QK_W + DIFF_V_W
XATTN_HEADS = 4
XATTN_DH = D_MODEL // XATTN_HEADS
D_FF_2 = ((8 * D_MODEL // 3 + 127) // 128) * 128
RET_CHUNK = 128
Q_BLOCK = 128
ROPE_BASE = 10000.0
EPS = 1e-6


def rmsnorm(x, g):
    xf = x.astype(jnp.float32)
    y = xf * lax.rsqrt(jnp.mean(xf * xf, axis=-1, keepdims=True) + EPS)
    return (y * g.astype(jnp.float32)).astype(x.dtype)

def swiglu(h, w_gate, w_up, w_down):
    return (jax.nn.silu(h @ w_gate) * (h @ w_up)) @ w_down

def rotary(t, pos):
    d = t.shape[-1]
    inv = 1.0 / (ROPE_BASE ** (jnp.arange(0, d, 2, dtype=jnp.float32) / d))
    ang = pos.astype(jnp.float32)[:, None] * inv[None, :]
    cos = jnp.cos(ang)[None, :, None, :].astype(t.dtype)
    sin = jnp.sin(ang)[None, :, None, :].astype(t.dtype)
    t1, t2 = t[..., : d // 2], t[..., d // 2:]
    return jnp.concatenate([t1 * cos - t2 * sin, t1 * sin + t2 * cos], axis=-1)

def retention_chunkwise(q, k, v):
    B, S, H, dk = q.shape
    dv = v.shape[-1]
    C = RET_CHUNK
    NC = S // C
    log_g = jnp.log(1.0 - 2.0 ** (-5.0 - jnp.arange(H, dtype=jnp.float32)))
    n = jnp.arange(C, dtype=jnp.float32)
    rel = n[:, None] - n[None, :]
    decay = jnp.where(rel[None] >= 0, jnp.exp(jnp.maximum(rel, 0.0)[None] * log_g[:, None, None]), 0.0)
    xi = jnp.exp((n[None, :] + 1.0) * log_g[:, None])
    zeta = jnp.exp((C - 1.0 - n[None, :]) * log_g[:, None])
    g_chunk = jnp.exp(C * log_g)

    def to_chunks(t):
        return t.astype(jnp.float32).reshape(B, NC, C, H, t.shape[-1]).transpose(1, 0, 3, 2, 4)

    qc, kc, vc = to_chunks(q), to_chunks(k), to_chunks(v)

    def step(R, inp):
        qi, ki, vi = inp
        inner = jnp.einsum('bhnd,bhmd->bhnm', qi, ki) * decay[None]
        o = jnp.einsum('bhnm,bhme->bhne', inner, vi)
        o = o + jnp.einsum('bhnd,bhde->bhne', qi, R) * xi[None, :, :, None]
        R = g_chunk[None, :, None, None] * R + jnp.einsum('bhmd,bhme->bhde', ki * zeta[None, :, :, None], vi)
        return R, o

    R0 = jnp.zeros((B, H, dk, dv), jnp.float32)
    _, out = lax.scan(step, R0, (qc, kc, vc))
    return out.transpose(1, 0, 3, 2, 4).reshape(B, S, H, dv)

def diff_attention(q, k, v, lam):
    B, S, H, _, dh = q.shape
    NB = S // Q_BLOCK
    scale = 1.0 / math.sqrt(dh)
    qb = q.reshape(B, NB, Q_BLOCK, H, 2, dh).transpose(1, 0, 2, 3, 4, 5)
    kpos = jnp.arange(S)

    def block(args):
        qi, i = args
        s = jnp.einsum('bqhcd,bkhcd->bhcqk', qi, k).astype(jnp.float32) * scale
        qpos = i * Q_BLOCK + jnp.arange(Q_BLOCK)
        mask = kpos[None, :] <= qpos[:, None]
        s = jnp.where(mask[None, None, None], s, -jnp.inf)
        p = jax.nn.softmax(s, axis=-1)
        a = p[:, :, 0] - lam * p[:, :, 1]
        return jnp.einsum('bhqk,bkhe->bqhe', a.astype(v.dtype), v)

    out = lax.map(block, (qb, jnp.arange(NB)))
    return out.transpose(1, 0, 2, 3, 4).reshape(B, S, H, v.shape[-1])

def memory_cross_attention(h, m, wq, wkv, wo):
    B, S, _ = h.shape
    M = m.shape[1]
    q = (h @ wq).reshape(B, S, XATTN_HEADS, XATTN_DH)
    kv = m @ wkv
    k = kv[..., :D_MODEL].reshape(B, M, XATTN_HEADS, XATTN_DH)
    v = kv[..., D_MODEL:].reshape(B, M, XATTN_HEADS, XATTN_DH)
    s = jnp.einsum('bshd,bmhd->bhsm', q, k).astype(jnp.float32) / math.sqrt(XATTN_DH)
    p = jax.nn.softmax(s, axis=-1).astype(v.dtype)
    o = jnp.einsum('bhsm,bmhd->bshd', p, v).reshape(B, S, D_MODEL)
    return o @ wo

def second_inputs(seed: int = 0) -> dict:
    key = jax.random.key(seed)
    ks = jax.random.split(key, 32)
    f32 = jnp.float32

    def w(k, shape, fan_in):
        return jax.random.normal(k, shape, f32) * (fan_in ** -0.5)

    def gain(k, shape):
        return 1.0 + 0.02 * jax.random.normal(k, shape, f32)

    L = DEPTH_2
    return {
        "x": jax.random.normal(ks[0], (BATCH, SEQ, D_MODEL), f32),
        "mem": jax.random.normal(ks[1], (BATCH, N_MEM, D_MODEL), f32),
        "ffn1_norm": gain(ks[2], (L, D_MODEL)),
        "ffn1_w_gate": w(ks[3], (L, D_MODEL, D_FF_2), D_MODEL),
        "ffn1_w_up": w(ks[4], (L, D_MODEL, D_FF_2), D_MODEL),
        "ffn1_w_down": w(ks[5], (L, D_FF_2, D_MODEL), D_FF_2),
        "mix_norm": gain(ks[6], (L, D_MODEL)),
        "w_in": w(ks[7], (L, D_MODEL, IN_COLS), D_MODEL),
        "ret_out_norm": gain(ks[8], (L, RET_HEADS, RET_DV)),
        "diff_lq1": 0.1 * jax.random.normal(ks[9], (L, DIFF_DH), f32),
        "diff_lk1": 0.1 * jax.random.normal(ks[10], (L, DIFF_DH), f32),
        "diff_lq2": 0.1 * jax.random.normal(ks[11], (L, DIFF_DH), f32),
        "diff_lk2": 0.1 * jax.random.normal(ks[12], (L, DIFF_DH), f32),
        "diff_out_norm": gain(ks[13], (L, DIFF_HEADS, DIFF_DV)),
        "w_out": w(ks[14], (L, MIX_W, D_MODEL), MIX_W),
        "xattn_norm": gain(ks[15], (L, D_MODEL)),
        "mem_norm": gain(ks[16], (L, D_MODEL)),
        "xattn_wq": w(ks[17], (L, D_MODEL, D_MODEL), D_MODEL),
        "xattn_wkv": w(ks[18], (L, D_MODEL, 2 * D_MODEL), D_MODEL),
        "xattn_wo": w(ks[19], (L, D_MODEL, D_MODEL), D_MODEL),
        "ffn2_norm": gain(ks[20], (L, D_MODEL)),
        "ffn2_w_gate": w(ks[21], (L, D_MODEL, D_FF_2), D_MODEL),
        "ffn2_w_up": w(ks[22], (L, D_MODEL, D_FF_2), D_MODEL),
        "ffn2_w_down": w(ks[23], (L, D_FF_2, D_MODEL), D_FF_2),
        "final_norm": gain(ks[24], (D_MODEL,)),
    }

def second_block(x, mem, ffn1_norm, ffn1_w_gate, ffn1_w_up, ffn1_w_down, mix_norm, w_in,
              ret_out_norm, diff_lq1, diff_lk1, diff_lq2, diff_lk2, diff_out_norm, w_out,
              xattn_norm, mem_norm, xattn_wq, xattn_wkv, xattn_wo,
              ffn2_norm, ffn2_w_gate, ffn2_w_up, ffn2_w_down, final_norm):
    B, S, _ = x.shape
    pos = jnp.arange(S)
    split_at = np.cumsum([RET_QK_W, RET_QK_W, RET_V_W, RET_V_W, DIFF_QK_W, DIFF_QK_W]).tolist()
    for l in range(DEPTH_2):
        x = x + 0.5 * swiglu(rmsnorm(x, ffn1_norm[l]), ffn1_w_gate[l], ffn1_w_up[l], ffn1_w_down[l])

        h = rmsnorm(x, mix_norm[l])
        p = h @ w_in[l]
        rq, rk, rv, rg, dq, dk, dv = jnp.split(p, split_at, axis=-1)

        rq = rotary(rq.reshape(B, S, RET_HEADS, RET_DK), pos)
        rk = rotary(rk.reshape(B, S, RET_HEADS, RET_DK), pos) * (RET_DK ** -0.5)
        rv = rv.reshape(B, S, RET_HEADS, RET_DV)
        y_ret = retention_chunkwise(rq, rk, rv).astype(x.dtype)
        y_ret = rmsnorm(y_ret, ret_out_norm[l]).reshape(B, S, RET_V_W) * jax.nn.silu(rg)

        lambda_init = 0.8 - 0.6 * math.exp(-0.3 * l)
        lam = (jnp.exp(jnp.sum(diff_lq1[l].astype(jnp.float32) * diff_lk1[l].astype(jnp.float32)))
               - jnp.exp(jnp.sum(diff_lq2[l].astype(jnp.float32) * diff_lk2[l].astype(jnp.float32)))
               + lambda_init)
        dq = dq.reshape(B, S, DIFF_HEADS, 2, DIFF_DH)
        dk = dk.reshape(B, S, DIFF_HEADS, 2, DIFF_DH)
        dv = dv.reshape(B, S, DIFF_HEADS, DIFF_DV)
        y_diff = diff_attention(dq, dk, dv, lam)
        y_diff = (rmsnorm(y_diff, diff_out_norm[l]) * (1.0 - lambda_init)).reshape(B, S, DIFF_V_W)

        x = x + jnp.concatenate([y_ret, y_diff], axis=-1) @ w_out[l]

        x = x + memory_cross_attention(rmsnorm(x, xattn_norm[l]), rmsnorm(mem, mem_norm[l]),
                                       xattn_wq[l], xattn_wkv[l], xattn_wo[l])

        x = x + 0.5 * swiglu(rmsnorm(x, ffn2_norm[l]), ffn2_w_gate[l], ffn2_w_up[l], ffn2_w_down[l])
    return rmsnorm(x, final_norm)


def setup_inputs(seed=0):
    out = dict(first_inputs(seed))
    for name, value in second_inputs(seed + 1).items():
        if name != "x":
            out[name + "_2"] = value
    return out


def reference(
    x, c, norm_g, final_g, ada_w, ada_b, conv_w_in, conv_w, conv_w_out, rw_mu, rw_w_rkv, rw_w_o,
    rw_w0, rw_w1, rw_w2, rw_a0, rw_a1, rw_a2, rw_g1, rw_g2, rw_k_k, rw_k_a, rw_r_k, rw_ln_w,
    rw_ln_b, rw_v0, rw_v1, rw_v2, mlp_w1, mlp_w2, mem_2, ffn1_norm_2, ffn1_w_gate_2,
    ffn1_w_up_2, ffn1_w_down_2, mix_norm_2, w_in_2, ret_out_norm_2, diff_lq1_2, diff_lk1_2,
    diff_lq2_2, diff_lk2_2, diff_out_norm_2, w_out_2, xattn_norm_2, mem_norm_2, xattn_wq_2,
    xattn_wkv_2, xattn_wo_2, ffn2_norm_2, ffn2_w_gate_2, ffn2_w_up_2, ffn2_w_down_2,
    final_norm_2,
):
    x = first_block(
        x, c, norm_g, final_g, ada_w, ada_b, conv_w_in, conv_w, conv_w_out, rw_mu, rw_w_rkv,
        rw_w_o, rw_w0, rw_w1, rw_w2, rw_a0, rw_a1, rw_a2, rw_g1, rw_g2, rw_k_k, rw_k_a, rw_r_k,
        rw_ln_w, rw_ln_b, rw_v0, rw_v1, rw_v2, mlp_w1, mlp_w2,
    )
    return second_block(
        x, mem_2, ffn1_norm_2, ffn1_w_gate_2, ffn1_w_up_2, ffn1_w_down_2, mix_norm_2, w_in_2,
        ret_out_norm_2, diff_lq1_2, diff_lk1_2, diff_lq2_2, diff_lk2_2, diff_out_norm_2,
        w_out_2, xattn_norm_2, mem_norm_2, xattn_wq_2, xattn_wkv_2, xattn_wo_2, ffn2_norm_2,
        ffn2_w_gate_2, ffn2_w_up_2, ffn2_w_down_2, final_norm_2,
    )


_drawn_inputs = setup_inputs


def setup_inputs(seed=0):
    import zlib

    import numpy as np

    out = dict(_drawn_inputs(seed))
    spreads = {}
    factors = {'rw_w1': 8.0,
     'rw_w2': 8.0,
     'rw_a0': 6.881,
     'rw_a1': 6.792,
     'rw_a2': 6.791,
     'rw_k_k': 2.892,
     'rw_ln_w': 6.559,
     'rw_ln_b': 8.0,
     'ffn1_norm_2': 6.202,
     'mix_norm_2': 3.218,
     'ret_out_norm_2': 8.0,
     'diff_lq1_2': 4.721,
     'diff_lk1_2': 8.0,
     'diff_out_norm_2': 25.355,
     'xattn_norm_2': 8.0,
     'mem_norm_2': 8.0,
     'ffn2_norm_2': 21.338,
     'final_norm_2': 8.016}
    for name, (base, spread) in spreads.items():
        noise = np.random.default_rng([zlib.crc32(name.encode()), seed]).standard_normal(out[name].shape)
        drawn = base * np.exp(spread * noise) if base else spread * noise
        out[name] = __import__('jax').numpy.asarray(drawn.astype(out[name].dtype))
    for name, factor in factors.items():
        out[name] = (out[name] * factor).astype(out[name].dtype)
    return out
```

```python
from contextlib import ExitStack
import math

import concourse.bass as bass
from concourse import mybir

F32 = mybir.dt.float32
U32 = mybir.dt.uint32
ALU = mybir.AluOpType
ACT = mybir.ActivationFunctionType
AX = mybir.AxisListType.X

MUL, ADD, SUB, MAXO = ALU.mult, ALU.add, ALU.subtract, ALU.max

VECS = ["g00", "g01", "g10", "g11", "final_g", "cw0", "cw1", "cw2",
        "mu0", "mu1", "mu2", "mu3", "mu4", "mu5", "w0", "a0", "k_k", "k_a", "r_k", "ln_w", "ln_b",
        "ffn1_norm", "mix_norm", "xattn_norm", "mem_norm", "ffn2_norm", "final_norm",
        "ret_norm", "diff_norm"]
VOFF = {n: 8 * i for i, n in enumerate(VECS)}

NSLOT = 6
NADA = 2


class Engines:

    def __init__(self, sems):
        self.sems = sems
        self.q = {n: [] for n in ("pe", "v", "a", "g", "sp")}
        self.count = {n: 0 for n in sems}
        self.seen = {n: {} for n in self.q}

    def emit(self, eng, fn, waits, sem=None, by=1):
        for s, v in flat(waits):
            if self.seen[eng].get(s, 0) < v:
                self.seen[eng][s] = v
                self.q[eng].append((None, self.sems[s], v))
        if sem is None:
            self.q[eng].append((fn, None, 0))
            return None
        self.count[sem] += by
        self.q[eng].append((fn, self.sems[sem], by))
        return (sem, self.count[sem])

    def play(self, name, eng):
        for fn, sem, v in self.q[name]:
            if fn is None:
                eng.wait_ge(sem, v)
            elif sem is None:
                fn(eng)
            else:
                fn(eng).then_inc(sem, v)


def flat(ts):
    out = []
    for t in ts:
        if t is None:
            continue
        if isinstance(t, tuple) and len(t) == 2 and isinstance(t[0], str):
            out.append(t)
        else:
            out += flat(t)
    return out


def build(nc, D, out):
    ctx = ExitStack()
    with ctx:
        def sb(name, shape, dt=F32):
            return ctx.enter_context(nc.sbuf_tensor(name, shape, dt))

        names = ["pe", "v", "a", "g", "out", "cst", "wvec"] + [f"r{i}" for i in range(NSLOT)] + \
                [f"d{i}" for i in range(NADA)] + ["cx", "cd"]
        sems = {n: ctx.enter_context(nc.semaphore("s_" + n)) for n in names}
        E = Engines(sems)

        ps = ctx.enter_context(nc.psum_tensor("ps", [128, 8, 512], F32))
        X = sb("X", [128, 8, 512])
        HP = sb("HP", [128, 8 * 513])
        AR = sb("AR", [128, 7, 8, 512])
        BIG = sb("BIG", [128, 12288])
        GH = sb("GH", [128, 2, 512])
        vec = sb("vec", [128, 8 * len(VECS)])
        ident = sb("ident", [128, 128])
        bones = sb("bones", [128, 128])
        ones = sb("ones", [128, 128])
        negm = sb("negm", [128, 128])
        mD = sb("mD", [128, 256])
        mE = sb("mE", [128, 256])
        mR = sb("mR", [128, 256])
        mod = sb("mod", [128, 96])
        adab = sb("adab", [128, 96])
        coef = sb("coef", [128, 32])
        omu = sb("omu", [128, 48])
        lmid = sb("lmid", [128, 8, 4])
        fct = sb("fct", [128, 8, 4])
        st = sb("st", [128, 16])
        stat = sb("stat", [128, 16])
        eps6 = sb("eps6", [128, 2])

        H = HP[:, :].rearrange("p (f t) -> p f t", t=513)
        H8 = HP[:, 0:4096].rearrange("p (f t) -> p f t", t=512)
        XM0, XM1, L, R, A, K, V = [AR[:, i] for i in range(7)]
        ring = [BIG[:, 1024 * i:1024 * (i + 1)] for i in range(NSLOT)]
        ada = [BIG[:, 6144 + 1024 * i:7168 + 1024 * i] for i in range(NADA)]
        cbc = BIG[:, 8192:9216]
        sqt = [BIG[:, 9216:9728], BIG[:, 9728:10240]]
        acc = BIG[:, 10240:10752]
        rstd = BIG[:, 10752:11264]
        T64 = [BIG[:, 11264:11776], BIG[:, 11776:12288]]

        def act(o, i, func, *w, scale=1.0, bias=0.0, accum=None):
            if accum is not None:
                return E.emit("a", lambda e: e.activation(o, i, func, bias=bias, scale=scale, accum_out=accum), w, "a")
            return E.emit("a", lambda e: e.activation(o, i, func, bias=bias, scale=scale), w, "a")

        def vcopy(o, i, *w):
            return E.emit("v", lambda e: e.tensor_copy(o, i), w, "v")

        def vtt(o, a, b, op, *w):
            return E.emit("v", lambda e: e.tensor_tensor(o, a, b, op), w, "v")

        def vts(o, a, s1, s2, op0, op1, *w):
            if op1 is None:
                return E.emit("v", lambda e: e.tensor_scalar(o, a, s1, None, op0), w, "v")
            return E.emit("v", lambda e: e.tensor_scalar(o, a, s1, s2, op0, op1), w, "v")

        def vstt(o, a, s, b, op0, op1, *w):
            return E.emit("v", lambda e: e.scalar_tensor_tensor(out=o, in0=a, scalar=s, in1=b, op0=op0, op1=op1), w, "v")

        def vrec(o, i, *w):
            return E.emit("v", lambda e: e.reciprocal(o, i), w, "v")

        def vset(o, val, *w):
            return E.emit("v", lambda e: e.memset(o, val), w, "v")

        def vpred(o, m, d, *w):
            return E.emit("v", lambda e: e.copy_predicated(o, m, d), w, "v")

        def vdot(junk, a, b, o, *w):
            return E.emit("v", lambda e: e.tensor_tensor_reduce(junk, a, b, 1.0, 0.0, MUL, ADD, o), w, "v")

        def vscan(o, d0, d1, *w):
            return E.emit("v", lambda e: e.tensor_tensor_scan(o, d0, d1, 0.0, MUL, ADD), w, "v")

        def vmax(o, i, *w):
            return E.emit("v", lambda e: e.tensor_reduce(o, i, AX, MAXO), w, "v")

        def mm(o, lhsT, rhs, start, stop, *w, inc=False):
            return E.emit("pe", lambda e: e.matmul(o, lhsT, rhs, start=start, stop=stop), w, "pe" if inc else None)

        def tr(o, i, *w, inc=False):
            return E.emit("pe", lambda e: e.transpose(o, i, ident[:, :]), w, "pe" if inc else None)

        def dma(eng, o, i, sem, *w):
            return E.emit(eng, lambda e: e.dma_start(o, i), w, sem, 16)

        bank_free = [[] for _ in range(8)]
        at = {"bank": 0, "slot": 0, "ada": 0}
        slot_free = [[] for _ in range(NSLOT)]
        ada_free = [[] for _ in range(NADA)]

        def bank():
            b = at["bank"]
            at["bank"] = (b + 1) % 8
            return b

        def load(src, parts, n):
            s = at["slot"]
            at["slot"] = (s + 1) % NSLOT
            t = dma("sp", ring[s][0:parts, 0:n], src, f"r{s}", slot_free[s])
            return s, t

        t_x = dma("sp", X[:, :, :], D["xT"], "cx")
        t_c = dma("sp", cbc, D["cb"], "cx")
        t_ab = dma("sp", adab[:, :], D["adab"], "cst")
        dma("sp", vec[:, :], D["vec"], "cst")
        dma("sp", ident[:, :], D["ident"], "cst")
        dma("sp", bones[:, :], D["bones"], "cst")
        dma("sp", negm[:, :], D["negm"], "cst")
        dma("sp", mD[:, :], D["mD"], "cst")
        dma("sp", mE[:, :], D["mE"], "cst")
        t_cst = dma("sp", mR[:, :], D["mR"], "cst")
        t_x = t_c
        t_one = vset(ones[:, :], 1.0)
        t_e0 = vset(eps6[:, 0:1], 1e-6)
        t_e1 = vset(eps6[:, 1:2], 64e-5)
        pad = vset(H[:, :, 0:1], 0.0)

        def vc(name, f, w=1):
            return vec[:, VOFF[name] + f:VOFF[name] + f + w]

        t = act(sqt[0], cbc[:, 0:512], ACT.Sigmoid, t_c)
        t2 = act(sqt[1], cbc[:, 512:1024], ACT.Sigmoid, t_c)
        t_s = [vtt(cbc[:, 0:512], cbc[:, 0:512], sqt[0], MUL, t), vtt(cbc[:, 512:1024], cbc[:, 512:1024], sqt[1], MUL, t2)]
        sq_free = [t_s[0], t_s[1]]

        mod_t = {}

        def ada_step(n=1):
            for _ in range(n):
                u = at["ada"]
                if u >= 96:
                    return
                at["ada"] = u + 1
                s = u % NADA
                t = dma("g", ada[s], D["adaw"][u], f"d{s}", ada_free[s])
                tt = vdot(ada[s], ada[s], cbc, mod[:, u:u + 1], t, t_s)
                ada_free[s] = [tt]
                if u % 8 == 7:
                    mod_t[u // 8] = vtt(mod[:, u - 7:u + 1], mod[:, u - 7:u + 1], adab[:, u - 7:u + 1], ADD, tt, t_ab, t_cst)

        def md(layer, j, f):
            u = layer * 48 + j * 8 + f
            return mod[:, u:u + 1]

        sq_n = {"n": 0, "acc": None}

        def sumsq(src, first, *w, n=512):
            i = sq_n["n"] % 2
            sq_n["n"] += 1
            t = act(sqt[i][:, 0:n], src, ACT.Square, sq_free[i], w)
            if first:
                t = vcopy(acc[:, 0:n], sqt[i][:, 0:n], t, sq_n["acc"])
            else:
                t = vtt(acc[:, 0:n], acc[:, 0:n], sqt[i][:, 0:n], ADD, t, sq_n["acc"])
            sq_n["acc"] = t
            sq_free[i] = t
            return t

        rstd_read = {"t": []}

        def finish_norm(lhsT, count, eps, o, n=512, src=None, w=()):
            b = bank()
            t = mm(ps[:, b, 0:n], lhsT, acc[:, 0:n] if src is None else src, True, True,
                   sq_n["acc"], bank_free[b], t_one, t_cst, w, inc=True)
            if src is None:
                sq_n["acc"] = t
            ta = act(o, ps[:, b, 0:n], ACT.Sqrt, t, rstd_read["t"], t_e0, t_e1, scale=1.0 / count, bias=eps)
            bank_free[b] = [ta]
            return vrec(o, o, ta)

        def proj(wname, blocks, kc, mcols, rhs, rhs_t, evac, n=512, parts=128, per=8, tick=0):
            for nb in blocks:
                b = bank()
                for k0 in range(0, kc, per):
                    k1 = min(kc, k0 + per)
                    m = mcols
                    s, tl = load(D[wname][nb, 0:parts, k0 * m:k1 * m], parts, (k1 - k0) * m)
                    for k in range(k0, k1):
                        last = k == k1 - 1
                        t = mm(ps[0:m, b, 0:n], ring[s][0:parts, (k - k0) * m:(k - k0 + 1) * m], rhs(k),
                               k == 0, k == kc - 1, tl, bank_free[b] if k == 0 else None, rhs_t[k], inc=last)
                    slot_free[s] = [t]
                bank_free[b] = evac(nb, ps[0:m, b, 0:n], t)
                ada_step(tick)
            return t

        for f in range(8):
            tq = sumsq(X[:, f], f == 0, t_x)
        x_t = [t_x] * 8
        h_free = [pad]

        def modulated(layer, j, gname):
            nonlocal h_free
            tr_ = finish_norm(ones[:, :], 1024.0, eps6[:, 0:1], rstd)
            hs = []
            reads = []
            tc = vstt(coef[:, 0:8], mod[:, layer * 48 + (j + 1) * 8:layer * 48 + (j + 2) * 8], 1.0, vc(gname, 0, 8),
                      ADD, MUL, mod_t[layer * 6 + j + 1], t_cst)
            for f in range(8):
                t = vstt(H[:, f, 1:513], X[:, f], coef[:, f:f + 1], rstd, MUL, MUL, tr_, tc, x_t[f], h_free)
                reads.append(t)
                hs.append(act(H[:, f, 1:513], H[:, f, 1:513], ACT.Identity, t, mod_t[layer * 6 + j], pad, bias=md(layer, j, f)))
            rstd_read["t"] = reads[-1]
            return hs

        def plain_norm(gname, dst, n=512, src=X, w=None):
            tr_ = finish_norm(ones[:, :], 1024.0, eps6[:, 0:1], rstd[:, 0:n], n)
            hs = [vstt(dst(f), src[:, f, 0:n], vc(gname, f), rstd[:, 0:n], MUL, MUL, tr_, x_t[f], w, t_cst) for f in range(8)]
            rstd_read["t"] = hs[-1]
            return hs

        def residual(gate, extra):
            def evac(m, p, t):
                t1 = vstt(X[:, m], p, gate(m), X[:, m], MUL, ADD, t, x_t[m], extra)
                x_t[m] = t1
                sumsq(X[:, m], m == 0, t1)
                return [t1]
            return evac

        ada_step(16)
        hs = modulated(0, 0, "g00")
        cg = [XM1[:, 0], XM1[:, 1]]
        cgf = [[], []]
        uu = [XM1[:, 2:4].rearrange("p a t -> p (a t)")[:, 0:514], XM1[:, 4:6].rearrange("p a t -> p (a t)")[:, 0:514]]
        up = [vset(u[:, 0:2], 0.0) for u in uu]
        uf = [[], []]
        cv = [XM1[:, 6], XM1[:, 7]]
        z_t = [None] * 8
        h = lambda k: H[:, k, 1:513]
        keep = {}

        def conv_evac(nb, p, t):
            j, i = nb % 8, nb % 2
            if nb // 8 == 1:
                keep["c"] = act(cg[i], p, ACT.Copy, t, cgf[i])
                return [keep["c"]]
            if nb // 8 == 2:
                t1 = vtt(uu[i][:, 2:514], cg[i], p, MUL, t, keep["c"], uf[i])
                cgf[i] = [t1]
                t2 = vts(cv[i], uu[i][:, 0:512], vc("cw0", j), None, MUL, None, t1, up, z_t[j - 2] if j > 1 else None)
                t3 = vstt(cv[i], uu[i][:, 1:513], vc("cw1", j), cv[i], MUL, ADD, t2)
                keep["z"] = vstt(cv[i], uu[i][:, 2:514], vc("cw2", j), cv[i], MUL, ADD, t3)
                uf[i] = [keep["z"]]
                return [t1]
            z_t[j] = vtt(XM0[:, j], cv[i], p, MUL, t, keep["z"])
            return [z_t[j]]

        order = [x for j in range(8) for x in (8 + j, 16 + j, j)]
        t = proj("cw_in", order, 8, 128, h, hs, conv_evac, tick=1)
        h_free = [t]
        proj("cw_out", range(8), 8, 128, lambda k: XM0[:, k], z_t,
             residual(lambda m: md(0, 2, m), mod_t[2]))

        def mlp(layer, w1, w2, tick):
            nonlocal h_free
            hs = modulated(layer, 3, "g%d1" % layer)
            hid = lambda k: AR[:, k // 8, k % 8]
            hid_t = [None] * 32

            def up_evac(nb, p, t):
                t1 = act(hid(nb), p, ACT.Relu, t, hid_free)
                hid_t[nb] = vtt(hid(nb), hid(nb), hid(nb), MUL, t1)
                return [t1]

            t = proj(w1, range(32), 8, 128, h, hs, up_evac, tick=tick)
            h_free = [t]
            g = residual(lambda m: md(layer, 5, m), mod_t[6 * layer + 5])
            return proj(w2, range(8), 32, 128, hid, hid_t, g)

        hid_free = [x_t, z_t]
        t_prev = mlp(0, "mw1_0", "mw2_0", 2)
        assert at["ada"] == 96

        hs = modulated(1, 0, "g10")
        for i in range(6):
            vts(omu[:, 8 * i:8 * i + 8], vc("mu%d" % i, 0, 8), -1.0, 1.0, MUL, ADD, t_cst)
        t_omu = ("v", E.count["v"])
        xm = [XM0, XM1]
        xm_free = [[t_prev], [t_prev]]
        last_mix = []

        def mix(mu, i):
            ts = []
            for f in range(8):
                ta = act(xm[i][:, f], H[:, f, 1:513], ACT.Identity, hs[f], t_omu, xm_free[i],
                         scale=omu[:, 8 * mu + f:8 * mu + f + 1])
                ts.append(vstt(xm[i][:, f], H[:, f, 0:512], vc("mu%d" % mu, f), xm[i][:, f], MUL, ADD, ta, hs[f]))
            last_mix[:] = ts[-1:]
            return ts

        def lora(w1, w2, ts, i, j, func, biasn, dst):
            keep = {}

            def e1(nb, p, t):
                keep["t"] = act(T64[j][0:64], p, func, t)
                return [keep["t"]]
            xm_free[i] = [proj(w1, [0], 8, 64, lambda k: xm[i][:, k], ts, e1)]
            s, tl = load(D[w2][0:64, :], 64, 1024)
            done = []
            for f in range(8):
                b = bank()
                t = mm(ps[:, b], ring[s][0:64, 128 * f:128 * f + 128], T64[j][0:64], True, True,
                       tl, keep["t"], bank_free[b], inc=True)
                ta = act(dst[:, f], ps[:, b], ACT.Sigmoid, t, t_prev, t_cst, bias=vc(biasn, f))
                bank_free[b] = [ta]
                done.append(ta)
            slot_free[s] = [t]
            return done

        ts = mix(1, 0)
        ts2 = mix(4, 1)
        l_t = lora("dw1", "dw2", ts, 0, 0, ACT.Tanh, "w0", L)
        a_t = lora("aw1", "aw2", ts2, 1, 1, ACT.Copy, "a0", A)
        ts = mix(5, 0)
        ts2 = mix(2, 1)
        gk = []

        def g_evac(m):
            def f(nb, p, t):
                ta = act(GH[0:m, nb], p, ACT.Sigmoid, t)
                gk.append(ta)
                return [ta]
            return f
        proj("gw1a", [0], 8, 128, lambda k: XM0[:, k], ts, g_evac(128))
        b = bank()
        s, tl = load(D["gw1b"][0], 128, 256)
        for k in range(8):
            t = mm(ps[0:32, b], ring[s][:, 32 * k:32 * k + 32], XM0[:, k], k == 0, k == 7, tl, bank_free[b], ts[k],
                   inc=k == 7)
        slot_free[s] = [t]
        xm_free[0] = [t]
        ta = act(GH[0:32, 1], ps[0:32, b], ACT.Sigmoid, t)
        gk.append(ta)
        bank_free[b] = [ta]

        def copy_evac(dst, toks):
            def f(nb, p, t):
                if nb % 2:
                    toks[nb] = act(dst[:, nb], p, ACT.Copy, t, t_prev)
                else:
                    toks[nb] = vcopy(dst[:, nb], p, t, t_prev)
                return [toks[nb]]
            return f
        k_t, v_t, r_t = [None] * 8, [None] * 8, [None] * 8
        xm_free[1] = [proj("wk", range(8), 8, 128, lambda k: XM1[:, k], ts2, copy_evac(K, k_t))]
        ts = mix(3, 0)
        ts2 = mix(0, 1)
        xm_free[0] = [proj("wv", range(8), 8, 128, lambda k: XM0[:, k], ts, copy_evac(V, v_t))]
        xm_free[1] = [proj("wr", range(8), 8, 128, lambda k: XM1[:, k], ts2, copy_evac(R, r_t))]

        kk_t = [None] * 8
        h8w = [last_mix, t]
        for f in range(8):
            t0 = vts(H8[:, f], K[:, f], vc("k_k", f), None, MUL, None, k_t[f], last_mix, hs)
            i = f % 2
            t1 = act(sqt[i], H8[:, f], ACT.Square, t0, sq_free[i])
            b = bank()
            t2 = mm(ps[:, b], bones[:, :], sqt[i], True, True, t1, bank_free[b], inc=True)
            sq_free[i] = t2
            t3 = vts(XM0[:, f], ps[:, b], 1e-24, None, MAXO, None, t2, xm_free[0])
            bank_free[b] = [t3]
            kk_t[f] = t3
        for f in range(8):
            t1 = act(XM0[:, f], XM0[:, f], ACT.Sqrt, kk_t[f])
            t2 = vrec(XM0[:, f], XM0[:, f], t1)
            kk_t[f] = vtt(H8[:, f], H8[:, f], XM0[:, f], MUL, t2)
        cmask = acc
        t1 = vset(cmask, 1.0, sq_n["acc"])
        t_cm = vset(cmask[:, 0:512:128], 0.0, t1)
        kp_t, lc_t = [None] * 8, [None] * 8
        for f in range(8):
            t1 = vts(sqt[f % 2], A[:, f], 1.0, vc("k_a", f), SUB, MUL, a_t[f], sq_free[f % 2])
            kp_t[f] = vstt(K[:, f], sqt[f % 2], 1.0, K[:, f], ADD, MUL, t1, k_t[f])
            sq_free[f % 2] = kp_t[f]
            t2 = vts(L[:, f], L[:, f], -math.exp(-0.5), None, MUL, None, l_t[f])
            lc_t[f] = vscan(XM1[:, f], cmask, L[:, f], t2, t_cm, xm_free[1])
        t_lm = vcopy(lmid[:, :, :], XM1[:, :, 63:512:128], lc_t)

        VT = XM0.rearrange("p a t -> p (a t)").rearrange("p (c n) -> p c n", c=4)
        vt_t = []
        for f in range(8):
            b = bank()
            for c in range(4):
                t = tr(ps[:, b, 128 * c:128 * c + 128], V[:, f, 128 * c:128 * c + 128], v_t[f], bank_free[b], t_cst,
                       inc=c == 3)
            t = act(VT[:, :, 128 * f:128 * f + 128], ps[:, b].rearrange("p (c n) -> p c n", c=4), ACT.Copy, t, kk_t)
            bank_free[b] = [t]
            vt_t.append(t)
        for f in range(8):
            i = f % 2
            t1 = vstt(sqt[i], R[:, f], vc("r_k", f), K[:, f], MUL, MUL, r_t[f], kp_t[f], sq_free[i])
            b = bank()
            t2 = mm(ps[:, b], bones[:, :], sqt[i], True, True, t1, bank_free[b], inc=True)
            v_t[f] = vtt(V[:, f], V[:, f], ps[:, b], MUL, t2, vt_t[f])
            bank_free[b] = [v_t[f]]
            lm = lmid[:, f, :].rearrange("p (c o) -> p c o", o=1).to_broadcast([128, 4, 128])
            x1 = XM1[:, f].rearrange("p (c t) -> p c t", t=128)
            t3 = vtt(x1, x1, lm, SUB, t_lm)
            t4 = vtt(L[:, f], XM1[:, f], L[:, f], SUB, t3)
            t5 = act(L[:, f], L[:, f], ACT.Exp, t4)
            l_t[f] = vstt(L[:, f], H8[:, f], -1.0, L[:, f], MUL, MUL, t5, kk_t[f])
            t7 = vtt(A[:, f], H8[:, f], A[:, f], MUL, kp_t[f])
            t8 = act(sqt[i], XM1[:, f], ACT.Exp, t3, t2, scale=-1.0)
            a_t[f] = vtt(A[:, f], A[:, f], sqt[i], MUL, t8, t7)
            k_t[f] = vtt(K[:, f], K[:, f], sqt[i], MUL, t8, t1)
            sq_free[i] = k_t[f]
            lc_t[f] = t3
        t_le = vcopy(fct[:, :, :], XM1[:, :, 127:512:128], lc_t)
        t_f = vtt(fct[:, :, 0:3], fct[:, :, 0:3], lmid[:, :, 1:4], ADD, t_le)
        t_f = act(fct[:, :, :], fct[:, :, :], ACT.Exp, t_f)
        for f in range(8):
            t = act(XM1[:, f], XM1[:, f], ACT.Exp, lc_t[f], t_le)
            r_t[f] = vtt(R[:, f], R[:, f], XM1[:, f], MUL, t, v_t[f])
        YT = XM1

        NB = [BIG[:, 512 * i:512 * i + 512] for i in range(18)]
        Wk, U, S = BIG[:, 9216:10240], BIG[:, 10240:11264], BIG[:, 11264:11776]
        Ym = HP[:, 0:2048].rearrange("p (g j t) -> p g j t", g=4, j=4)
        Mbr = HP[:, 2048:4096].rearrange("p (g j t) -> p g j t", g=4, j=4)
        before = [("v", E.count["v"]), ("a", E.count["a"]), ("pe", E.count["pe"])]
        vset(Mbr, 0.0, before)
        for i in (0, 1, 7, 8, 9, 10, 16, 17):
            t_z = vset(NB[i], 0.0, before)
        t_z = ("v", E.count["v"])
        id4 = ident[:, :].rearrange("p (o t) -> p o t", o=1).to_broadcast([128, 4, 128])
        q4 = lambda x: x.rearrange("p (j t) -> p j t", j=4)
        q2 = lambda x: x.rearrange("p (j t) -> p j t", j=2)

        def four(lhs, rhs, *w):
            b = bank()
            for j in range(4):
                t = mm(ps[:, b, 128 * j:128 * j + 128], lhs[:, 128 * j:128 * j + 128], rhs[:, 128 * j:128 * j + 128],
                       True, True, w, bank_free[b], inc=j == 3)
            return b, t

        def four_a(dst, lhs, rhs, *w):
            b, t = four(lhs, rhs, w)
            t = act(dst, ps[:, b], ACT.Copy, t)
            bank_free[b] = [t]
            return t

        def four_v(dst, lhs, rhs, *w):
            b, t = four(lhs, rhs, w)
            t = vcopy(dst, ps[:, b], t)
            bank_free[b] = [t]
            return t

        def four_add(dst, acc_, lhs, rhs, *w):
            b, t = four(lhs, rhs, w)
            t = vtt(dst, acc_, ps[:, b], ADD, t, w)
            bank_free[b] = [t]
            return t

        def four_tr(dst, x, w):
            b = bank()
            for j in range(4):
                t = tr(ps[:, b, 128 * j:128 * j + 128], x[:, 128 * j:128 * j + 128], w, bank_free[b], inc=j == 3)
            t = act(dst, ps[:, b], ACT.Copy, t)
            bank_free[b] = [t]
            return t

        ready = {}

        def group(c, g, B, state_done):
            Dm, Em, Mak, Mkr, b1, b2, b3, b4, b5 = B
            td = []
            cs = slice(128 * c, 128 * c + 128)
            for p in range(2):
                pp = slice(64 * p, 64 * p + 64)
                b = bank()
                for fi in range(2):
                    f = 2 * g + fi
                    t = mm(ps[:, b, 256 * fi:256 * fi + 256], A[pp, f, cs], AR[pp, 2:4, f, cs], True, True,
                           a_t[f], l_t[f], r_t[f], bank_free[b], inc=fi == 1)
                bv = ps[:, b].rearrange("p (i r t) -> p i r t", i=2, r=2)
                m2 = slice(256 * p, 256 * p + 256)
                td.append(vpred(q2(Dm[:, m2]), q2(mD[:, 0:256].bitcast(U32)), bv[:, :, 0], t, t_z, B_free[id(B)]))
                td.append(vpred(q2(Em[:, m2]), q2(mE[:, 0:256].bitcast(U32)), bv[:, :, 0], t, t_z))
                t = vpred(Mbr[:, g, 2 * p:2 * p + 2], q2(mR[:, 0:256].bitcast(U32)), bv[:, :, 1], t, t_z, state_done)
                bank_free[b] = [t]
                td.append(t)
            ready[c, g, "br"] = t
            tk = []
            for p in range(2):
                pp = slice(64 * p, 64 * p + 64)
                b = bank()
                for fi in range(2):
                    f = 2 * g + fi
                    t = mm(ps[:, b, 256 * fi:256 * fi + 256], K[pp, f, cs], AR[pp, 2:4, f, cs], True, True,
                           k_t[f], bank_free[b], inc=fi == 1)
                bv = ps[:, b].rearrange("p (i r t) -> p i r t", i=2, r=2)
                m2 = slice(256 * p, 256 * p + 256)
                ma = [q2(mD[:, 0:256].bitcast(U32)), q2(mE[:, 0:256].bitcast(U32))]
                vpred(q2(Mak[:, m2]), ma[0], bv[:, :, 0], t)
                vpred(q2(Mak[:, m2]), ma[1], bv[:, :, 0], ("v", E.count["v"]))
                t = vpred(q2(Mkr[:, m2]), q2(mR[:, 0:256].bitcast(U32)), bv[:, :, 1], t)
                bank_free[b] = [t]
                tk.append(t)
            yield
            t_d = four_tr(b1, Dm, td)
            t_1 = vtt(q4(b4), q4(Dm), id4, ADD, td)
            b = bank()
            for j in range(4):
                p, fi = j // 2, j % 2
                hc = (2 * g + fi) * 128 + 64 * p
                t = mm(ps[:, b, 64 * j:64 * j + 64], Mak[:, 128 * j:128 * j + 128], VT[:, c, hc:hc + 64], True, True,
                       tk, vt_t, bank_free[b], inc=j == 3)
            wd = Wk.rearrange("p (q n) -> p q n", q=2)[:, :, 128 * g:128 * g + 128]
            t = vcopy(wd, q2(ps[:, b, 0:256]), t, state_done)
            bank_free[b] = [t]
            ready[c, g, "w"] = t
            b = bank()
            for j in range(4):
                p, fi = j // 2, j % 2
                hc = (2 * g + fi) * 128 + 64 * p
                t = mm(ps[64 * p:64 * p + 64, b, 128 * fi:128 * fi + 128], VT[:, c, hc:hc + 64],
                       Mkr[:, 128 * j:128 * j + 128], True, True, bank_free[b], inc=j == 3)
            t = act(YT[:, 2 * g:2 * g + 2, cs], q2(ps[:, b, 0:256]), ACT.Copy, t, r_t)
            bank_free[b] = [t]
            ready[c, g, "y"] = t
            yield
            ta = four_v(b2, b1, Dm, t_d, td)
            tb = four_a(b3, Dm, b1)
            yield
            tc = four_v(b1, b3, b2, ta, tb)
            td4 = four_a(b5, b2, b3)
            t_1 = four_add(b4, b4, b3, b4, t_1)
            yield
            te = four_a(b2, b1, b5, tc, td4)
            t_1 = four_add(b4, b4, b5, b4, t_1)
            yield
            t_1 = four_add(b4, b4, b2, b4, t_1, te)
            yield
            ta = four_tr(b1, b4, t_1)
            yield
            tb = four_a(b2, Em, b1, ta)
            tc = four_v(b3, b1, Em)
            yield
            ta = four_a(b5, b3, b2, tb, tc)
            te = four_v(b1, b2, b3)
            t_1 = four_add(b4, b4, b2, b4, t_1)
            yield
            tb = four_a(b2, b1, b5, ta, te)
            t_1 = four_add(b4, b4, b5, b4, t_1)
            yield
            ym = Ym[:, g].rearrange("p j t -> p (j t)")
            b, t = four(b2, b4, tb, t_1)
            t = vtt(ym, b4, ps[:, b], ADD, t, t_1, state_done)
            bank_free[b] = [t]
            ready[c, g, "T"] = t
            B_free[id(B)] = [t]

        bufs = [NB[0:2] + NB[7:9] + NB[2:7], NB[9:11] + NB[16:18] + NB[11:16]]
        B_free = {id(x): [] for x in bufs}

        s_t = None
        done = []
        for c in range(4):
            cs = slice(128 * c, 128 * c + 128)
            for g0 in (0, 2):
                live = [group(c, g0 + i, bufs[i], done) for i in range(2)]
                while live:
                    for x in list(live):
                        try:
                            next(x)
                        except StopIteration:
                            live.remove(x)
            tk_t = []
            if c < 3:
                for x, xt in ((A, a_t), (K, k_t)):
                    for hf in range(2):
                        b = bank()
                        for f in range(4 * hf, 4 * hf + 4):
                            t = tr(ps[:, b, 128 * (f % 4):128 * (f % 4) + 128], x[:, f, cs], bank_free[b], inc=f % 4 == 3)
                        t = act(x[:, 4 * hf:4 * hf + 4, cs], q4(ps[:, b]), ACT.Copy, t)
                        bank_free[b] = [t]
                        tk_t.append(t)
            w_t = []
            for p in range(2):
                pp = slice(64 * p, 64 * p + 64)
                wt = [ready[c, g, "w"] for g in range(4)]
                if c:
                    b = bank()
                    for f in range(8):
                        t = mm(ps[:, b, 64 * f:64 * f + 64], L[pp, f, cs], S[pp, 64 * f:64 * f + 64], True, True,
                               s_t, bank_free[b], inc=f == 7)
                    t = vtt(Wk[:, 512 * p:512 * p + 512], Wk[:, 512 * p:512 * p + 512], ps[:, b], ADD, t, wt)
                    bank_free[b] = [t]
                    w_t.append([t])
                else:
                    w_t.append(wt)
            u_t = []
            for p in range(2):
                b = bank()
                for f in range(8):
                    t = mm(ps[:, b, 64 * f:64 * f + 64], Ym[:, f // 2, 2 * p + f % 2],
                           Wk[:, 512 * p + 64 * f:512 * p + 64 * f + 64], True, True,
                           w_t[p], [ready[c, g, "T"] for g in range(4)], bank_free[b], inc=f == 7)
                if p:
                    t = vcopy(U[:, 512:1024], ps[:, b], t, done)
                else:
                    t = act(U[:, 0:512], ps[:, b], ACT.Copy, t, done)
                bank_free[b] = [t]
                u_t.append(t)
            y_t = []
            for hf in range(2):
                b = bank()
                for f in range(4 * hf, 4 * hf + 4):
                    for p in range(2):
                        pp = slice(64 * p, 64 * p + 64)
                        o = ps[pp, b, 128 * (f % 4):128 * (f % 4) + 128]
                        if c:
                            mm(o, S[pp, 64 * f:64 * f + 64], R[pp, f, cs], True, False, bank_free[b], s_t)
                        t = mm(o, U[:, 512 * p + 64 * f:512 * p + 64 * f + 64], Mbr[:, f // 2, 2 * p + f % 2],
                               c == 0, True, u_t, bank_free[b], [ready[c, g, "br"] for g in range(4)],
                               inc=f % 4 == 3 and p == 1)
                yv = YT[:, 4 * hf:4 * hf + 4, cs]
                t = vtt(yv, yv, q4(ps[:, b]), ADD, t, [ready[c, g, "y"] for g in range(4)])
                bank_free[b] = [t]
                y_t.append(t)
            done = y_t
            if c < 3:
                b = bank()
                for f in range(8):
                    for p in range(2):
                        o = ps[64 * p:64 * p + 64, b, 64 * f:64 * f + 64]
                        n = slice(64 * p, 64 * p + 64)
                        mm(o, A[:, f, 128 * c + 64 * p:128 * c + 64 * p + 64], U[:, 512 * p + 64 * f:512 * p + 64 * f + 64],
                           True, False, tk_t, bank_free[b])
                        t = mm(o, K[:, f, 128 * c + 64 * p:128 * c + 64 * p + 64],
                               VT[:, c, 128 * f + 64 * p:128 * f + 64 * p + 64], False, True, inc=f == 7 and p == 1)
                fb = fct[:, :, c:c + 1].to_broadcast([128, 8, 64])
                s3 = S.rearrange("p (f v) -> p f v", v=64)
                p3 = ps[:, b].rearrange("p (f v) -> p f v", v=64)
                if c:
                    t2 = vtt(S, S, ps[:, b], ADD, t)
                    s_t = vtt(s3, s3, fb, MUL, t2, t_f)
                else:
                    s_t = vtt(s3, p3, fb, MUL, t, t_f)
                bank_free[b] = [s_t]
                done = y_t + [s_t]
        after = [("v", E.count["v"]), ("a", E.count["a"]), ("pe", E.count["pe"])]
        for s in range(NSLOT):
            slot_free[s] = list(after)
        sq_free[:] = [after, after]
        sq_n["acc"] = after
        rstd_read["t"] = after

        s0, tl0 = load(D["gw2"][0:128, :], 128, 1024)
        s1, tl1 = load(D["gw2"][128:160, :], 32, 1024)
        o_t = [None] * 8
        for f in range(8):
            i = f % 2
            b = bank()
            t = mm(ps[:, b], bones[:, :], YT[:, f], True, True, y_t, bank_free[b], inc=True)
            t = vstt(YT[:, f], ps[:, b], -1.0 / 64, YT[:, f], MUL, ADD, t)
            bank_free[b] = [t]
            t1 = act(sqt[i], YT[:, f], ACT.Square, t, sq_free[i])
            b = bank()
            t2 = mm(ps[:, b], bones[:, :], sqt[i], True, True, t1, bank_free[b], inc=True)
            sq_free[i] = t2
            t3 = act(A[:, f], ps[:, b], ACT.Sqrt, t2, after, t_e1, scale=1.0 / 64, bias=eps6[:, 1:2])
            bank_free[b] = [t3]
            t4 = vrec(A[:, f], A[:, f], t3)
            t5 = vstt(YT[:, f], YT[:, f], vc("ln_w", f), A[:, f], MUL, MUL, t4, t1)
            t6 = vstt(YT[:, f], YT[:, f], vc("ln_b", f), V[:, f], ADD, ADD, t5)
            b = bank()
            mm(ps[:, b], ring[s0][:, 128 * f:128 * f + 128], GH[:, 0], True, False, tl0, gk, bank_free[b])
            t = mm(ps[:, b], ring[s1][0:32, 128 * f:128 * f + 128], GH[0:32, 1], False, True, tl1, inc=True)
            o_t[f] = vtt(YT[:, f], YT[:, f], ps[:, b], MUL, t, t6)
            bank_free[b] = [o_t[f]]
        slot_free[s0] = slot_free[s1] = [t]
        proj("w_o", range(8), 8, 128, lambda k: YT[:, k], o_t, residual(lambda m: md(1, 2, m), mod_t[8]))
        h_free = [after]
        hid_free = [x_t, o_t]
        t_prev = mlp(1, "mw1_1", "mw2_1", 0)

        tr_ = finish_norm(ones[:, :], 1024.0, eps6[:, 0:1], rstd)
        for f in range(8):
            x_t[f] = vstt(X[:, f], X[:, f], vc("final_g", f), rstd, MUL, MUL, tr_, x_t[f], t_cst)
            sumsq(X[:, f], f == 0, x_t[f])
        rstd_read["t"] = x_t[7]

        hdst = lambda f: H[:, f, 1:513]

        def ffn(n, gname):
            nonlocal h_free, t_prev
            hs = plain_norm(gname, hdst, w=h_free)
            hid = lambda k: AR[:, k // 8, k % 8]
            sg = [AR[:, 3, 0], AR[:, 3, 1]]
            sgf = [[t_prev], [t_prev]]
            hid_t = [None] * 22
            keep = {}

            def evac(nb, p, t):
                j, i = nb % 22, nb % 2
                if nb < 22:
                    t1 = act(sg[i], p, ACT.Sigmoid, t, sgf[i])
                    keep[j] = vtt(sg[i], sg[i], p, MUL, t1)
                    return [keep[j]]
                hid_t[j] = vtt(hid(j), sg[j % 2], p, MUL, t, keep[j], t_prev)
                sgf[j % 2] = [hid_t[j]]
                return [hid_t[j]]

            t = proj("f%dgu" % n, [x for j in range(22) for x in (j, 22 + j)], 8, 128, h, hs, evac)
            h_free = [t]
            t_prev = proj("f%dd" % n, range(8), 22, 128, hid, hid_t, residual(lambda m: 0.5, None))

        ffn(1, "ffn1_norm")

        hs = plain_norm("mix_norm", hdst, w=h_free)
        P = lambda k: AR[:, 2 + k // 8, k % 8]
        p_t = [None] * 24
        K8 = K.rearrange("p a t -> p (a t)")
        V8 = V.rearrange("p a t -> p (a t)")
        dec = K8[:, 0:2048].rearrange("p (h t) -> p h t", h=4)
        rot = K8[:, 2048:3072].rearrange("p (h t) -> p h t", h=2)
        perm = K8[:, 3072:3200]
        lq = K8[:, 3200:3456]
        t_at = dma("sp", K8[:, 0:3200], D["att"], "cd", t_prev)
        t_at = dma("sp", lq, D["lq"], "cd", t_prev)

        def p_evac(nb, p, t):
            if nb % 2:
                p_t[nb] = act(P(nb), p, ACT.Copy, t, t_prev)
            else:
                p_t[nb] = vcopy(P(nb), p, t, t_prev)
            return [p_t[nb]]
        h_free = [proj("w_in", range(24), 8, 128, h, hs, p_evac)]
        ta = vdot(K8[:, 3500:3564], lq[:, 0:64], lq[:, 64:128], st[:, 0:1], t_at)
        tb = vdot(K8[:, 3600:3664], lq[:, 128:192], lq[:, 192:256], st[:, 1:2], t_at)
        ta = act(st[:, 2:4], st[:, 0:2], ACT.Exp, ta, tb)
        ta = vtt(st[:, 4:5], st[:, 3:4], st[:, 2:3], SUB, ta)
        t_lam = vts(st[:, 4:5], st[:, 4:5], -(0.8 - 0.6 * math.exp(-0.3 * 0)), None, ADD, None, ta)
        for k in range(4):
            b = bank()
            t = mm(ps[:, b], perm, P(k), True, True, p_t[k], t_at, bank_free[b], inc=True)
            t1 = vtt(sqt[k % 2], ps[:, b], rot[:, 1], MUL, t, sq_free[k % 2])
            bank_free[b] = [t1]
            t2 = vtt(P(k), P(k), rot[:, 0], MUL, t)
            p_t[k] = vtt(P(k), P(k), sqt[k % 2], ADD, t1, t2)
            sq_free[k % 2] = p_t[k]
        rvT = XM1.rearrange("p a t -> p (a t)")[:, 0:2048].rearrange("p (c n) -> p c n", c=4)
        dvT = XM1.rearrange("p a t -> p (a t)")[:, 2048:4096].rearrange("p (c n) -> p c n", c=4)
        vv = []
        for dst, k0 in ((rvT, 4), (dvT, 20)):
            for k in range(4):
                b = bank()
                for c in range(4):
                    t = tr(ps[:, b, 128 * c:128 * c + 128], P(k0 + k)[:, 128 * c:128 * c + 128], p_t[k0 + k], bank_free[b],
                           inc=c == 3)
                t = act(dst[:, :, 128 * k:128 * k + 128], q4(ps[:, b]), ACT.Copy, t, t_prev)
                bank_free[b] = [t]
                vv.append(t)
        O = XM0
        o_t = [None] * 8
        pb_ = [V8[:, 0:512], V8[:, 512:1024]]
        pf = [[t_prev], [t_prev]]
        n_p = 0

        def head_norm(o_bank, t, dst, gcol):
            i = sq_n["n"] % 2
            sq_n["n"] += 1
            t1 = act(sqt[i], ps[:, o_bank], ACT.Square, t, sq_free[i])
            b = bank()
            t2 = mm(ps[:, b], ones[:, :], sqt[i], True, True, t1, bank_free[b], inc=True)
            t3 = act(sqt[i], ps[:, b], ACT.Sqrt, t2, scale=1.0 / 128, bias=eps6[:, 0:1])
            bank_free[b] = [t3]
            t4 = vrec(sqt[i], sqt[i], t3)
            t5 = vstt(dst, ps[:, o_bank], gcol, sqt[i], MUL, MUL, t4, t_prev)
            bank_free[o_bank] = [t5]
            sq_free[i] = t5
            return t5

        for hh in range(4):
            pp = slice(64 * (hh % 2), 64 * (hh % 2) + 64)
            q_, k_ = P(hh // 2), P(2 + hh // 2)
            ob = bank()
            for s in range(4):
                n = 512 - 128 * s
                b = bank()
                t = mm(ps[:, b, 0:n], k_[pp, 128 * s:128 * s + 128], q_[pp, 128 * s:512], True, True,
                       p_t[hh // 2], p_t[2 + hh // 2], bank_free[b], inc=True)
                i = n_p % 2
                n_p += 1
                t = vtt(pb_[i][:, 0:n], ps[:, b, 0:n], dec[:, hh, 0:n], MUL, t, pf[i], t_at)
                bank_free[b] = [t]
                t = mm(ps[:, ob, 128 * s:512], rvT[:, s, 128 * hh:128 * hh + 128], pb_[i][:, 0:n], s == 0, s == 3,
                       t, vv, bank_free[ob], inc=True)
                pf[i] = [t]
            o_t[hh] = head_norm(ob, t, O[:, hh], vc("ret_norm", hh))
        for hh in range(4):
            g = P(8 + hh)
            i = hh % 2
            t = act(sqt[i], g, ACT.Sigmoid, p_t[8 + hh], sq_free[i])
            t = vtt(sqt[i], sqt[i], g, MUL, t)
            o_t[hh] = vtt(O[:, hh], O[:, hh], sqt[i], MUL, t, o_t[hh])
            sq_free[i] = o_t[hh]

        ATb = [V8[:, 2048:4096].rearrange("p (j q) -> p j q", j=4), K8[:, 0:2048].rearrange("p (j q) -> p j q", j=4)]
        EB = [V8[:, 512 * i:512 * i + 512] for i in range(4)]
        ebf = [[pf, o_t[0:4]] for _ in range(4)]
        atf = [[t_prev], [pf, o_t[0:4]]]
        stt_n = 0
        for hh in range(4):
            dq, dk = P(12 + hh), P(16 + hh)
            ats = ATb[hh % 2]
            ev = []
            for i in range(4):
                n = 128 * (i + 1)
                es = []
                for cc in range(2):
                    pp = slice(64 * cc, 64 * cc + 64)
                    b = bank()
                    mm(ps[:, b, 0:n], dq[pp, 128 * i:128 * i + 128], dk[pp, 0:n], True, False,
                       p_t[12 + hh], p_t[16 + hh], bank_free[b])
                    t = mm(ps[:, b, n - 128:n], ident[:, :], negm[:, :], False, True, inc=True)
                    x = stt_n % 4
                    sc = stat[:, 4 * x:4 * x + 4]
                    t1 = vmax(sc[:, 0:1], ps[:, b, 0:n], t, ebf[x])
                    t2 = vts(sc[:, 1:2], sc[:, 0:1], -0.125, None, MUL, None, t1)
                    t3 = act(EB[x][:, 0:n], ps[:, b, 0:n], ACT.Exp, t2, ebf[x], scale=0.125, bias=sc[:, 1:2],
                             accum=sc[:, 2:3])
                    bank_free[b] = [t3]
                    t4 = vrec(sc[:, 3:4], sc[:, 2:3], t3)
                    es.append((x, sc, t4))
                    stt_n += 1
                (x0, s0_, ta), (x1, s1_, tb) = es
                t5 = vts(EB[x0][:, 0:n], EB[x0][:, 0:n], s0_[:, 3:4], None, MUL, None, ta)
                t6 = vtt(s1_[:, 3:4], s1_[:, 3:4], st[:, 4:5], MUL, tb, t_lam)
                t7 = vstt(EB[x0][:, 0:n], EB[x1][:, 0:n], s1_[:, 3:4], EB[x0][:, 0:n], MUL, ADD, t5, t6)
                b = bank()
                for j in range(i + 1):
                    t = tr(ps[:, b, 128 * j:128 * j + 128], EB[x0][:, 128 * j:128 * j + 128], t7, bank_free[b], inc=j == i)
                ebf[x0], ebf[x1] = [t], [t7]
                t = act(ats[:, 0:i + 1, 128 * i:128 * i + 128], ps[:, b, 0:n].rearrange("p (j q) -> p j q", q=128),
                        ACT.Copy, t, atf[hh % 2])
                bank_free[b] = [t]
                ev.append(t)
            ob = bank()
            for j in range(4):
                t = mm(ps[:, ob, 128 * j:512], dvT[:, j, 128 * hh:128 * hh + 128], ats[:, j, 128 * j:512], j == 0, j == 3,
                       ev, vv, bank_free[ob], inc=j == 3)
            atf[hh % 2] = [t]
            t = head_norm(ob, t, O[:, 4 + hh], vc("diff_norm", hh))
            o_t[4 + hh] = vts(O[:, 4 + hh], O[:, 4 + hh], 0.6 * math.exp(0.0) + 0.2, None, MUL, None, t)
        t_prev = [proj("w_out", range(8), 8, 128, lambda k: O[:, k], o_t, residual(lambda m: 1.0, None)), atf, o_t]

        hs = plain_norm("xattn_norm", hdst, w=h_free)
        MEM, MN = L, R
        t_m = dma("sp", MEM[:, :, 0:256], D["memT"], "cx", t_prev)
        Q = XM0
        q_t = [None] * 8
        t_q = {}

        def q_evac(nb, p, t):
            if nb % 2:
                q_t[nb] = act(Q[:, nb], p, ACT.Copy, t, t_prev)
            else:
                q_t[nb] = vcopy(Q[:, nb], p, t, t_prev)
            return [q_t[nb]]
        acc_save = sq_n["acc"]
        h_free = [proj("wq", range(8), 8, 128, h, hs, q_evac)]
        for f in range(8):
            sumsq(MEM[:, f, 0:256], f == 0, t_m, n=256)
        tr_ = finish_norm(ones[:, :], 1024.0, eps6[:, 0:1], rstd[:, 0:256], 256)
        ms = [vstt(MN[:, f, 0:256], MEM[:, f, 0:256], vc("mem_norm", f), rstd[:, 0:256], MUL, MUL, tr_, t_prev) for f in range(8)]
        rstd_read["t"] = ms[-1]
        kv_t = [None] * 16

        def kv_evac(nb, p, t):
            o = (XM1[:, nb, 0:256] if nb < 8 else A[:, nb - 8, 0:256])
            if nb % 2:
                kv_t[nb] = act(o, p, ACT.Copy, t, t_prev)
            else:
                kv_t[nb] = vcopy(o, p, t, t_prev)
            return [kv_t[nb]]
        proj("wkv", range(16), 8, 128, lambda k: MN[:, k, 0:256], ms, kv_evac, n=256)
        MV = K8[:, 0:2048].rearrange("p (c n) -> p c n", c=2)
        mv_t = []
        for k in range(8):
            b = bank()
            for c in range(2):
                t = tr(ps[:, b, 128 * c:128 * c + 128], A[:, k, 128 * c:128 * c + 128], kv_t[8 + k], bank_free[b], inc=c == 1)
            t = act(MV[:, :, 128 * k:128 * k + 128], q2(ps[:, b, 0:256]), ACT.Copy, t, t_prev)
            bank_free[b] = [t]
            mv_t.append(t)
        PTb = [V8[:, 2048:3072].rearrange("p (j q) -> p j q", j=2), V8[:, 3072:4096].rearrange("p (j q) -> p j q", j=2)]
        ptf = [[t_prev], [t_prev]]
        ebf = [[t_prev] for _ in range(4)]
        XO = L
        n_e = 0
        for hh in range(4):
            ev = []
            for i in range(4):
                b = bank()
                for e in range(2):
                    t = mm(ps[:, b, 0:256], Q[:, 2 * hh + e, 128 * i:128 * i + 128], XM1[:, 2 * hh + e, 0:256], e == 0, e == 1,
                           q_t[2 * hh + e], kv_t[2 * hh + e], bank_free[b], inc=e == 1)
                x = n_e % 4
                n_e += 1
                sc = stat[:, 4 * x:4 * x + 4]
                t1 = vmax(sc[:, 0:1], ps[:, b, 0:256], t, ebf[x])
                t2 = vts(sc[:, 1:2], sc[:, 0:1], -0.0625, None, MUL, None, t1)
                t3 = act(EB[x][:, 0:256], ps[:, b, 0:256], ACT.Exp, t2, ebf[x], scale=0.0625, bias=sc[:, 1:2],
                         accum=sc[:, 2:3])
                bank_free[b] = [t3]
                t4 = vrec(sc[:, 3:4], sc[:, 2:3], t3)
                t5 = vts(EB[x][:, 0:256], EB[x][:, 0:256], sc[:, 3:4], None, MUL, None, t4)
                b = bank()
                for j in range(2):
                    t = tr(ps[:, b, 128 * j:128 * j + 128], EB[x][:, 128 * j:128 * j + 128], t5, bank_free[b], inc=j == 1)
                ebf[x] = [t]
                t = act(PTb[hh % 2][:, :, 128 * i:128 * i + 128], q2(ps[:, b, 0:256]), ACT.Copy, t, ptf[hh % 2])
                bank_free[b] = [t]
                ev.append(t)
            for e in range(2):
                b = bank()
                for j in range(2):
                    t = mm(ps[:, b], MV[:, j, 256 * hh + 128 * e:256 * hh + 128 * e + 128], PTb[hh % 2][:, j], j == 0, j == 1,
                           ev, mv_t, bank_free[b], inc=j == 1)
                k = 2 * hh + e
                o_t[k] = vcopy(XO[:, k], ps[:, b], t, ms)
                bank_free[b] = [o_t[k]]
            ptf[hh % 2] = [t]
        t_prev = proj("wo", range(8), 8, 128, lambda k: XO[:, k], o_t, residual(lambda m: 1.0, None))

        ffn(2, "ffn2_norm")
        tr_ = finish_norm(ones[:, :], 1024.0, eps6[:, 0:1], rstd)
        for f in range(8):
            t = vstt(XM0[:, f], X[:, f], vc("final_norm", f), rstd, MUL, MUL, tr_, x_t[f], t_prev)
            t_out = dma("sp", out[:, f, :], XM0[:, f], "out", t)
        E.emit("sp", lambda e: e.nop(), [t_out])

        block = ctx.enter_context(nc.Block())

        @block.sync
        def _(eng):
            E.play("sp", eng)

        @block.gpsimd
        def _(eng):
            E.play("g", eng)

        @block.scalar
        def _(eng):
            E.play("a", eng)

        @block.vector
        def _(eng):
            E.play("v", eng)

        @block.tensor
        def _(eng):
            E.play("pe", eng)


def kernel(**inp):
    import numpy as np
    import concourse.bacc as bacc
    from concourse import mybir as mb
    from concourse.bass_utils import run_bass_kernel_spmd as run

    a = {k: np.asarray(v) for k, v in inp.items()}

    def blocks(w, m=128):
        K, N = w.shape
        return w.reshape(K // 128, 128, N // m, m).transpose(2, 1, 0, 3).reshape(N // m, 128, K // 128 * m)

    def feat(v):
        return v.reshape(-1, 128).T

    d = {}
    d["xT"] = a["x"][0].T.reshape(8, 128, 512).transpose(1, 0, 2)
    d["memT"] = a["mem_2"][0].T.reshape(8, 128, 256).transpose(1, 0, 2)
    d["cb"] = np.broadcast_to(a["c"], (128, 1024))
    d["adab"] = feat(a["ada_b"].reshape(-1))
    d["adaw"] = a["ada_w"].transpose(0, 2, 1).reshape(96, 128, 1024)
    pad = np.zeros((128, 4), np.float32)
    cols = {"g00": a["norm_g"][0, 0], "g01": a["norm_g"][0, 1], "g10": a["norm_g"][1, 0], "g11": a["norm_g"][1, 1],
            "final_g": a["final_g"], "cw0": a["conv_w"][0, 0], "cw1": a["conv_w"][0, 1], "cw2": a["conv_w"][0, 2],
            "w0": a["rw_w0"], "a0": a["rw_a0"], "k_k": a["rw_k_k"], "k_a": a["rw_k_a"], "r_k": a["rw_r_k"],
            "ln_w": a["rw_ln_w"], "ln_b": a["rw_ln_b"], "ffn1_norm": a["ffn1_norm_2"], "mix_norm": a["mix_norm_2"],
            "xattn_norm": a["xattn_norm_2"], "mem_norm": a["mem_norm_2"], "ffn2_norm": a["ffn2_norm_2"],
            "final_norm": a["final_norm_2"], "ret_norm": a["ret_out_norm_2"], "diff_norm": a["diff_out_norm_2"]}
    for i in range(6):
        cols["mu%d" % i] = a["rw_mu"][0, i]
    d["vec"] = np.concatenate([x for n in VECS for x in ([feat(cols[n].reshape(-1))] +
                                                         ([pad] if cols[n].size == 512 else []))], axis=1)
    d["cw_in"] = blocks(a["conv_w_in"][0])
    d["cw_out"] = blocks(a["conv_w_out"][0])
    for i in range(2):
        d["mw1_%d" % i] = blocks(a["mlp_w1"][i])
        d["mw2_%d" % i] = blocks(a["mlp_w2"][i])
    d["wr"], d["wk"], d["wv"] = [blocks(a["rw_w_rkv"][0, i]) for i in range(3)]
    d["w_o"] = blocks(a["rw_w_o"][0])
    d["dw1"] = blocks(a["rw_w1"][0], 64)
    d["aw1"] = blocks(a["rw_a1"][0], 64)
    d["dw2"] = a["rw_w2"][0]
    d["aw2"] = a["rw_a2"][0]
    d["gw1a"] = blocks(a["rw_g1"][0][:, 0:128])
    d["gw1b"] = blocks(a["rw_g1"][0][:, 128:160], 32)
    d["gw2"] = a["rw_g2"][0]
    for i in (1, 2):
        d["f%dgu" % i] = np.concatenate([blocks(a["ffn%d_w_gate_2" % i][0]), blocks(a["ffn%d_w_up_2" % i][0])])
        d["f%dd" % i] = blocks(a["ffn%d_w_down_2" % i][0])
    d["w_in"] = blocks(a["w_in_2"][0])
    d["w_out"] = blocks(a["w_out_2"][0])
    d["wq"] = blocks(a["xattn_wq_2"][0])
    d["wkv"] = blocks(a["xattn_wkv_2"][0])
    d["wo"] = blocks(a["xattn_wo_2"][0])
    d["lq"] = np.broadcast_to(np.concatenate([a["diff_lq1_2"], a["diff_lk1_2"], a["diff_lq2_2"], a["diff_lk2_2"]], 1), (128, 256))

    i = np.arange(128)
    d["ident"] = np.eye(128, dtype=np.float32)
    d["bones"] = (i[:, None] // 64 == i[None, :] // 64).astype(np.float32)
    d["negm"] = np.where(i[None, :] > i[:, None], np.float32(-1e30), np.float32(0))
    same = i[:, None] // 16 == i[None, :] // 16
    lt = i[:, None] < i[None, :]
    d["mD"] = np.tile((lt & same).astype(np.float32), (1, 2))
    d["mE"] = np.tile((lt & ~same).astype(np.float32), (1, 2))
    d["mR"] = np.tile((i[:, None] <= i[None, :]).astype(np.float32), (1, 2))
    rel = np.arange(512)[None, :] - i[:, None]
    dec = []
    for hh in range(4):
        lg = np.log(1.0 - 2.0 ** (-5.0 - hh))
        dec.append(np.where(rel >= 0, np.exp(np.maximum(rel, 0) * lg), 0.0) * 64.0 ** -0.5)
    inv = (1.0 / (np.float32(10000.0) ** (np.arange(0, 64, 2, dtype=np.float32) / np.float32(64)))).astype(np.float32)
    ang = (np.arange(512, dtype=np.float32)[None, :] * inv[i % 32][:, None]).astype(np.float32).astype(np.float64)
    perm = np.zeros((128, 128))
    for m in range(128):
        if m % 64 < 32:
            perm[m + 32, m] = -1.0
        else:
            perm[m - 32, m] = 1.0
    d["att"] = np.concatenate(dec + [np.cos(ang), np.sin(ang), perm], axis=1).astype(np.float32)

    nc = bacc.Bacc("TRN2", target_bir_lowering=False, num_devices=1)
    arrays, D = {}, {}
    for n, v in d.items():
        v = np.ascontiguousarray(v)
        arrays["in_" + n] = v
        D[n] = nc.dram_tensor("in_" + n, v.shape, mb.dt.from_np(v.dtype), kind="ExternalInput").ap()
    o = nc.dram_tensor("out_dram", (128, 8, 512), mb.dt.float32, kind="ExternalOutput").ap()
    build(nc, D, o)
    r = run(nc, [arrays], core_ids=[0])
    got = r.results[0]["out_dram"]
    return np.ascontiguousarray(got.transpose(2, 1, 0).reshape(1, 512, 1024))
```

```python
from contextlib import ExitStack
import math

from concourse import mybir

F32 = mybir.dt.float32
F32R = mybir.dt.float32r
U32 = mybir.dt.uint32
ALU = mybir.AluOpType
ACT = mybir.ActivationFunctionType
AX = mybir.AxisListType.X

MUL, ADD, SUB, MAXO = ALU.mult, ALU.add, ALU.subtract, ALU.max

VECS = ["g00", "g01", "g10", "g11", "final_g", "cw0", "cw1", "cw2",
        "mu0", "mu1", "mu2", "mu3", "mu4", "mu5", "w0", "a0", "k_k", "k_a", "r_k", "ln_w", "ln_b",
        "ffn1_norm", "mix_norm", "xattn_norm", "mem_norm", "ffn2_norm", "final_norm",
        "ret_norm", "diff_norm"]
VOFF = {n: 8 * i for i, n in enumerate(VECS)}

NRAW = 4
NSPLIT = 3
NADA = 6
AHEAD = 2

PROJ = [("cw_in", "k", 24, 8), ("cw_out", "m", 8, 8),
        ("mw1_0a", "k", 16, 8), ("mw2_0a", "m", 8, 16), ("mw1_0b", "k", 16, 8), ("mw2_0b", "m", 8, 16),
        ("dw1", "m", 1, 8), ("aw1", "m", 1, 8), ("aw2", "k", 8, 1), ("gw1", "m", 2, 8),
        ("wv", "k", 8, 8), ("wk", "k", 8, 8), ("dw2", "k", 8, 1), ("wr", "k", 8, 8),
        ("gw2", "k", 8, 2), ("w_o", "m", 8, 8),
        ("mw1_1a", "k", 16, 8), ("mw2_1a", "m", 8, 16), ("mw1_1b", "k", 16, 8), ("mw2_1b", "m", 8, 16),
        ("f1gu", "k", 40, 8), ("f1gux", "k", 4, 8), ("f1d", "m", 8, 22),
        ("w_in", "k", 24, 8), ("w_out", "m", 8, 8), ("wq", "k", 8, 8), ("wkv", "k", 16, 8), ("wo", "m", 8, 8),
        ("f2gu", "k", 40, 8), ("f2gux", "k", 4, 8), ("f2d", "m", 8, 22)]


def pieces():
    out = []
    for name, kind, nb, kc in PROJ:
        if kind == "k":
            out += [(name, g, k, min(8, nb)) for g in range(max(1, nb // 8)) for k in range(kc)]
        else:
            out += [(name, b, k, min(8, kc - k)) for b in range(nb) for k in range(0, kc, 8)]
    return out


class Engines:

    def __init__(self, sems):
        self.sems = sems
        self.q = {n: [] for n in ("pe", "v", "a", "g", "sp")}
        self.count = {n: 0 for n in sems}
        self.seen = {n: {} for n in self.q}

    def emit(self, eng, fn, waits, sem=None, by=1):
        for s, v in flat(waits):
            if self.seen[eng].get(s, 0) < v:
                self.seen[eng][s] = v
                self.q[eng].append((None, self.sems[s], v))
        if sem is None:
            self.q[eng].append((fn, None, 0))
            return None
        self.count[sem] += by
        self.q[eng].append((fn, self.sems[sem], by))
        return (sem, self.count[sem])

    def play(self, name, eng):
        for fn, sem, v in self.q[name]:
            if fn is None:
                eng.wait_ge(sem, v)
            elif sem is None:
                fn(eng)
            else:
                fn(eng).then_inc(sem, v)


def flat(ts):
    out = []
    for t in ts:
        if t is None:
            continue
        if isinstance(t, tuple) and len(t) == 2 and isinstance(t[0], str):
            out.append(t)
        else:
            out += flat(t)
    return out


def build(nc, D, out):
    ctx = ExitStack()
    with ctx:
        def sb(name, shape, dt=F32):
            return ctx.enter_context(nc.sbuf_tensor(name, shape, dt))

        names = ["pe", "v", "a", "g", "out", "cst", "cx", "cd"] + [f"r{i}" for i in range(NRAW)] + \
                [f"d{i}" for i in range(NADA)]
        sems = {n: ctx.enter_context(nc.semaphore("s_" + n)) for n in names}
        E = Engines(sems)

        ps = ctx.enter_context(nc.psum_tensor("ps", [128, 8, 512], F32))
        X = sb("X", [128, 8, 512])
        GH = sb("GH", [128, 2, 512])
        vec = sb("vec", [128, 8 * len(VECS)])
        ident = sb("ident", [128, 128])
        bones = sb("bones", [128, 128])
        ones = sb("ones", [128, 128])
        negm = sb("negm", [128, 128])
        msk = sb("msk", [128, 768])
        mod = sb("mod", [128, 96])
        adab = sb("adab", [128, 96])
        coef = sb("coef", [128, 8])
        omu = sb("omu", [128, 48])
        lmid = sb("lmid", [128, 8, 4])
        fct = sb("fct", [128, 8, 4])
        st = sb("st", [128, 8])
        stat = sb("stat", [128, 32])
        eps6 = sb("eps6", [128, 2])

        SQ = (nc.sbuf_base + 31) // 32 * 32
        RG = SQ + 8192
        WK = RG + 40960

        def at_(name, off, shape, dt=F32):
            return nc.alloc_sbuf_tensor_at(name, shape, dt, offset=off)

        sqa = at_("sqa", SQ, [128, 4, 512])
        sqt = [sqa[:, 0], sqa[:, 1]]
        acc, rstd = sqa[:, 2], sqa[:, 3]
        raw_ = at_("raw", RG, [128, NRAW, 1024])
        WHs = at_("WHs", RG + 16384, [128, NSPLIT, 1024], F32R)
        WLs = at_("WLs", RG + 16384 + 4096 * NSPLIT, [128, NSPLIT, 1024], F32R)
        HH = at_("HH", WK, [128, 8, 512], F32R)
        HL = at_("HL", WK + 16384, [128, 8, 512], F32R)
        HID = at_("HID", WK + 32768, [128, 2, 22, 512], F32R)
        tmp_ = at_("tmp", WK + 122880, [128, 4, 512])
        cbc = at_("cbc", WK + 131072, [128, 1024])[:, :]
        ada = at_("ada", WK + 98304, [128, NADA, 1024])
        HM = at_("HM", WK + 32768, [128, 2, 16, 512], F32R)
        cvt = at_("cvt", WK + 49152, [128, 2 * 528 + 2 * 512])
        HP = at_("HP", WK, [128, 8 * 513])
        MX = [[at_("M%d%s" % (i, n), WK + 16416 + 32768 * i + 16384 * j, [128, 8, 512], F32R) for j, n in enumerate("HL")]
              for i in range(2)]
        LR = at_("LR", WK + 16416, [128, 2, 8, 512])
        VY = at_("VY", WK + 49184, [128, 2, 8, 512])
        KVA = at_("KVA", WK + 81952, [128, 3, 8, 512])
        T64w = at_("T64w", WK + 131104, [128, 2, 512], F32R)
        T64a = at_("T64a", WK + 98336, [128, 2, 512], F32R)
        GHs = at_("GHs", WK + 49184, [128, 2, 2, 512], F32R)
        nb_ = at_("nb", RG, [128, 9728])
        Pq = at_("Pq", WK + 32768, [128, 24, 512])
        rdT = at_("rdT", WK + 81920, [128, 2, 4, 512])
        att = at_("att", WK + 98304, [128, 3584])
        atb = at_("atb", WK + 112640, [128, 2, 4, 512])
        Qx = at_("Qx", WK + 32768, [128, 8, 512])
        MEM = at_("MEM", WK + 49152, [128, 8, 256])
        MNs = at_("MNs", WK + 57344, [128, 2, 8, 256], F32R)
        KTm = at_("KTm", WK + 73728, [128, 8, 256])
        VFm = at_("VFm", WK + 81920, [128, 8, 256])
        MV = at_("MV", WK + 90112, [128, 2, 1024])
        PTx = at_("PTx", WK + 98304, [128, 2, 2, 512])
        EBx = at_("EBx", WK + 106496, [128, 4, 256])
        tmp2 = at_("tmp2", WK + 112640, [128, 4, 512])
        OUT = at_("OUT", WK + 32768, [128, 8, 512])

        H = HP[:, :].rearrange("p (f t) -> p f t", t=513)
        H8 = HP[:, 0:4096].rearrange("p (f t) -> p f t", t=512)
        L, R = LR[:, 0], LR[:, 1]
        K, V, A = KVA[:, 0], KVA[:, 1], KVA[:, 2]

        def act(o, i, func, *w, scale=1.0, bias=0.0, accum=None):
            if accum is not None:
                return E.emit("a", lambda e: e.activation(o, i, func, bias=bias, scale=scale, accum_out=accum), w, "a")
            return E.emit("a", lambda e: e.activation(o, i, func, bias=bias, scale=scale), w, "a")

        def gtt(o, a, b, op, *w):
            return E.emit("g", lambda e: e.tensor_tensor(o, a, b, op), w, "g")

        def warm(func):
            return act(st[:, 7:8], eps6[:, 0:1], func, t_e0, ("a", E.count["a"]))

        def vcopy(o, i, *w):
            return E.emit("v", lambda e: e.tensor_copy(o, i), w, "v")

        def vtt(o, a, b, op, *w):
            return E.emit("v", lambda e: e.tensor_tensor(o, a, b, op), w, "v")

        def vts(o, a, s1, s2, op0, op1, *w):
            if op1 is None:
                return E.emit("v", lambda e: e.tensor_scalar(o, a, s1, None, op0), w, "v")
            return E.emit("v", lambda e: e.tensor_scalar(o, a, s1, s2, op0, op1), w, "v")

        def vstt(o, a, s, b, op0, op1, *w):
            return E.emit("v", lambda e: e.scalar_tensor_tensor(out=o, in0=a, scalar=s, in1=b, op0=op0, op1=op1), w, "v")

        def vrec(o, i, *w):
            return E.emit("v", lambda e: e.reciprocal(o, i), w, "v")

        def vset(o, val, *w):
            return E.emit("v", lambda e: e.memset(o, val), w, "v")

        def vpred(o, m, d, *w):
            return E.emit("v", lambda e: e.copy_predicated(o, m, d), w, "v")

        def vdot(junk, a, b, o, *w):
            return E.emit("v", lambda e: e.tensor_tensor_reduce(junk, a, b, 1.0, 0.0, MUL, ADD, o), w, "v")

        def vscan(o, d0, d1, *w):
            return E.emit("v", lambda e: e.tensor_tensor_scan(o, d0, d1, 0.0, MUL, ADD), w, "v")

        def vmax(o, i, *w):
            return E.emit("v", lambda e: e.tensor_reduce(o, i, AX, MAXO), w, "v")

        def mm(o, lhsT, rhs, start, stop, *w, inc=False):
            return E.emit("pe", lambda e: e.matmul(o, lhsT, rhs, start=start, stop=stop), w, "pe" if inc else None)

        def tr(o, i, *w, inc=False):
            return E.emit("pe", lambda e: e.transpose(o, i, ident[:, :]), w, "pe" if inc else None)

        def dma(eng, o, i, sem, *w):
            return E.emit(eng, lambda e: e.dma_start(o, i), w, sem, 16)

        bank_free = [[] for _ in range(8)]
        at = {"bank": 0, "ada": 0}
        ada_free = [[] for _ in range(NADA)]

        def bank():
            b = at["bank"]
            at["bank"] = (b + 1) % 8
            return b

        want = pieces()
        raw_t, raw_free = {}, [[] for _ in range(NRAW)]
        spl_t, spl_free = {}, [[] for _ in range(NSPLIT)]
        nx = {"dma": 0, "split": 0, "use": 0, "stop": [w[0] for w in want].index("gw2")}

        def ahead():
            while nx["split"] < min(nx["use"] + AHEAD + 1, nx["stop"]):
                u = nx["split"]
                s, r = u % NSPLIT, u % NRAW
                n = want[u][3] * 128
                while nx["dma"] <= u:
                    dma_piece()
                th = act(WHs[:, s, 0:n], raw_[:, r, 0:n], ACT.Copy, raw_t[u], spl_free[s])
                tl = vtt(WLs[:, s, 0:n], raw_[:, r, 0:n], WHs[:, s, 0:n].bitcast(F32), SUB, th)
                spl_t[u] = [th, tl]
                raw_free[r] = [tl]
                nx["split"] += 1
            while nx["dma"] < min(nx["split"] + NRAW, nx["stop"]):
                dma_piece()

        def dma_piece():
            u = nx["dma"]
            name, a_, k, n = want[u]
            src = D[name][a_, k] if kinds[name] == "k" else D[name][a_, :, 128 * k:128 * (k + n)]
            raw_t[u] = dma("sp", raw_[:, u % NRAW, 0:128 * n], src, f"r{u % NRAW}", raw_free[u % NRAW])
            nx["dma"] += 1

        kinds = {n: k for n, k, _, _ in PROJ}
        sizes = {n: (nb, kc) for n, _, nb, kc in PROJ}

        def piece(*key):
            u = nx["use"]
            assert want[u][0:3] == key, (want[u], key)
            ahead()
            nx["use"] += 1
            return u % NSPLIT, spl_t[u]

        for f in range(0, 8, 4):
            dma("sp", X[:, f:f + 4, :], D["xT"][:, f:f + 4, :], "cx")
        t_c = dma("sp", cbc, D["cb"], "cx")
        t_ab = dma("sp", adab[:, :], D["adab"], "cst")
        dma("sp", vec[:, :], D["vec"], "cst")
        dma("sp", ident[:, :], D["ident"], "cst")
        dma("sp", bones[:, :], D["bones"], "cst")
        dma("sp", negm[:, :], D["negm"], "cst")
        t_cst = dma("sp", msk[:, :], D["msk"], "cst")
        t_x = t_c
        t_one = vset(ones[:, :], 1.0)
        t_e0 = vset(eps6[:, 0:1], 1e-6)
        t_e1 = vset(eps6[:, 1:2], 64e-5)
        def vc(name, f, w=1):
            return vec[:, VOFF[name] + f:VOFF[name] + f + w]

        t = act(sqt[0], cbc[:, 0:512], ACT.Sigmoid, t_c)
        t2 = act(sqt[1], cbc[:, 512:1024], ACT.Sigmoid, t_c)
        t_s = [vtt(cbc[:, 0:512], cbc[:, 0:512], sqt[0], MUL, t), vtt(cbc[:, 512:1024], cbc[:, 512:1024], sqt[1], MUL, t2)]
        sq_free = [t_s[0], t_s[1]]

        mod_t = {}

        def ada_step(n=1):
            for _ in range(n):
                u = at["ada"]
                if u >= 96:
                    return
                at["ada"] = u + 1
                s = u % NADA
                t = dma("g", ada[:, s], D["adaw"][u], f"d{s}", ada_free[s])
                tt = vdot(ada[:, s], ada[:, s], cbc, mod[:, u:u + 1], t, t_s)
                ada_free[s] = [tt]
                if u % 8 == 7:
                    mod_t[u // 8] = vtt(mod[:, u - 7:u + 1], mod[:, u - 7:u + 1], adab[:, u - 7:u + 1], ADD, tt, t_ab, t_cst)

        def md(layer, j, f):
            u = layer * 48 + j * 8 + f
            return mod[:, u:u + 1]

        sq_n = {"n": 0, "acc": None}

        def sumsq(src, first, *w, n=512):
            i = sq_n["n"] % 2
            sq_n["n"] += 1
            t = act(sqt[i][:, 0:n], src, ACT.Square, sq_free[i], w)
            if first:
                t = vcopy(acc[:, 0:n], sqt[i][:, 0:n], t, sq_n["acc"])
            else:
                t = vtt(acc[:, 0:n], acc[:, 0:n], sqt[i][:, 0:n], ADD, t, sq_n["acc"])
            sq_n["acc"] = t
            sq_free[i] = t
            return t

        rstd_read = {"t": []}

        def finish_norm(lhsT, count, eps, o, n=512, src=None, w=()):
            b = bank()
            t = mm(ps[:, b, 0:n], lhsT, acc[:, 0:n] if src is None else src, True, True,
                   sq_n["acc"], bank_free[b], t_one, t_cst, w, inc=True)
            if src is None:
                sq_n["acc"] = t
            ta = act(o, ps[:, b, 0:n], ACT.Sqrt, t, rstd_read["t"], t_e0, t_e1, scale=1.0 / count, bias=eps)
            bank_free[b] = [ta]
            return vrec(o, o, ta)

        def mm3(o, s, c, x, start, stop, *w, inc=False):
            hi, lo = x
            mm(o, WHs[:, s, c], hi, start, False, w)
            mm(o, WHs[:, s, c], lo, False, False)
            return mm(o, WLs[:, s, c], hi, False, stop, inc=inc)

        def proj(name, rhs, rhs_t, evac, n=512, each=None):
            nb, kc = sizes[name]
            if kinds[name] == "k":
                w = min(8, nb)
                for g in range(nb // w):
                    bs = [bank() for _ in range(w)]
                    for k in range(kc):
                        s, tw = piece(name, g, k)
                        for m in range(w):
                            last = k == kc - 1
                            t = mm3(ps[:, bs[m], 0:n], s, slice(128 * m, 128 * m + 128), rhs(k), k == 0, last,
                                    tw, rhs_t[k], bank_free[bs[m]] if k == 0 else None, inc=last or m == w - 1)
                            if last:
                                bank_free[bs[m]] = [t]
                        spl_free[s] = [t]
                        if each:
                            each()
                    for m in range(w):
                        t_m = bank_free[bs[m]][0]
                        bank_free[bs[m]] = evac(g * w + m, ps[:, bs[m], 0:n], t_m)
            else:
                for m in range(nb):
                    b = bank()
                    for k0 in range(0, kc, 8):
                        s, tw = piece(name, m, k0)
                        k1 = min(kc, k0 + 8)
                        for k in range(k0, k1):
                            t = mm3(ps[:, b, 0:n], s, slice(128 * (k - k0), 128 * (k - k0) + 128), rhs(k), k == 0,
                                    k == kc - 1, tw, rhs_t[k], bank_free[b] if k == 0 else None, inc=k == k1 - 1)
                        spl_free[s] = [t]
                        if each:
                            each()
                    bank_free[b] = evac(m, ps[:, b, 0:n], t)
            return t

        for f in range(8):
            tq = sumsq(X[:, f], f == 0, t_x)
        x_t = [t_x] * 8
        h_free = []

        def modulated(layer, j, gname, full=False):
            nonlocal h_free
            warm(ACT.Sqrt)
            tr_ = finish_norm(ones[:, :], 1024.0, eps6[:, 0:1], rstd)
            hs = []
            tc = vstt(coef[:, 0:8], mod[:, layer * 48 + (j + 1) * 8:layer * 48 + (j + 2) * 8], 1.0, vc(gname, 0, 8),
                      ADD, MUL, mod_t[layer * 6 + j + 1], t_cst, h_free)
            for f in range(8):
                if full:
                    t = vstt(H[:, f, 1:513], X[:, f], coef[:, f:f + 1], rstd, MUL, MUL, tr_, tc, x_t[f], h_free)
                    hs.append(act(H[:, f, 1:513], H[:, f, 1:513], ACT.Identity, t, mod_t[layer * 6 + j],
                                  bias=md(layer, j, f)))
                    continue
                i = f % 2
                t = vstt(sqt[i], X[:, f], coef[:, f:f + 1], rstd, MUL, MUL, tr_, tc, x_t[f], sq_free[i])
                th = act(HH[:, f], sqt[i], ACT.Identity, t, mod_t[layer * 6 + j], h_free, bias=md(layer, j, f))
                tl = vstt(HL[:, f], sqt[i], md(layer, j, f), HH[:, f].bitcast(F32), ADD, SUB, th)
                sq_free[i] = tl
                hs.append([th, tl])
            rstd_read["t"] = hs[-1] if not full else t
            return hs

        def split(hi, lo, x, t, *w, eng="v"):
            th = act(hi, x, ACT.Copy, t, w)
            if eng == "v":
                return [th, vtt(lo, x, hi.bitcast(F32), SUB, th, w)]
            return [th, gtt(lo, x, hi.bitcast(F32), SUB, th, w)]

        def plain_norm(gname, n=512, src=X, hi=HH, lo=HL, w=None):
            tr_ = finish_norm(ones[:, :], 1024.0, eps6[:, 0:1], rstd[:, 0:n], n)
            hs = []
            for f in range(8):
                i = f % 2
                t = vstt(sqt[i][:, 0:n], src[:, f, 0:n], vc(gname, f), rstd[:, 0:n], MUL, MUL, tr_, x_t[f], w, t_cst,
                         sq_free[i])
                r = split(hi[:, f], lo[:, f], sqt[i][:, 0:n], t, w)
                sq_free[i] = r[1]
                hs.append(r)
            rstd_read["t"] = hs[-1]
            return hs

        def residual(gate, extra, last=True):
            def evac(m, p, t):
                if m == 0 and last:
                    warm(ACT.Sqrt)
                t1 = vstt(X[:, m], p, gate(m), X[:, m], MUL, ADD, t, x_t[m], extra)
                x_t[m] = t1
                if last:
                    sumsq(X[:, m], m == 0, t1)
                return [t1]
            return evac

        ada_step(16)
        hs = modulated(0, 0, "g00")
        cg = [cvt[:, 512 * i:512 * i + 512] for i in range(2)]
        cv = [tmp_[:, i] for i in range(4)]
        uu = [cvt[:, 1024 + 528 * i:1024 + 528 * i + 514] for i in range(2)]
        cgf = [[], []]
        up = [vset(u[:, 0:2], 0.0) for u in uu]
        uf = [[], []]
        cvf = [[] for _ in range(4)]
        z_t = [None] * 8
        h = lambda k: (HH[:, k], HL[:, k])
        hm = lambda k: (HM[:, 0, k], HM[:, 1, k])
        hid = lambda k: (HID[:, 0, k], HID[:, 1, k])
        keep = {}

        def conv_evac(n, p, t):
            j, what = n // 3, n % 3
            i, c = j % 2, j % 4
            if what == 0:
                keep["c"] = act(cg[i], p, ACT.Copy, t, cgf[i])
                return [keep["c"]]
            if what == 1:
                t1 = vtt(uu[i][:, 2:514], cg[i], p, MUL, t, keep["c"], uf[i])
                cgf[i] = [t1]
                t2 = vts(cv[c], uu[i][:, 0:512], vc("cw0", j), None, MUL, None, t1, up, cvf[c])
                t3 = vstt(cv[c], uu[i][:, 1:513], vc("cw1", j), cv[c], MUL, ADD, t2)
                keep["z"] = vstt(cv[c], uu[i][:, 2:514], vc("cw2", j), cv[c], MUL, ADD, t3)
                uf[i] = [keep["z"]]
                return [t1]
            t1 = vtt(cv[c], cv[c], p, MUL, t, keep["z"])
            z_t[j] = split(HM[:, 0, j], HM[:, 1, j], cv[c], t1)
            cvf[c] = z_t[j]
            return [t1]

        t = proj("cw_in", h, hs, conv_evac, each=ada_step)
        h_free = [t]
        proj("cw_out", hm, z_t, residual(lambda m: md(0, 2, m), mod_t[2]))

        tmf = [[z_t] for _ in range(4)]

        def mlp(layer, each=None):
            nonlocal h_free
            hs = modulated(layer, 3, "g%d1" % layer)
            for half in range(2):
                hid_t = [None] * 16

                def up_evac(nb, p, t):
                    i = nb % 4
                    t1 = act(tmp_[:, i], p, ACT.Relu, t, tmf[i])
                    th = act(HM[:, 0, nb], tmp_[:, i], ACT.Square, t1)
                    t2 = vtt(tmp_[:, i], tmp_[:, i], tmp_[:, i], MUL, th)
                    tl = vtt(HM[:, 1, nb], tmp_[:, i], HM[:, 0, nb].bitcast(F32), SUB, t2)
                    hid_t[nb] = [th, tl]
                    tmf[i] = [tl]
                    return [t1]

                x = "%d%s" % (layer, "ab"[half])
                t = proj("mw1_" + x, h, hs, up_evac, each=each)
                h_free = [t]
                g = residual(lambda m: md(layer, 5, m), mod_t.get(6 * layer + 5, []), half == 1)
                t = proj("mw2_" + x, hm, hid_t, gate_late(g, layer), each=each)
            return t

        def gate_late(g, layer):
            def evac(m, p, t):
                return g(m, p, [t, mod_t[6 * layer + 5]])
            return evac

        t_prev = mlp(0, ada_step)
        assert at["ada"] == 96

        hs = modulated(1, 0, "g10", True)
        pad = vset(H[:, :, 0:1], 0.0, t_prev)
        for i in range(6):
            t_omu = vts(omu[:, 8 * i:8 * i + 8], vc("mu%d" % i, 0, 8), -1.0, 1.0, MUL, ADD, t_cst)
        xm_free = [[t_prev], [t_prev]]
        xm = lambda i: (lambda k: (MX[i][0][:, k], MX[i][1][:, k]))
        mix_read = []

        def mix(mu, i):
            ts = []
            for f in range(8):
                j = f % 2
                ta = act(sqt[j], H[:, f, 1:513], ACT.Identity, hs[f], t_omu, sq_free[j],
                         scale=omu[:, 8 * mu + f:8 * mu + f + 1])
                tb = vstt(sqt[j], H[:, f, 0:512], vc("mu%d" % mu, f), sqt[j], MUL, ADD, ta, hs[f], pad)
                r = split(MX[i][0][:, f], MX[i][1][:, f], sqt[j], tb, xm_free[i], eng="g")
                sq_free[j] = r
                ts.append(r)
            mix_read[:] = [tb]
            return ts

        gh_free = []

        def small_evac(func, hi, lo, toks, mul=1.0):
            def f(nb, p, t):
                t1 = act(GH[:, nb], p, func, t, gh_free)
                toks.append(t1)
                if hi is not None:
                    toks[-1] = split(hi, lo, GH[:, nb], t1, t_prev)
                    gh_free[:] = toks[-1]
                return [t1]
            return f

        def sig_evac(dst, bias, toks, w):
            def f(nb, p, t):
                toks[nb] = act(dst[:, nb], p, ACT.Sigmoid, t, w, t_cst, bias=vc(bias, nb))
                return [toks[nb]]
            return f

        def copy_evac(dst, toks, w):
            def f(nb, p, t):
                if nb % 2:
                    toks[nb] = act(dst[:, nb], p, ACT.Copy, t, w)
                else:
                    toks[nb] = vcopy(dst[:, nb], p, t, w)
                return [toks[nb]]
            return f

        ts = mix(1, 0)
        ts2 = mix(4, 1)
        tw, ta_, gk = [], [], []
        a_t, k_t, v_t, r_t, l_t = [[None] * 8 for _ in range(5)]
        t0 = proj("dw1", xm(0), ts, small_evac(ACT.Tanh, T64w[:, 0], T64w[:, 1], tw))
        xm_free[0] = [t0]
        ts = mix(5, 0)
        t0 = proj("aw1", xm(1), ts2, small_evac(ACT.Copy, T64a[:, 0], T64a[:, 1], ta_))
        xm_free[1] = [t0]
        ts2 = mix(3, 1)
        proj("aw2", lambda k: (T64a[:, 0], T64a[:, 1]), ta_, sig_evac(A, "a0", a_t, t_prev))
        t0 = proj("gw1", xm(0), ts, small_evac(ACT.Sigmoid, None, None, gk))
        xm_free[0] = [t0]
        ts = mix(2, 0)
        t0 = proj("wv", xm(1), ts2, copy_evac(V, v_t, t_prev))
        xm_free[1] = [t0]
        ts2 = mix(0, 1)
        t_kdone = proj("wk", xm(0), ts, copy_evac(K, k_t, t_prev))
        proj("dw2", lambda k: (T64w[:, 0], T64w[:, 1]), tw, sig_evac(L, "w0", l_t, t_kdone))

        kk_t, kp_t, lc_t, x_1, ksq = [[None] * 8 for _ in range(5)]
        cmask = acc
        t1 = vset(cmask, 1.0, sq_n["acc"])
        t_cm = vset(cmask[:, 0:512:128], 0.0, t1)
        state = {"f": 0}
        VT = VY[:, 0].rearrange("p a t -> p (a t)").rearrange("p (c n) -> p c n", c=4)
        YT = VY[:, 1]

        def kk_norm(f):
            b = bank()
            t2 = mm(ps[:, b], bones[:, :], sqt[f % 2], True, True, ksq[f], t_cst, bank_free[b], inc=True)
            sq_free[f % 2] = t2
            return b, t2

        def while_r():
            f = state["f"]
            state["f"] += 1
            t0 = vts(H8[:, f], K[:, f], vc("k_k", f), None, MUL, None, k_t[f], mix_read, hs)
            kk_t[f] = t0
            t2 = vts(L[:, f], L[:, f], -math.exp(-0.5), None, MUL, None, l_t[f])
            l_t[f] = t2
            t1 = vts(sqt[f % 2], A[:, f], 1.0, vc("k_a", f), SUB, MUL, a_t[f], sq_free[f % 2])
            kp_t[f] = vstt(K[:, f], sqt[f % 2], 1.0, K[:, f], ADD, MUL, t1, t0)
            sq_free[f % 2] = kp_t[f]
            a_t[f] = gtt(A[:, f], H8[:, f], A[:, f], MUL, kp_t[f])

        t_r = proj("wr", xm(1), ts2, copy_evac(R, r_t, t_kdone), each=while_r)
        after_r = [t_r]
        for f in range(8):
            b = bank()
            for c in range(4):
                t = tr(ps[:, b, 128 * c:128 * c + 128], V[:, f, 128 * c:128 * c + 128], v_t[f], bank_free[b], t_cst,
                       inc=c == 3)
            v_t[f] = t
            i = f % 2
            ksq[f] = act(sqt[i], H8[:, f], ACT.Square, kk_t[f], sq_free[i])
            t = act(VT[:, :, 128 * f:128 * f + 128], ps[:, b].rearrange("p (c n) -> p c n", c=4), ACT.Copy, t, after_r)
            bank_free[b] = [t]
            x_1[f] = t
            b, t2 = kk_norm(f)
            t3 = vts(YT[:, f], ps[:, b], 1e-24, None, MAXO, None, t2, after_r)
            bank_free[b] = [t3]
            ksq[f] = act(YT[:, f], YT[:, f], ACT.Sqrt, t3)
        vt_t = list(x_1)
        for f in range(8):
            i = f % 2
            t2 = vrec(YT[:, f], YT[:, f], ksq[f])
            a_t[f] = gtt(A[:, f], A[:, f], YT[:, f], MUL, t2, a_t[f])
            kk_t[f] = vtt(H8[:, f], H8[:, f], YT[:, f], MUL, t2, a_t[f])
            t1 = vstt(sqt[i], R[:, f], vc("r_k", f), K[:, f], MUL, MUL, r_t[f], kp_t[f], sq_free[i])
            b = bank()
            t2 = mm(ps[:, b], bones[:, :], sqt[i], True, True, t1, bank_free[b], inc=True)
            v_t[f] = vtt(V[:, f], V[:, f], ps[:, b], MUL, t2, v_t[f])
            bank_free[b] = [v_t[f]]
            lc = YT[:, f]
            t3 = vscan(lc, cmask, L[:, f], l_t[f], t_cm, kk_t[f], a_t[f])
            t4 = vcopy(lmid[:, f, :], lc[:, 63:512:128], t3)
            lm = lmid[:, f, :].rearrange("p (c o) -> p c o", o=1).to_broadcast([128, 4, 128])
            x1 = lc.rearrange("p (c t) -> p c t", t=128)
            t5 = vtt(x1, x1, lm, SUB, t4)
            x_1[f] = t5
            lc_t[f] = vcopy(fct[:, f, :], lc[:, 127:512:128], t5)
            t6 = gtt(L[:, f], lc, L[:, f], SUB, t5)
            t7 = act(L[:, f], L[:, f], ACT.Exp, t6)
            l_t[f] = vstt(L[:, f], H8[:, f], -1.0, L[:, f], MUL, MUL, t7, kk_t[f])
            t8 = act(sqt[i], lc, ACT.Exp, t5, t2, scale=-1.0)
            a_t[f] = gtt(A[:, f], A[:, f], sqt[i], MUL, t8)
            k_t[f] = gtt(K[:, f], K[:, f], sqt[i], MUL, t8, t1)
            sq_free[i] = k_t[f]
            t9 = act(lc, lc, ACT.Exp, t6, t8, lc_t[f])
            r_t[f] = vtt(R[:, f], R[:, f], lc, MUL, t9, t1)
        t_f = vtt(fct[:, :, 0:3], fct[:, :, 0:3], lmid[:, :, 1:4], ADD, lc_t)
        t_f = act(fct[:, :, :], fct[:, :, :], ACT.Exp, t_f)

        nb = lambda i, n=512: nb_[:, 512 * i:512 * i + n]
        XTb, TTb, XXb = [[nb(4 * q + i) for i in range(4)] for q in range(3)]
        Pb = [nb_[:, 6144 + 256 * i:6400 + 256 * i] for i in range(4)]
        Makb, Mkrb = [nb(14), nb(15)], [nb(16), nb(17)]
        S = nb(18)
        Wk = sqa[:, 0:2].rearrange("p a t -> p (a t)")
        U = sqa[:, 2:4].rearrange("p a t -> p (a t)")
        Ym = HP[:, 0:2048].rearrange("p (g j t) -> p g j t", g=4, j=4)
        Mbr = HP[:, 2048:4096].rearrange("p (g j t) -> p g j t", g=4, j=4)
        before = [("v", E.count["v"]), ("a", E.count["a"]), ("pe", E.count["pe"]), ("g", E.count["g"])]
        for x in [Mbr] + XXb + Makb + Mkrb:
            t_z = vset(x, 0.0, before)
        t_z = ("v", E.count["v"])
        bc = lambda m, n: m.rearrange("p (o t) -> p o t", o=1).to_broadcast([128, n, m.shape[1]])
        id4 = bc(ident[:, :], 4)
        mX, mR = bc(msk[:, 0:128].bitcast(U32), 2), bc(msk[:, 128:256].bitcast(U32), 2)
        m1 = bc(msk[:, 256:384], 4)
        q4 = lambda x: x.rearrange("p (j t) -> p j t", j=4)
        q2 = lambda x: x.rearrange("p (j t) -> p j t", j=2)

        def four_tr(dst, x, *w):
            b = bank()
            for j in range(4):
                t = tr(ps[:, b, 128 * j:128 * j + 128], x[:, 128 * j:128 * j + 128], w, bank_free[b], inc=j == 3)
            t = act(dst, ps[:, b], ACT.Copy, t)
            bank_free[b] = [t]
            return t

        ready = {}
        gfree = [[], []]

        def group(c, g, state_done):
            Mak, Mkr = Makb[g % 2], Mkrb[g % 2]
            Xm, XT, TT, Pm = XXb[g], XTb[g], TTb[g], Pb[g]
            T = Ym[:, g].rearrange("p j t -> p (j t)")
            td = []
            cs = slice(128 * c, 128 * c + 128)
            for p in range(2):
                pp = slice(64 * p, 64 * p + 64)
                b = bank()
                for fi in range(2):
                    f = 2 * g + fi
                    t = mm(ps[:, b, 256 * fi:256 * fi + 256], A[pp, f, cs], LR[pp, :, f, cs], True, True,
                           a_t[f], l_t[f], r_t[f], bank_free[b], inc=fi == 1)
                bv = ps[:, b].rearrange("p (i r t) -> p i r t", i=2, r=2)
                m2 = slice(256 * p, 256 * p + 256)
                td.append(vpred(q2(Xm[:, m2]), mX, bv[:, :, 0], t, t_z))
                t = vpred(Mbr[:, g, 2 * p:2 * p + 2], mR, bv[:, :, 1], t, t_z, state_done)
                bank_free[b] = [t]
            ready[c, g, "br"] = t
            tk = []
            for p in range(2):
                pp = slice(64 * p, 64 * p + 64)
                b = bank()
                for fi in range(2):
                    f = 2 * g + fi
                    t = mm(ps[:, b, 256 * fi:256 * fi + 256], K[pp, f, cs], LR[pp, :, f, cs], True, True,
                           k_t[f], bank_free[b], inc=fi == 1)
                bv = ps[:, b].rearrange("p (i r t) -> p i r t", i=2, r=2)
                m2 = slice(256 * p, 256 * p + 256)
                vpred(q2(Mak[:, m2]), mX, bv[:, :, 0], t, gfree[g % 2])
                t = vpred(q2(Mkr[:, m2]), mR, bv[:, :, 1], t)
                bank_free[b] = [t]
                tk.append(t)
            t_x = four_tr(XT, Xm, td)
            t = vtt(q4(T), q4(Xm), m1, MUL, td, state_done)
            t_t = vtt(q4(T), q4(T), id4, ADD, t)
            yield
            b = bank()
            for j in range(4):
                p, fi = j // 2, j % 2
                hc = (2 * g + fi) * 128 + 64 * p
                t = mm(ps[:, b, 64 * j:64 * j + 64], Mak[:, 128 * j:128 * j + 128], VT[:, c, hc:hc + 64], True, True,
                       tk, vt_t, bank_free[b], inc=j == 3)
            wd = Wk.rearrange("p (q n) -> p q n", q=2)[:, :, 128 * g:128 * g + 128]
            t = act(wd, q2(ps[:, b, 0:256]), ACT.Copy, t, state_done)
            bank_free[b] = [t]
            ready[c, g, "w"] = t
            b = bank()
            for j in range(4):
                p, fi = j // 2, j % 2
                hc = (2 * g + fi) * 128 + 64 * p
                t = mm(ps[64 * p:64 * p + 64, b, 128 * fi:128 * fi + 128], VT[:, c, hc:hc + 64],
                       Mkr[:, 128 * j:128 * j + 128], True, True, bank_free[b], inc=j == 3)
            gfree[g % 2] = [t]
            t = act(YT[:, 2 * g:2 * g + 2, cs], q2(ps[:, b, 0:256]), ACT.Copy, t, r_t)
            bank_free[b] = [t]
            ready[c, g, "y"] = t
            t_tt = four_tr(TT, T, t_t)
            yield
            n = 2
            for lv in range(6):
                odd = lambda x: x.rearrange("p (n two b) -> p n two b", two=2, b=n)[:, :, 1]
                b = bank()
                for j in range(4):
                    t = mm(ps[:, b, 64 * j:64 * j + 64], XT[:, 128 * j:128 * j + 128], odd(T[:, 128 * j:128 * j + 128]),
                           True, True, t_x, t_t, bank_free[b], inc=j == 3)
                t = vtt(q4(Pm), q4(ps[:, b, 0:256]), bc(msk[:, 384 + 64 * lv:448 + 64 * lv], 4), MUL, t)
                bank_free[b] = [t]
                yield
                b = bank()
                for j in range(4):
                    t = mm(ps[:, b, 64 * j:64 * j + 64], TT[:, 128 * j:128 * j + 128], Pm[:, 64 * j:64 * j + 64],
                           True, True, t_tt, t, bank_free[b], inc=j == 3)
                t_t = vtt(odd(T), odd(T), ps[:, b, 0:256].rearrange("p (n b) -> p n b", b=n), ADD, t)
                bank_free[b] = [t_t]
                yield
                if lv < 5:
                    t_tt = four_tr(TT, T, t_t)
                    yield
                n *= 2
            ready[c, g, "T"] = t_t

        s_t = None
        done = []
        for c in range(4):
            cs = slice(128 * c, 128 * c + 128)
            live = [group(c, g, done) for g in range(2)]
            for _ in range(2):
                for x in live:
                    next(x)
            live += [group(c, g, done) for g in range(2, 4)]
            while live:
                for x in list(live):
                    try:
                        next(x)
                    except StopIteration:
                        live.remove(x)
            tk_t = []
            if c < 3:
                for x, xt in ((A, a_t), (K, k_t)):
                    for hf in range(2):
                        b = bank()
                        for f in range(4 * hf, 4 * hf + 4):
                            t = tr(ps[:, b, 128 * (f % 4):128 * (f % 4) + 128], x[:, f, cs], bank_free[b], inc=f % 4 == 3)
                        t = act(x[:, 4 * hf:4 * hf + 4, cs], q4(ps[:, b]), ACT.Copy, t)
                        bank_free[b] = [t]
                        tk_t.append(t)
            w_t = []
            for p in range(2):
                pp = slice(64 * p, 64 * p + 64)
                wt = [ready[c, g, "w"] for g in range(4)]
                if c:
                    b = bank()
                    for f in range(8):
                        t = mm(ps[:, b, 64 * f:64 * f + 64], L[pp, f, cs], S[pp, 64 * f:64 * f + 64], True, True,
                               s_t, bank_free[b], inc=f == 7)
                    t = vtt(Wk[:, 512 * p:512 * p + 512], Wk[:, 512 * p:512 * p + 512], ps[:, b], ADD, t, wt)
                    bank_free[b] = [t]
                    w_t.append([t])
                else:
                    w_t.append(wt)
            u_t = []
            for p in range(2):
                b = bank()
                for f in range(8):
                    t = mm(ps[:, b, 64 * f:64 * f + 64], Ym[:, f // 2, 2 * p + f % 2],
                           Wk[:, 512 * p + 64 * f:512 * p + 64 * f + 64], True, True,
                           w_t[p], [ready[c, g, "T"] for g in range(4)], bank_free[b], inc=f == 7)
                if p:
                    t = vcopy(U[:, 512:1024], ps[:, b], t, done)
                else:
                    t = act(U[:, 0:512], ps[:, b], ACT.Copy, t, done)
                bank_free[b] = [t]
                u_t.append(t)
            y_t = []
            for hf in range(2):
                b = bank()
                for f in range(4 * hf, 4 * hf + 4):
                    for p in range(2):
                        pp = slice(64 * p, 64 * p + 64)
                        o = ps[pp, b, 128 * (f % 4):128 * (f % 4) + 128]
                        if c:
                            mm(o, S[pp, 64 * f:64 * f + 64], R[pp, f, cs], True, False, bank_free[b], s_t)
                        t = mm(o, U[:, 512 * p + 64 * f:512 * p + 64 * f + 64], Mbr[:, f // 2, 2 * p + f % 2],
                               c == 0, True, u_t, bank_free[b], [ready[c, g, "br"] for g in range(4)],
                               inc=f % 4 == 3 and p == 1)
                yv = YT[:, 4 * hf:4 * hf + 4, cs]
                t = vtt(yv, yv, q4(ps[:, b]), ADD, t, [ready[c, g, "y"] for g in range(4)])
                bank_free[b] = [t]
                y_t.append(t)
            done = y_t
            if c < 3:
                b = bank()
                for f in range(8):
                    for p in range(2):
                        o = ps[64 * p:64 * p + 64, b, 64 * f:64 * f + 64]
                        n = slice(64 * p, 64 * p + 64)
                        mm(o, A[:, f, 128 * c + 64 * p:128 * c + 64 * p + 64], U[:, 512 * p + 64 * f:512 * p + 64 * f + 64],
                           True, False, tk_t, bank_free[b])
                        t = mm(o, K[:, f, 128 * c + 64 * p:128 * c + 64 * p + 64],
                               VT[:, c, 128 * f + 64 * p:128 * f + 64 * p + 64], False, True, inc=f == 7 and p == 1)
                fb = fct[:, :, c:c + 1].to_broadcast([128, 8, 64])
                s3 = S.rearrange("p (f v) -> p f v", v=64)
                p3 = ps[:, b].rearrange("p (f v) -> p f v", v=64)
                if c:
                    t2 = vtt(S, S, ps[:, b], ADD, t)
                    s_t = vtt(s3, s3, fb, MUL, t2, t_f)
                else:
                    s_t = vtt(s3, p3, fb, MUL, t, t_f)
                bank_free[b] = [s_t]
                done = y_t + [s_t]
        after = [("v", E.count["v"]), ("a", E.count["a"]), ("pe", E.count["pe"])]
        for s in range(NRAW):
            raw_free[s] = list(after)
        for s in range(NSPLIT):
            spl_free[s] = list(after)
        nx["stop"] = len(want)
        ahead()
        sq_free[:] = [after, after]
        sq_n["acc"] = after
        rstd_read["t"] = after

        ghs = [split(GHs[:, 0, j], GHs[:, 1, j], GH[:, j], gk, after) for j in range(2)]
        o_t = [None] * 8
        for f in range(8):
            i = f % 2
            b = bank()
            t = mm(ps[:, b], bones[:, :], YT[:, f], True, True, y_t, bank_free[b], inc=True)
            t = vstt(YT[:, f], ps[:, b], -1.0 / 64, YT[:, f], MUL, ADD, t)
            bank_free[b] = [t]
            o_t[f] = [act(sqt[i], YT[:, f], ACT.Square, t, sq_free[i])]
            b = bank()
            t2 = mm(ps[:, b], bones[:, :], sqt[i], True, True, o_t[f], bank_free[b], inc=True)
            sq_free[i] = t2
            t3 = act(A[:, f], ps[:, b], ACT.Sqrt, t2, after, t_e1, scale=1.0 / 64, bias=eps6[:, 1:2])
            bank_free[b] = [t3]
            t4 = vrec(A[:, f], A[:, f], t3)
            t5 = vstt(YT[:, f], YT[:, f], vc("ln_w", f), A[:, f], MUL, MUL, t4, o_t[f])
            o_t[f] = vstt(YT[:, f], YT[:, f], vc("ln_b", f), V[:, f], ADD, ADD, t5)

        def gate_evac(nb, p, t):
            t1 = vtt(YT[:, nb], YT[:, nb], p, MUL, t, o_t[nb])
            o_t[nb] = split(MX[0][0][:, nb], MX[0][1][:, nb], YT[:, nb], t1, after)
            return [t1]
        proj("gw2", lambda k: (GHs[:, 0, k], GHs[:, 1, k]), ghs, gate_evac)
        proj("w_o", xm(0), o_t, residual(lambda m: md(1, 2, m), mod_t[8]))
        h_free = [x_t[7]]
        tmf = [[after] for _ in range(4)]
        t_prev = mlp(1)

        tr_ = finish_norm(ones[:, :], 1024.0, eps6[:, 0:1], rstd)
        for f in range(8):
            x_t[f] = vstt(X[:, f], X[:, f], vc("final_g", f), rstd, MUL, MUL, tr_, x_t[f], t_cst)
            sumsq(X[:, f], f == 0, x_t[f])
        rstd_read["t"] = x_t[7]

        def ffn(n, gname):
            nonlocal h_free, t_prev
            warm(ACT.Sqrt)
            hs = plain_norm(gname, w=h_free)
            warm(ACT.Sigmoid)
            sg = [tmp_[:, i] for i in range(4)]
            sgf = [[t_prev] for _ in range(4)]
            hid_t = [None] * 22
            keep = {"base": 0}

            def evac(nb, p, t):
                j, i = keep["base"] + nb // 2, (nb // 2) % 4
                if nb % 2 == 0:
                    t1 = act(sg[i], p, ACT.Sigmoid, t, sgf[i])
                    keep[j] = vtt(sg[i], sg[i], p, MUL, t1)
                    return [keep[j]]
                t1 = vtt(sg[i], sg[i], p, MUL, t, keep[j])
                hid_t[j] = split(HID[:, 0, j], HID[:, 1, j], sg[i], t1, t_prev)
                sgf[i] = hid_t[j]
                return [t1]

            proj("f%dgu" % n, h, hs, evac)
            keep["base"] = 20
            h_free = [proj("f%dgux" % n, h, hs, evac)]
            t_prev = proj("f%dd" % n, hid, hid_t, residual(lambda m: 0.5, None))

        ffn(1, "ffn1_norm")

        warm(ACT.Sqrt)
        hs = plain_norm("mix_norm", w=h_free)
        P = lambda k: Pq[:, k]
        p_t = [None] * 24
        dec = att[:, 0:2048].rearrange("p (h t) -> p h t", h=4)
        rot = att[:, 2048:3072].rearrange("p (h t) -> p h t", h=2)
        perm = att[:, 3072:3200]
        lq = att[:, 3200:3456]
        t_at = dma("sp", att[:, 0:3200], D["att"], "cd", t_prev, h_free)
        t_at = dma("sp", lq, D["lq"], "cd", t_prev)

        def p_evac(nb, p, t):
            if nb % 2:
                p_t[nb] = act(P(nb), p, ACT.Copy, t, t_prev)
            else:
                p_t[nb] = vcopy(P(nb), p, t, t_prev)
            return [p_t[nb]]
        h_free = [proj("w_in", h, hs, p_evac)]
        lqj = att[:, 3456:3584]
        ta = vdot(lqj[:, 0:64], lq[:, 0:64], lq[:, 64:128], st[:, 0:1], t_at)
        tb = vdot(lqj[:, 64:128], lq[:, 128:192], lq[:, 192:256], st[:, 1:2], t_at)
        ta = act(st[:, 2:4], st[:, 0:2], ACT.Exp, ta, tb)
        ta = vtt(st[:, 4:5], st[:, 3:4], st[:, 2:3], SUB, ta)
        t_lam = vts(st[:, 4:5], st[:, 4:5], -(0.8 - 0.6 * math.exp(-0.3 * 0)), None, ADD, None, ta)
        for k in range(4):
            b = bank()
            t = mm(ps[:, b], perm, P(k), True, True, p_t[k], t_at, bank_free[b], inc=True)
            t1 = vtt(sqt[k % 2], ps[:, b], rot[:, 1], MUL, t, sq_free[k % 2])
            bank_free[b] = [t1]
            t2 = vtt(P(k), P(k), rot[:, 0], MUL, t)
            p_t[k] = vtt(P(k), P(k), sqt[k % 2], ADD, t1, t2)
            sq_free[k % 2] = p_t[k]
        rvT, dvT = rdT[:, 0], rdT[:, 1]
        vv = []
        for dst, k0 in ((rvT, 4), (dvT, 20)):
            for k in range(4):
                b = bank()
                for c in range(4):
                    t = tr(ps[:, b, 128 * c:128 * c + 128], P(k0 + k)[:, 128 * c:128 * c + 128], p_t[k0 + k], bank_free[b],
                           inc=c == 3)
                t = act(dst[:, :, 128 * k:128 * k + 128], q4(ps[:, b]), ACT.Copy, t, t_prev)
                bank_free[b] = [t]
                vv.append(t)
        O = lambda k: (HH[:, k], HL[:, k])
        o_t = [None] * 8
        pb_ = [P(20), P(21), P(22), P(23)]
        pf = [[vv] for _ in range(4)]
        late = []

        def then():
            while late:
                late.pop(0)()

        def head_norm(o_bank, t, fin):
            i = sq_n["n"] % 2
            sq_n["n"] += 1
            t1 = act(sqt[i], ps[:, o_bank], ACT.Square, t, sq_free[i])
            sq_free[i] = t1

            def rest():
                b = free_bank(obs.values())
                t2 = mm(ps[:, b], ones[:, :], sqt[i], True, True, t1, bank_free[b], inc=True)
                t3 = act(sqt[i], ps[:, b], ACT.Sqrt, t2, scale=1.0 / 128, bias=eps6[:, 0:1])
                bank_free[b] = [t3]
                sq_free[i] = fin(sqt[i], vrec(sqt[i], sqt[i], t3))
            late.append(rest)

        for hh in range(4):
            i = hh
            t = act(tmp2[:, i], P(8 + hh), ACT.Sigmoid, p_t[8 + hh], t_prev)
            p_t[8 + hh] = gtt(P(8 + hh), tmp2[:, i], P(8 + hh), MUL, t)
        warm(ACT.Sqrt)
        items = [(hh, q) for hh in range(4) for q in range(4)]
        sc_t, obs = {}, {}

        def ret_scores(n):
            hh, q = items[n]
            pp = slice(64 * (hh % 2), 64 * (hh % 2) + 64)
            w = 512 - 128 * q
            b = free_bank(obs.values())
            t = mm(ps[:, b, 0:w], P(2 + hh // 2)[pp, 128 * q:128 * q + 128], P(hh // 2)[pp, 128 * q:512], True, True,
                   p_t[hh // 2], p_t[2 + hh // 2], bank_free[b], inc=True)
            i = n % 4
            t = vtt(pb_[i][:, 0:w], ps[:, b, 0:w], dec[:, hh, 0:w], MUL, t, pf[i], t_at)
            bank_free[b] = [t]
            sc_t[n] = t

        def free_bank(busy):
            b = bank()
            while b in busy:
                b = bank()
            return b

        ret_scores(0)
        ret_scores(1)
        for n, (hh, q) in enumerate(items):
            if n + 2 < 16:
                ret_scores(n + 2)
            if q == 0:
                obs[hh] = free_bank(obs.values())
            w = 512 - 128 * q
            i = n % 4
            t = mm(ps[:, obs[hh], 128 * q:512], rvT[:, q, 128 * hh:128 * hh + 128], pb_[i][:, 0:w], q == 0, q == 3,
                   sc_t[n], vv, bank_free[obs[hh]] if q == 0 else None, inc=True)
            pf[i] = [t]
            if q == 1:
                then()
            if q == 3:
                def fin(r, t4, hh=hh, ob=obs[hh]):
                    t5 = vstt(r, ps[:, ob], vc("ret_norm", hh), r, MUL, MUL, t4)
                    bank_free[ob] = [t5]
                    t6 = vtt(r, r, P(8 + hh), MUL, t5, p_t[8 + hh])
                    o_t[hh] = split(HH[:, hh], HL[:, hh], r, t6, h_free)
                    del obs[hh]
                    return o_t[hh]
                head_norm(obs[hh], t, fin)

        EB = [P(4 + i) for i in range(4)] + [P(20 + i) for i in range(4)]
        ebf = [[vv] for _ in range(4)] + [[pf[i]] for i in range(4)]
        atf = [[t_prev, h_free, p_t[8:12]], [t_prev, h_free]]
        es_of, evs = {}, {}
        n_s = [0]

        def diff_scores(n):
            hh, i = items[n]
            w = 128 * (i + 1)
            es = []
            for cc in range(2):
                pp = slice(64 * cc, 64 * cc + 64)
                b = free_bank(obs.values())
                mm(ps[:, b, 0:w], P(12 + hh)[pp, 128 * i:128 * i + 128], P(16 + hh)[pp, 0:w], True, False,
                   p_t[12 + hh], p_t[16 + hh], bank_free[b])
                t = mm(ps[:, b, w - 128:w], ident[:, :], negm[:, :], False, True, inc=True)
                x = n_s[0] % 8
                n_s[0] += 1
                sc = stat[:, 4 * x:4 * x + 4]
                t1 = vmax(sc[:, 0:1], ps[:, b, 0:w], t, ebf[x])
                t2 = vts(sc[:, 1:2], sc[:, 0:1], -0.125, None, MUL, None, t1)
                t3 = act(EB[x][:, 0:w], ps[:, b, 0:w], ACT.Exp, t2, ebf[x], scale=0.125, bias=sc[:, 1:2], accum=sc[:, 2:3])
                bank_free[b] = [t3]
                es.append((x, sc, vrec(sc[:, 3:4], sc[:, 2:3], t3)))
            (x0, s0_, ta), (x1, s1_, tb) = es
            t5 = vts(EB[x0][:, 0:w], EB[x0][:, 0:w], s0_[:, 3:4], None, MUL, None, ta)
            t6 = vtt(s1_[:, 3:4], s1_[:, 3:4], st[:, 4:5], MUL, tb, t_lam)
            t7 = vstt(EB[x0][:, 0:w], EB[x1][:, 0:w], s1_[:, 3:4], EB[x0][:, 0:w], MUL, ADD, t5, t6)
            es_of[n] = (x0, x1, t7)

        diff_scores(0)
        diff_scores(1)
        diff_scores(2)
        then()
        warm(ACT.Exp)
        for n, (hh, i) in enumerate(items):
            w = 128 * (i + 1)
            x0, x1, t7 = es_of[n]
            b = free_bank(obs.values())
            for j in range(i + 1):
                t = tr(ps[:, b, 128 * j:128 * j + 128], EB[x0][:, 128 * j:128 * j + 128], t7, bank_free[b], inc=j == i)
            ebf[x0], ebf[x1] = [t], [t7]
            t = act(atb[:, hh % 2, 0:i + 1, 128 * i:128 * i + 128], ps[:, b, 0:w].rearrange("p (j q) -> p j q", q=128),
                    ACT.Copy, t, atf[hh % 2])
            bank_free[b] = [t]
            evs.setdefault(hh, []).append(t)
            if n + 3 < 16:
                diff_scores(n + 3)
            if i == 1:
                then()
            if i == 3:
                ob = free_bank(obs.values())
                obs[hh] = ob
                for j in range(4):
                    t = mm(ps[:, ob, 128 * j:512], dvT[:, j, 128 * hh:128 * hh + 128], atb[:, hh % 2, j, 128 * j:512],
                           j == 0, j == 3, evs[hh], vv, bank_free[ob], inc=j == 3)
                atf[hh % 2] = [t]

                def fin(r, t4, hh=hh, ob=ob):
                    t5 = vstt(r, ps[:, ob], vc("diff_norm", hh), r, MUL, MUL, t4)
                    bank_free[ob] = [t5]
                    t6 = vts(r, r, 1.0 - (0.8 - 0.6 * math.exp(-0.3 * 0)), None, MUL, None, t5)
                    o_t[4 + hh] = split(HH[:, 4 + hh], HL[:, 4 + hh], r, t6, h_free)
                    del obs[hh]
                    return o_t[4 + hh]
                head_norm(ob, t, fin)
        then()
        t = proj("w_out", O, o_t, residual(lambda m: 1.0, None))
        h_free = [t]
        t_prev = [t, atf, ("g", E.count["g"]), ("v", E.count["v"]), ("a", E.count["a"])]

        t_m = dma("sp", MEM[:, :, :], D["memT"], "cx", t_prev)
        hs = plain_norm("xattn_norm", w=h_free)
        q_t = [None] * 8
        kv_t = [None] * 16
        h_free = [proj("wq", h, hs, copy_evac(Qx, q_t, t_prev))]
        for f in range(8):
            sumsq(MEM[:, f], f == 0, t_m, n=256)
        ms = plain_norm("mem_norm", 256, MEM, MNs[:, 0], MNs[:, 1], w=t_prev)

        def kv_evac(nb, p, t):
            o = KTm[:, nb] if nb < 8 else VFm[:, nb - 8]
            kv_t[nb] = act(o, p, ACT.Copy, t, t_prev) if nb % 2 else vcopy(o, p, t, t_prev)
            return [kv_t[nb]]
        proj("wkv", lambda k: (MNs[:, 0, k], MNs[:, 1, k]), ms, kv_evac, n=256)
        mv_t = []
        for k in range(8):
            b = bank()
            for c in range(2):
                t = tr(ps[:, b, 128 * c:128 * c + 128], VFm[:, k, 128 * c:128 * c + 128], kv_t[8 + k], bank_free[b], inc=c == 1)
            t = act(MV[:, :, 128 * k:128 * k + 128], q2(ps[:, b, 0:256]), ACT.Copy, t, t_prev)
            bank_free[b] = [t]
            mv_t.append(t)
        ptf = [[t_prev], [t_prev]]
        ebf = [[t_prev] for _ in range(4)]
        es_of, evs = {}, {}

        def x_scores(n):
            hh, i = items[n]
            b = bank()
            for e in range(2):
                t = mm(ps[:, b, 0:256], Qx[:, 2 * hh + e, 128 * i:128 * i + 128], KTm[:, 2 * hh + e], e == 0, e == 1,
                       q_t[2 * hh + e], kv_t[2 * hh + e], bank_free[b], inc=e == 1)
            x = n % 4
            sc = stat[:, 4 * x:4 * x + 4]
            t1 = vmax(sc[:, 0:1], ps[:, b, 0:256], t, ebf[x])
            t2 = vts(sc[:, 1:2], sc[:, 0:1], -0.0625, None, MUL, None, t1)
            t3 = act(EBx[:, x], ps[:, b, 0:256], ACT.Exp, t2, ebf[x], scale=0.0625, bias=sc[:, 1:2], accum=sc[:, 2:3])
            bank_free[b] = [t3]
            t4 = vrec(sc[:, 3:4], sc[:, 2:3], t3)
            es_of[n] = vts(EBx[:, x], EBx[:, x], sc[:, 3:4], None, MUL, None, t4)

        for n in range(3):
            x_scores(n)
        for n, (hh, i) in enumerate(items):
            x = n % 4
            b = bank()
            for j in range(2):
                t = tr(ps[:, b, 128 * j:128 * j + 128], EBx[:, x, 128 * j:128 * j + 128], es_of[n], bank_free[b], inc=j == 1)
            ebf[x] = [t]
            t = act(PTx[:, hh % 2, :, 128 * i:128 * i + 128], q2(ps[:, b, 0:256]), ACT.Copy, t, ptf[hh % 2])
            bank_free[b] = [t]
            evs.setdefault(hh, []).append(t)
            if n + 3 < 16:
                x_scores(n + 3)
            if i == 3:
                for e in range(2):
                    b = bank()
                    for j in range(2):
                        t = mm(ps[:, b], MV[:, j, 256 * hh + 128 * e:256 * hh + 128 * e + 128], PTx[:, hh % 2, j], j == 0, j == 1,
                               evs[hh], mv_t, bank_free[b], inc=j == 1)
                    k = 2 * hh + e
                    th = act(HH[:, k], ps[:, b], ACT.Copy, t, h_free)
                    o_t[k] = [th, vtt(HL[:, k], ps[:, b], HH[:, k].bitcast(F32), SUB, th)]
                    bank_free[b] = [o_t[k][1]]
                ptf[hh % 2] = [t]
        t = proj("wo", O, o_t, residual(lambda m: 1.0, None))
        h_free = [t]
        t_prev = [t, ("g", E.count["g"]), ("v", E.count["v"]), ("a", E.count["a"])]

        ffn(2, "ffn2_norm")
        tr_ = finish_norm(ones[:, :], 1024.0, eps6[:, 0:1], rstd)
        for f in range(8):
            t = vstt(OUT[:, f], X[:, f], vc("final_norm", f), rstd, MUL, MUL, tr_, x_t[f], t_prev)
            t_out = dma("sp", out[:, f, :], OUT[:, f], "out", t)
        E.emit("sp", lambda e: e.nop(), [t_out])

        block = ctx.enter_context(nc.Block())

        @block.sync
        def _(eng):
            E.play("sp", eng)

        @block.gpsimd
        def _(eng):
            E.play("g", eng)

        @block.scalar
        def _(eng):
            E.play("a", eng)

        @block.vector
        def _(eng):
            E.play("v", eng)

        @block.tensor
        def _(eng):
            E.play("pe", eng)


def kernel(**inp):
    import numpy as np
    import concourse.bacc as bacc
    from concourse import mybir as mb
    from concourse.bass_utils import run_bass_kernel_spmd as run

    a = {k: np.asarray(v) for k, v in inp.items()}

    def blocks(w, m=128):
        K, N = w.shape
        return w.reshape(K // 128, 128, N // m, m).transpose(2, 1, 0, 3).reshape(N // m, 128, K // 128 * m)

    def feat(v):
        return v.reshape(-1, 128).T

    d = {}
    d["xT"] = a["x"][0].T.reshape(8, 128, 512).transpose(1, 0, 2)
    d["memT"] = a["mem_2"][0].T.reshape(8, 128, 256).transpose(1, 0, 2)
    d["cb"] = np.broadcast_to(a["c"], (128, 1024))
    d["adab"] = feat(a["ada_b"].reshape(-1))
    d["adaw"] = a["ada_w"].transpose(0, 2, 1).reshape(96, 128, 1024)
    pad = np.zeros((128, 4), np.float32)
    cols = {"g00": a["norm_g"][0, 0], "g01": a["norm_g"][0, 1], "g10": a["norm_g"][1, 0], "g11": a["norm_g"][1, 1],
            "final_g": a["final_g"], "cw0": a["conv_w"][0, 0], "cw1": a["conv_w"][0, 1], "cw2": a["conv_w"][0, 2],
            "w0": a["rw_w0"], "a0": a["rw_a0"], "k_k": a["rw_k_k"], "k_a": a["rw_k_a"], "r_k": a["rw_r_k"],
            "ln_w": a["rw_ln_w"], "ln_b": a["rw_ln_b"], "ffn1_norm": a["ffn1_norm_2"], "mix_norm": a["mix_norm_2"],
            "xattn_norm": a["xattn_norm_2"], "mem_norm": a["mem_norm_2"], "ffn2_norm": a["ffn2_norm_2"],
            "final_norm": a["final_norm_2"], "ret_norm": a["ret_out_norm_2"], "diff_norm": a["diff_out_norm_2"]}
    for i in range(6):
        cols["mu%d" % i] = a["rw_mu"][0, i]
    d["vec"] = np.concatenate([x for n in VECS for x in ([feat(cols[n].reshape(-1))] +
                                                         ([pad] if cols[n].size == 512 else []))], axis=1)
    def kpieces(w, per=8):
        K, N = w.shape
        return w.reshape(K // 128, 128, N // (128 * per), 128 * per).transpose(2, 0, 1, 3)

    def woven(*ws):
        K = ws[0].shape[0]
        return np.stack([w.reshape(K, -1, 128) for w in ws], axis=2).reshape(K, -1)

    def padded(w, K, N):
        out = np.zeros((K, N), w.dtype)
        out[0:w.shape[0], 0:w.shape[1]] = w
        return out

    wb, wc, wh = np.split(a["conv_w_in"][0], 3, axis=1)
    d["cw_in"] = kpieces(woven(wc, wh, wb))
    d["cw_out"] = blocks(a["conv_w_out"][0])
    for i in range(2):
        for j in range(2):
            x = "%d%s" % (i, "ab"[j])
            d["mw1_" + x] = kpieces(a["mlp_w1"][i][:, 2048 * j:2048 * j + 2048])
            d["mw2_" + x] = blocks(a["mlp_w2"][i][2048 * j:2048 * j + 2048])
    d["wr"], d["wk"], d["wv"] = [kpieces(a["rw_w_rkv"][0, i]) for i in range(3)]
    d["w_o"] = blocks(a["rw_w_o"][0])
    d["dw1"] = blocks(padded(a["rw_w1"][0], 1024, 128))
    d["aw1"] = blocks(padded(a["rw_a1"][0], 1024, 128))
    d["gw1"] = blocks(padded(a["rw_g1"][0], 1024, 256))
    d["dw2"] = kpieces(padded(a["rw_w2"][0], 128, 1024))
    d["aw2"] = kpieces(padded(a["rw_a2"][0], 128, 1024))
    d["gw2"] = kpieces(padded(a["rw_g2"][0], 256, 1024))
    for i in (1, 2):
        w = woven(a["ffn%d_w_gate_2" % i][0], a["ffn%d_w_up_2" % i][0])
        d["f%dgu" % i] = kpieces(w[:, 0:5120])
        d["f%dgux" % i] = kpieces(w[:, 5120:], 4)
        d["f%dd" % i] = blocks(a["ffn%d_w_down_2" % i][0])
    d["w_in"] = kpieces(a["w_in_2"][0])
    d["w_out"] = blocks(a["w_out_2"][0])
    d["wq"] = kpieces(a["xattn_wq_2"][0])
    d["wkv"] = kpieces(a["xattn_wkv_2"][0])
    d["wo"] = blocks(a["xattn_wo_2"][0])
    d["lq"] = np.broadcast_to(np.concatenate([a["diff_lq1_2"], a["diff_lk1_2"], a["diff_lq2_2"], a["diff_lk2_2"]], 1), (128, 256))

    i = np.arange(128)
    d["ident"] = np.eye(128, dtype=np.float32)
    d["bones"] = (i[:, None] // 64 == i[None, :] // 64).astype(np.float32)
    d["negm"] = np.where(i[None, :] > i[:, None], np.float32(-1e30), np.float32(0))
    m = [i[:, None] < i[None, :], i[:, None] <= i[None, :], (i[:, None] // 2 == i[None, :] // 2) & (i[:, None] < i[None, :])]
    b = 2
    while b < 128:
        t = i[(i // b) % 2 == 1]
        m.append((i[:, None] // (2 * b) == t[None, :] // (2 * b)) & ((i[:, None] // b) % 2 == 0))
        b *= 2
    d["msk"] = np.concatenate(m, axis=1).astype(np.float32)
    rel = np.arange(512)[None, :] - i[:, None]
    dec = []
    for hh in range(4):
        lg = np.log(1.0 - 2.0 ** (-5.0 - hh))
        dec.append(np.where(rel >= 0, np.exp(np.maximum(rel, 0) * lg), 0.0) * 64.0 ** -0.5)
    inv = (1.0 / (np.float32(10000.0) ** (np.arange(0, 64, 2, dtype=np.float32) / np.float32(64)))).astype(np.float32)
    ang = (np.arange(512, dtype=np.float32)[None, :] * inv[i % 32][:, None]).astype(np.float32).astype(np.float64)
    perm = np.zeros((128, 128))
    for m in range(128):
        if m % 64 < 32:
            perm[m + 32, m] = -1.0
        else:
            perm[m - 32, m] = 1.0
    d["att"] = np.concatenate(dec + [np.cos(ang), np.sin(ang), perm], axis=1).astype(np.float32)

    nc = bacc.Bacc("TRN2", target_bir_lowering=False, num_devices=1)
    arrays, D = {}, {}
    for n, v in d.items():
        v = np.ascontiguousarray(v)
        arrays["in_" + n] = v
        D[n] = nc.dram_tensor("in_" + n, v.shape, mb.dt.from_np(v.dtype), kind="ExternalInput").ap()
    o = nc.dram_tensor("out_dram", (128, 8, 512), mb.dt.float32, kind="ExternalOutput").ap()
    build(nc, D, o)
    r = run(nc, [arrays], core_ids=[0])
    got = r.results[0]["out_dram"]
    return np.ascontiguousarray(got.transpose(2, 1, 0).reshape(1, 512, 1024))
```

```python
from contextlib import ExitStack
import math

from concourse import mybir

F32 = mybir.dt.float32
F32R = mybir.dt.float32r
U32 = mybir.dt.uint32
ALU = mybir.AluOpType
ACT = mybir.ActivationFunctionType
AX = mybir.AxisListType.X

MUL, ADD, SUB, MAXO = ALU.mult, ALU.add, ALU.subtract, ALU.max

VECS = ["g00", "g01", "g10", "g11", "final_g", "cw0", "cw1", "cw2",
        "mu0", "mu1", "mu2", "mu3", "mu4", "mu5", "w0", "a0", "k_k", "k_a", "r_k", "ln_w", "ln_b",
        "ffn1_norm", "mix_norm", "xattn_norm", "mem_norm", "ffn2_norm", "final_norm",
        "ret_norm", "diff_norm"]
VOFF = {n: 8 * i for i, n in enumerate(VECS)}

NRAW = 4
NSPLIT = 3
NADA = 6
AHEAD = 2

PROJ = [("cw_in", "k", 24, 8), ("cw_out", "m", 8, 8),
        ("mw1_0a", "k", 16, 8), ("mw2_0a", "m", 8, 16), ("mw1_0b", "k", 16, 8), ("mw2_0b", "m", 8, 16),
        ("wv", "k", 8, 8), ("dw1", "m", 1, 8), ("aw1", "m", 1, 8), ("gw1", "m", 2, 8),
        ("aw2", "k", 8, 1), ("wk", "k", 8, 8), ("dw2", "k", 8, 1), ("wr", "h", 8, 8),
        ("gw2", "k", 8, 2), ("w_o", "m", 8, 8),
        ("mw1_1a", "k", 16, 8), ("mw2_1a", "m", 8, 16), ("mw1_1b", "k", 16, 8), ("mw2_1b", "m", 8, 16),
        ("f1gu", "k", 40, 8), ("f1gux", "k", 4, 8), ("f1d", "m", 8, 22),
        ("w_in", "k", 24, 8), ("w_out", "m", 8, 8), ("wq", "h", 8, 8), ("wkv", "k", 16, 8), ("wo", "m", 8, 8),
        ("f2gu", "k", 40, 8), ("f2gux", "k", 4, 8), ("f2d", "m", 8, 22)]


WIDE = {"k": 8, "h": 4}


def pieces():
    out = []
    for name, kind, nb, kc in PROJ:
        if kind != "m":
            w = min(WIDE[kind], nb)
            out += [(name, g, k, w) for g in range(nb // w) for k in range(kc)]
        else:
            out += [(name, b, k, min(8, kc - k)) for b in range(nb) for k in range(0, kc, 8)]
    return out


class Engines:

    def __init__(self, sems):
        self.sems = sems
        self.q = {n: [] for n in ("pe", "v", "a", "g", "sp")}
        self.count = {n: 0 for n in sems}
        self.seen = {n: {} for n in self.q}

    def emit(self, eng, fn, waits, sem=None, by=1):
        for s, v in flat(waits):
            if self.seen[eng].get(s, 0) < v:
                self.seen[eng][s] = v
                self.q[eng].append((None, self.sems[s], v))
        if sem is None:
            self.q[eng].append((fn, None, 0))
            return None
        self.count[sem] += by
        self.q[eng].append((fn, self.sems[sem], by))
        return (sem, self.count[sem])

    def play(self, name, eng):
        for fn, sem, v in self.q[name]:
            if fn is None:
                eng.wait_ge(sem, v)
            elif sem is None:
                fn(eng)
            else:
                fn(eng).then_inc(sem, v)


def flat(ts):
    out = []
    for t in ts:
        if t is None:
            continue
        if isinstance(t, tuple) and len(t) == 2 and isinstance(t[0], str):
            out.append(t)
        else:
            out += flat(t)
    return out


def build(nc, D, out):
    ctx = ExitStack()
    with ctx:
        def sb(name, shape, dt=F32):
            return ctx.enter_context(nc.sbuf_tensor(name, shape, dt))

        names = ["pe", "v", "a", "g", "out", "cst", "cx", "cb", "cd", "ck"] + [f"r{i}" for i in range(NRAW)] + \
                [f"d{i}" for i in range(NADA)] + [f"e{i}" for i in range(16)]
        sems = {n: ctx.enter_context(nc.semaphore("s_" + n)) for n in names}
        E = Engines(sems)

        ps = ctx.enter_context(nc.psum_tensor("ps", [128, 8, 512], F32))
        X = sb("X", [128, 8, 512])
        GH = sb("GH", [128, 2, 512])
        vec = sb("vec", [128, 8 * len(VECS)])
        ident = sb("ident", [128, 128])
        bones = sb("bones", [128, 128])
        ones = sb("ones", [128, 128])
        negm = sb("negm", [128, 128])
        msk = sb("msk", [128, 768])
        mod = sb("mod", [128, 96])
        adab = sb("adab", [128, 96])
        coef = sb("coef", [128, 8])
        omu = sb("omu", [128, 48])
        lmid = sb("lmid", [128, 8, 4])
        fct = sb("fct", [128, 8, 4])
        st = sb("st", [128, 8])
        stat = sb("stat", [128, 32])
        eps6 = sb("eps6", [128, 2])

        SQ = (nc.sbuf_base + 31) // 32 * 32
        RG = SQ + 8192
        WK = RG + 40960

        def at_(name, off, shape, dt=F32):
            return nc.alloc_sbuf_tensor_at(name, shape, dt, offset=off)

        sqa = at_("sqa", SQ, [128, 4, 512])
        sqt = [sqa[:, 0], sqa[:, 1]]
        acc, rstd = sqa[:, 2], sqa[:, 3]
        raw_ = at_("raw", RG, [128, NRAW, 1024])
        WHs = at_("WHs", RG + 16384, [128, NSPLIT, 1024], F32R)
        WLs = at_("WLs", RG + 16384 + 4096 * NSPLIT, [128, NSPLIT, 1024], F32R)
        HH = at_("HH", WK, [128, 8, 512], F32R)
        HL = at_("HL", WK + 16384, [128, 8, 512], F32R)
        HID = at_("HID", WK + 32768, [128, 2, 22, 512], F32R)
        tmp_ = at_("tmp", WK + 122880, [128, 4, 512])
        cbc = at_("cbc", WK + 131072, [128, 1024])[:, :]
        ada = at_("ada", WK + 98304, [128, NADA, 1024])
        ada1 = at_("ada1", WK + 32768, [128, 16, 1024])
        HM = at_("HM", WK + 32768, [128, 2, 16, 512], F32R)
        cvt = at_("cvt", WK + 49152, [128, 2 * 528 + 2 * 512])
        HP = at_("HP", WK, [128, 8 * 513])
        MX = [[at_("M%d%s" % (i, n), WK + 16416 + 32768 * i + 16384 * j, [128, 8, 512], F32R) for j, n in enumerate("HL")]
              for i in range(2)]
        LR = at_("LR", WK + 16416, [128, 2, 8, 512])
        VY = at_("VY", WK + 49184, [128, 2, 8, 512])
        KVA = at_("KVA", WK + 81952, [128, 3, 8, 512])
        T64w = at_("T64w", WK + 131104, [128, 2, 512], F32R)
        T2 = at_("T2", WK + 131104, [128, 2, 512])
        T64a = at_("T64a", WK + 81952, [128, 2, 512], F32R)
        GHs = at_("GHs", WK + 49184, [128, 2, 2, 512], F32R)
        nb_ = at_("nb", RG, [128, 9728])
        Pq = at_("Pq", WK + 32768, [128, 24, 512])
        rdT = at_("rdT", WK + 81920, [128, 2, 4, 512])
        att = at_("att", WK + 98304, [128, 3584])
        atb = at_("atb", WK + 112640, [128, 2, 4, 512])
        Qx = at_("Qx", WK + 32768, [128, 8, 512])
        MEM = at_("MEM", WK + 49152, [128, 8, 256])
        MNs = at_("MNs", WK + 57344, [128, 2, 8, 256], F32R)
        KTm = at_("KTm", WK + 73728, [128, 8, 256])
        VFm = at_("VFm", WK + 81920, [128, 8, 256])
        MV = at_("MV", WK + 90112, [128, 2, 1024])
        PTx = at_("PTx", WK + 98304, [128, 2, 2, 512])
        EBx = at_("EBx", WK + 106496, [128, 4, 256])
        tmp2 = at_("tmp2", WK + 112640, [128, 4, 512])
        OX = [at_("OXH", WK + 49152, [128, 8, 512], F32R), at_("OXL", WK + 114688, [128, 8, 512], F32R)]
        OUT = at_("OUT", WK + 32768, [128, 8, 512])

        H = HP[:, :].rearrange("p (f t) -> p f t", t=513)
        H8 = HP[:, 0:4096].rearrange("p (f t) -> p f t", t=512)
        L, R = LR[:, 0], LR[:, 1]
        K, V, A = KVA[:, 0], KVA[:, 1], KVA[:, 2]

        def act(o, i, func, *w, scale=1.0, bias=0.0, accum=None):
            if accum is not None:
                return E.emit("a", lambda e: e.activation(o, i, func, bias=bias, scale=scale, accum_out=accum), w, "a")
            return E.emit("a", lambda e: e.activation(o, i, func, bias=bias, scale=scale), w, "a")

        def gtt(o, a, b, op, *w):
            return E.emit("g", lambda e: e.tensor_tensor(o, a, b, op), w, "g")

        def warm(func):
            return act(st[:, 7:8], eps6[:, 0:1], func, t_e0, ("a", E.count["a"]))

        def vcopy(o, i, *w):
            return E.emit("v", lambda e: e.tensor_copy(o, i), w, "v")

        def vtt(o, a, b, op, *w):
            return E.emit("v", lambda e: e.tensor_tensor(o, a, b, op), w, "v")

        def vts(o, a, s1, s2, op0, op1, *w):
            if op1 is None:
                return E.emit("v", lambda e: e.tensor_scalar(o, a, s1, None, op0), w, "v")
            return E.emit("v", lambda e: e.tensor_scalar(o, a, s1, s2, op0, op1), w, "v")

        def vstt(o, a, s, b, op0, op1, *w):
            return E.emit("v", lambda e: e.scalar_tensor_tensor(out=o, in0=a, scalar=s, in1=b, op0=op0, op1=op1), w, "v")

        def vrec(o, i, *w):
            return E.emit("v", lambda e: e.reciprocal(o, i), w, "v")

        def vset(o, val, *w):
            return E.emit("v", lambda e: e.memset(o, val), w, "v")

        def vpred(o, m, d, *w):
            return E.emit("v", lambda e: e.copy_predicated(o, m, d), w, "v")

        def vdot(junk, a, b, o, *w):
            return E.emit("v", lambda e: e.tensor_tensor_reduce(junk, a, b, 1.0, 0.0, MUL, ADD, o), w, "v")

        def vscan(o, d0, d1, *w):
            return E.emit("v", lambda e: e.tensor_tensor_scan(o, d0, d1, 0.0, MUL, ADD), w, "v")

        def vmax(o, i, *w):
            return E.emit("v", lambda e: e.tensor_reduce(o, i, AX, MAXO), w, "v")

        def mm(o, lhsT, rhs, start, stop, *w, inc=False):
            return E.emit("pe", lambda e: e.matmul(o, lhsT, rhs, start=start, stop=stop), w, "pe" if inc else None)

        def tr(o, i, *w, inc=False):
            return E.emit("pe", lambda e: e.transpose(o, i, ident[:, :]), w, "pe" if inc else None)

        def dma(eng, o, i, sem, *w):
            return E.emit(eng, lambda e: e.dma_start(o, i), w, sem, 16)

        bank_free = [[] for _ in range(8)]
        busy = set()
        at = {"bank": 0, "ada": 16}
        ada_free = [[] for _ in range(NADA)]

        def bank():
            while at["bank"] in busy:
                at["bank"] = (at["bank"] + 1) % 8
            b = at["bank"]
            at["bank"] = (b + 1) % 8
            return b

        want = pieces()
        raw_t, raw_free = {}, [[] for _ in range(NRAW)]
        piece_t = {}
        spl_t, spl_free = {}, [[] for _ in range(NSPLIT)]
        nx = {"dma": 0, "split": 0, "use": 0, "stop": [w[0] for w in want].index("gw2")}

        def ahead():
            while nx["split"] < min(nx["use"] + AHEAD + 1, nx["stop"]):
                u = nx["split"]
                s, r = u % NSPLIT, u % NRAW
                n = want[u][3] * 128
                while nx["dma"] <= u:
                    dma_piece()
                th = act(WHs[:, s, 0:n], raw_[:, r, 0:n], ACT.Copy, raw_t[u], spl_free[s])
                tl = vtt(WLs[:, s, 0:n], raw_[:, r, 0:n], WHs[:, s, 0:n].bitcast(F32), SUB, th)
                spl_t[u] = [th, tl]
                raw_free[r] = [tl]
                nx["split"] += 1
            while nx["dma"] < min(nx["split"] + NRAW, nx["stop"]):
                dma_piece()

        def dma_piece():
            u = nx["dma"]
            name, a_, k, n = want[u]
            src = D[name][a_, k] if kinds[name] != "m" else D[name][a_, :, 128 * k:128 * (k + n)]
            raw_t[u] = dma("sp", raw_[:, u % NRAW, 0:128 * n], src, f"r{u % NRAW}", raw_free[u % NRAW])
            nx["dma"] += 1

        kinds = {n: k for n, k, _, _ in PROJ}
        sizes = {n: (nb, kc) for n, _, nb, kc in PROJ}

        def piece(*key):
            u = nx["use"]
            assert want[u][0:3] == key, (want[u], key)
            ahead()
            nx["use"] += 1
            return u % NSPLIT, spl_t[u]

        dma("sp", X[:, 0:4, :], D["xT"][:, 0:4, :], "cx")
        t_c = dma("sp", cbc, D["cb"], "cb")
        t_x0 = dma("sp", X[:, 4:8, :], D["xT"][:, 4:8, :], "cx")
        dma("sp", adab[:, :], D["adab"], "cst")
        t_ab = dma("sp", vec[:, :], D["vec"], "cst")
        ada1_t = {}
        for f in range(8):
            for j in (8, 0):
                ada1_t[j + f] = dma("sp", ada1[:, j + f], D["adaw"][j + f], f"e{j + f}")
            if f < NRAW:
                dma_piece()
        dma("g", ident[:, :], D["ident"], "cd")
        dma("g", bones[:, :], D["bones"], "cd")
        dma("g", negm[:, :], D["negm"], "cd")
        t_cst = [t_ab, dma("g", msk[:, :], D["msk"], "cd")]
        t_x = t_x0
        t_one = vset(ones[:, :], 1.0)
        t_e0 = vset(eps6[:, 0:1], 1e-6)
        t_e1 = vset(eps6[:, 1:2], 64e-5)
        def vc(name, f, w=1):
            return vec[:, VOFF[name] + f:VOFF[name] + f + w]

        t = act(sqt[0], cbc[:, 0:512], ACT.Sigmoid, t_c)
        t2 = act(sqt[1], cbc[:, 512:1024], ACT.Sigmoid, t_c)
        t_s = [vtt(cbc[:, 0:512], cbc[:, 0:512], sqt[0], MUL, t), vtt(cbc[:, 512:1024], cbc[:, 512:1024], sqt[1], MUL, t2)]
        sq_free = [t_s[0], t_s[1]]

        mod_t = {}

        def ada_step(n=1):
            for _ in range(n):
                u = at["ada"]
                if u >= 96:
                    return
                at["ada"] = u + 1
                s = u % NADA
                t = dma("g", ada[:, s], D["adaw"][u], f"d{s}", ada_free[s])
                tt = vdot(ada[:, s], ada[:, s], cbc, mod[:, u:u + 1], t, t_s)
                ada_free[s] = [tt]
                if u % 8 == 7:
                    mod_t[u // 8] = vtt(mod[:, u - 7:u + 1], mod[:, u - 7:u + 1], adab[:, u - 7:u + 1], ADD, tt, t_ab, t_cst)

        def md(layer, j, f):
            u = layer * 48 + j * 8 + f
            return mod[:, u:u + 1]

        sq_n = {"n": 0, "acc": None}

        def sumsq(src, first, *w, n=512):
            i = sq_n["n"] % 2
            sq_n["n"] += 1
            t = act(sqt[i][:, 0:n], src, ACT.Square, sq_free[i], w)
            if first:
                t = vcopy(acc[:, 0:n], sqt[i][:, 0:n], t, sq_n["acc"])
            else:
                t = vtt(acc[:, 0:n], acc[:, 0:n], sqt[i][:, 0:n], ADD, t, sq_n["acc"])
            sq_n["acc"] = t
            sq_free[i] = t
            return t

        rstd_read = {"t": []}

        def finish_norm(lhsT, count, eps, o, n=512, src=None, w=()):
            b = bank()
            t = mm(ps[:, b, 0:n], lhsT, acc[:, 0:n] if src is None else src, True, True,
                   sq_n["acc"], bank_free[b], t_one, t_cst, w, inc=True)
            if src is None:
                sq_n["acc"] = t
            ta = act(o, ps[:, b, 0:n], ACT.Sqrt, t, rstd_read["t"], t_e0, t_e1, scale=1.0 / count, bias=eps)
            bank_free[b] = [ta]
            return vrec(o, o, ta)

        def mm3(o, s, c, x, start, stop, *w, inc=False):
            hi, lo = x
            mm(o, WHs[:, s, c], hi, start, False, w)
            mm(o, WHs[:, s, c], lo, False, False)
            return mm(o, WLs[:, s, c], hi, False, stop, inc=inc)

        def proj(name, rhs, rhs_t, evac, n=512, each=None):
            nb, kc = sizes[name]
            if kinds[name] != "m":
                w = min(WIDE[kinds[name]], nb)
                for g in range(nb // w):
                    bs = [bank() for _ in range(w)]
                    busy.update(bs)
                    for k in range(kc):
                        s, tw = piece(name, g, k)
                        for m in range(w):
                            last = k == kc - 1
                            t = mm3(ps[:, bs[m], 0:n], s, slice(128 * m, 128 * m + 128), rhs(k), k == 0, last,
                                    tw, rhs_t[k], bank_free[bs[m]] if k == 0 else None, inc=last or m == w - 1)
                            if last:
                                bank_free[bs[m]] = [t]
                        spl_free[s] = [t]
                        piece_t[name, k] = t
                        if each:
                            each()
                    busy.difference_update(bs)
                    for m in range(w):
                        t_m = bank_free[bs[m]][0]
                        bank_free[bs[m]] = evac(g * w + m, ps[:, bs[m], 0:n], t_m)
            else:
                for m in range(nb):
                    b = bank()
                    for k0 in range(0, kc, 8):
                        s, tw = piece(name, m, k0)
                        k1 = min(kc, k0 + 8)
                        for k in range(k0, k1):
                            t = mm3(ps[:, b, 0:n], s, slice(128 * (k - k0), 128 * (k - k0) + 128), rhs(k), k == 0,
                                    k == kc - 1, tw, rhs_t[k], bank_free[b] if k == 0 else None, inc=k == k1 - 1)
                        spl_free[s] = [t]
                        if each:
                            each()
                    bank_free[b] = evac(m, ps[:, b, 0:n], t)
            return t

        for f in range(8):
            tq = sumsq(X[:, f], f == 0, t_x)
        x_t = [t_x] * 8
        h_free = []

        def modulated(layer, j, gname, full=False):
            hs = [None] * 8
            for _ in modulate(layer, j, gname, full, hs):
                pass
            return hs

        def modulate(layer, j, gname, full, hs):
            warm(ACT.Sqrt)
            tr_ = finish_norm(ones[:, :], 1024.0, eps6[:, 0:1], rstd)
            first = (layer, j) == (0, 0)
            if not first:
                tc = vstt(coef[:, 0:8], mod[:, layer * 48 + (j + 1) * 8:layer * 48 + (j + 2) * 8], 1.0,
                          vc(gname, 0, 8), ADD, MUL, mod_t[layer * 6 + j + 1], t_cst, h_free)
            for f in range(8):
                if first:
                    for u in (8 + f, f):
                        t = vdot(ada1[:, u], ada1[:, u], cbc, mod[:, u:u + 1], ada1_t[u], t_s)
                        mod_t[u // 8] = vtt(mod[:, u:u + 1], mod[:, u:u + 1], adab[:, u:u + 1], ADD, t, t_ab, t_cst)
                    tc = vstt(coef[:, f:f + 1], mod[:, 8 + f:9 + f], 1.0, vc(gname, f), ADD, MUL, mod_t[1])
                if full:
                    t = vstt(H[:, f, 1:513], X[:, f], coef[:, f:f + 1], rstd, MUL, MUL, tr_, tc, x_t[f], h_free)
                    hs[f] = act(H[:, f, 1:513], H[:, f, 1:513], ACT.Identity, t, mod_t[layer * 6 + j],
                                bias=md(layer, j, f))
                    yield
                    continue
                i = f % 2
                t = vstt(sqt[i], X[:, f], coef[:, f:f + 1], rstd, MUL, MUL, tr_, tc, x_t[f], sq_free[i])
                th = act(HH[:, f], sqt[i], ACT.Identity, t, mod_t[layer * 6 + j], h_free, bias=md(layer, j, f))
                tl = vstt(HL[:, f], sqt[i], md(layer, j, f), HH[:, f].bitcast(F32), ADD, SUB, th)
                sq_free[i] = tl
                hs[f] = [th, tl]
                yield
            rstd_read["t"] = hs[-1] if not full else t

        def split(hi, lo, x, t, *w, eng="v"):
            th = act(hi, x, ACT.Copy, t, w)
            if eng == "v":
                return [th, vtt(lo, x, hi.bitcast(F32), SUB, th, w)]
            return [th, gtt(lo, x, hi.bitcast(F32), SUB, th, w)]

        def plain_norm(gname, n=512, src=X, hi=HH, lo=HL, w=None):
            tr_ = finish_norm(ones[:, :], 1024.0, eps6[:, 0:1], rstd[:, 0:n], n)
            hs = []
            for f in range(8):
                i = f % 2
                t = vstt(sqt[i][:, 0:n], src[:, f, 0:n], vc(gname, f), rstd[:, 0:n], MUL, MUL, tr_, x_t[f], w, t_cst,
                         sq_free[i])
                r = split(hi[:, f], lo[:, f], sqt[i][:, 0:n], t, w)
                sq_free[i] = r[1]
                hs.append(r)
            rstd_read["t"] = hs[-1]
            return hs

        later = {}

        def residual(gate, extra, last=True, follow=None):
            def evac(m, p, t):
                if m == 0 and last:
                    warm(ACT.Sqrt)
                t1 = vstt(X[:, m], p, gate(m), X[:, m], MUL, ADD, t, x_t[m], extra)
                x_t[m] = t1
                if last:
                    sumsq(X[:, m], m == 0, t1)
                if follow:
                    gains, w = follow
                    th = act(HH[:, m], X[:, m], ACT.Identity, t1, w, h_free, scale=gains[:, m:m + 1])
                    tl = vstt(HL[:, m], X[:, m], gains[:, m:m + 1], HH[:, m].bitcast(F32), MUL, SUB, th)
                    later[m] = [th, tl]
                    x_t[m] = [t1, tl]
                return [t1]
            return evac

        hs = [None] * 8
        norm0 = modulate(0, 0, "g00", False, hs)
        next(norm0)
        ahead()
        next(norm0)

        def first_each():
            if next(norm0, "end") == "end":
                ada_step()

        cg = [cvt[:, 512 * i:512 * i + 512] for i in range(2)]
        cv = [tmp_[:, i] for i in range(4)]
        uu = [cvt[:, 1024 + 528 * i:1024 + 528 * i + 514] for i in range(2)]
        cgf = [[], []]
        up = []
        uf = [[], []]
        cvf = [[] for _ in range(4)]
        z_t = [None] * 8
        h = lambda k: (HH[:, k], HL[:, k])
        hm = lambda k: (HM[:, 0, k], HM[:, 1, k])
        hid = lambda k: (HID[:, 0, k], HID[:, 1, k])
        keep = {}

        def conv_evac(n, p, t):
            j, what = n // 3, n % 3
            i, c = j % 2, j % 4
            if what == 0:
                if j == 0:
                    up.extend(vset(u[:, 0:2], 0.0) for u in uu)
                keep["c"] = act(cg[i], p, ACT.Copy, t, cgf[i])
                return [keep["c"]]
            if what == 1:
                t1 = vtt(uu[i][:, 2:514], cg[i], p, MUL, t, keep["c"], uf[i])
                cgf[i] = [t1]
                t2 = vts(cv[c], uu[i][:, 0:512], vc("cw0", j), None, MUL, None, t1, up, cvf[c])
                t3 = vstt(cv[c], uu[i][:, 1:513], vc("cw1", j), cv[c], MUL, ADD, t2)
                keep["z"] = vstt(cv[c], uu[i][:, 2:514], vc("cw2", j), cv[c], MUL, ADD, t3)
                uf[i] = [keep["z"]]
                return [t1]
            t1 = vtt(cv[c], cv[c], p, MUL, t, keep["z"])
            z_t[j] = split(HM[:, 0, j], HM[:, 1, j], cv[c], t1)
            cvf[c] = z_t[j]
            return [t1]

        t = proj("cw_in", h, hs, conv_evac, each=first_each)
        h_free = [t]
        proj("cw_out", hm, z_t, residual(lambda m: md(0, 2, m), mod_t[2]), each=ada_step)

        tmf = [[z_t] for _ in range(4)]

        def mlp(layer, each=None, second=None):
            nonlocal h_free
            hs = modulated(layer, 3, "g%d1" % layer)
            for half in range(2):
                hid_t = [None] * 16

                def up_evac(nb, p, t):
                    i = nb % 4
                    t1 = act(tmp_[:, i], p, ACT.Relu, t, tmf[i])
                    th = act(HM[:, 0, nb], tmp_[:, i], ACT.Square, t1)
                    t2 = vtt(tmp_[:, i], tmp_[:, i], tmp_[:, i], MUL, th)
                    tl = vtt(HM[:, 1, nb], tmp_[:, i], HM[:, 0, nb].bitcast(F32), SUB, t2)
                    hid_t[nb] = [th, tl]
                    tmf[i] = [tl]
                    return [t1]

                x = "%d%s" % (layer, "ab"[half])
                t = proj("mw1_" + x, h, hs, up_evac, each=each)
                h_free = [t]
                g = residual(lambda m: md(layer, 5, m), mod_t.get(6 * layer + 5, []), half == 1,
                             second if half else None)
                t = proj("mw2_" + x, hm, hid_t, gate_late(g, layer, second and half), each=each)
            return t

        def gate_late(g, layer, second=False):
            def evac(m, p, t):
                if second:
                    return both(g, m, p, t)
                return g(m, p, [t, mod_t[6 * layer + 5]])
            return evac

        t_prev = mlp(0, ada_step)
        assert at["ada"] == 96

        hs = [None] * 8
        norm10 = modulate(1, 0, "g10", True, hs)
        pad = vset(H[:, :, 0:1], 0.0, t_prev)
        for i in range(6):
            t_omu = vts(omu[:, 8 * i:8 * i + 8], vc("mu%d" % i, 0, 8), -1.0, 1.0, MUL, ADD, t_cst)
        xm_free = [[t_prev], [t_prev]]
        xm = lambda i: (lambda k: (MX[i][0][:, k], MX[i][1][:, k]))
        mix_read = []

        m4 = [sqt[0], sqt[1], acc]
        m4f = [None] * 3

        def mix(mu, i, ts, early=None):
            for f in range(8):
                j = f % len(m4)
                ta = act(m4[j], H[:, f, 1:513], ACT.Identity, hs[f], t_omu, m4f[j],
                         scale=omu[:, 8 * mu + f:8 * mu + f + 1])
                tb = vstt(m4[j], H[:, f, 0:512], vc("mu%d" % mu, f), m4[j], MUL, ADD, ta, hs[f], pad)
                r = split(MX[i][0][:, f], MX[i][1][:, f], m4[j], tb, early(f) if early else xm_free[i], eng="gv"[f % 2])
                m4f[j] = [r]
                ts[f] = r
                mix_read[:] = [tb]
                yield

        gh_free = []

        def small_evac(func, hi, lo, toks, mul=1.0):
            def f(nb, p, t):
                t1 = act(GH[:, nb], p, func, t, gh_free)
                toks.append(t1)
                if hi is not None:
                    toks[-1] = split(hi, lo, GH[:, nb], t1, t_prev)
                    gh_free[:] = toks[-1]
                return [t1]
            return f

        def sig_evac(dst, bias, toks, w):
            def f(nb, p, t):
                toks[nb] = act(dst[:, nb], p, ACT.Sigmoid, t, w, t_cst, bias=vc(bias, nb))
                return [toks[nb]]
            return f

        def copy_evac(dst, toks, w):
            def f(nb, p, t):
                if nb % 2:
                    toks[nb] = act(dst[:, nb], p, ACT.Copy, t, w)
                else:
                    toks[nb] = vcopy(dst[:, nb], p, t, w)
                return [toks[nb]]
            return f

        def chain(*gs):
            for g in gs:
                yield from g

        def steps(g, n):
            for _ in range(n):
                next(g, None)

        m_t = [[None] * 8 for _ in range(6)]
        tw, ta_, gk = [], [], []
        a_t, k_t, v_t, r_t, l_t = [[None] * 8 for _ in range(5)]
        first = mix(3, 0, m_t[3])
        for n, _ in enumerate(norm10):
            if n == 0:
                m4f[:] = [[sq_free[0]], [sq_free[1]], [sq_n["acc"]]]
            if n < 3:
                next(first)
        m4.append(rstd)
        m4f.append([rstd_read["t"]])
        t_xout = dma("g", D["x_keep"], X[:, :, :], "ck", x_t)
        mixes = chain(first, mix(1, 1, m_t[1]), mix(4, 0, m_t[4], lambda f: piece_t["wv", f]))
        t0 = proj("wv", xm(0), m_t[3], copy_evac(V, v_t, t_prev), each=lambda: steps(mixes, 2))

        xm_free[0] = [t0]
        steps(mixes, 9)
        t0 = proj("dw1", xm(1), m_t[1], small_evac(ACT.Tanh, T64w[:, 0], T64w[:, 1], tw))
        xm_free[1] = [t0]
        steps(mix(5, 1, m_t[5]), 9)
        t0 = proj("aw1", xm(0), m_t[4], small_evac(ACT.Copy, T64a[:, 0], T64a[:, 1], ta_))
        xm_free[0] = [t0]
        mixes = mix(2, 0, m_t[2])
        t0 = proj("gw1", xm(1), m_t[5], small_evac(ACT.Sigmoid, None, None, gk), each=lambda: steps(mixes, 2))
        xm_free[1] = [t0]
        proj("aw2", lambda k: (T64a[:, 0], T64a[:, 1]), ta_, sig_evac(A, "a0", a_t, t_prev))
        mixes = chain(mixes, mix(0, 1, m_t[0]))
        t_kdone = proj("wk", xm(0), m_t[2], copy_evac(K, k_t, t_prev), each=lambda: steps(mixes, 2))
        steps(mixes, 20)
        proj("dw2", lambda k: (T64w[:, 0], T64w[:, 1]), tw, sig_evac(L, "w0", l_t, t_kdone))

        SC = -math.exp(-0.5)
        tp = [sqt[0], sqt[1], rstd, T2[:, 0], T2[:, 1]]
        tpf = [m4f[0], m4f[1], m4f[3], [], []]
        tp_n = [0]

        def temp():
            i = tp_n[0] % 5
            tp_n[0] += 1
            return i, tp[i]

        cmask = acc
        t1 = vset(cmask, 1.0, m4f[2])
        t_cm = vset(cmask[:, 0:512:128], 0.0, t1)
        VT = VY[:, 0].rearrange("p a t -> p (a t)").rearrange("p (c n) -> p c n", c=4)
        YT = VY[:, 1]
        kk_t, e_t, fc_t = [None] * 8, [None] * 8, [None] * 8

        def decays(f):
            kk_t[f] = act(H8[:, f], K[:, f], ACT.Identity, k_t[f], mix_read, hs, scale=vc("k_k", f))
            i, x = temp()
            t1 = vts(x, A[:, f], 1.0, vc("k_a", f), SUB, MUL, a_t[f], tpf[i])
            t_k = vstt(K[:, f], x, 1.0, K[:, f], ADD, MUL, t1, kk_t[f])
            tpf[i] = [t_k]
            lc = X[:, f]
            t3 = vscan(lc, cmask, L[:, f], l_t[f], t_cm, t_xout, hs)
            t4 = vcopy(lmid[:, f, :], lc[:, 63:512:128], t3)
            lm = lmid[:, f, :].rearrange("p (c o) -> p c o", o=1).to_broadcast([128, 4, 128])
            x1 = lc.rearrange("p (c t) -> p c t", t=128)
            t5 = (gtt if f < 4 else vtt)(x1, x1, lm, SUB, t4)
            fc_t[f] = vcopy(fct[:, f, :], lc[:, 127:512:128], t5)
            t6 = gtt(L[:, f], lc, L[:, f], SUB, t5)
            yield
            i, x = temp()
            t8 = act(x, lc, ACT.Exp, t5, tpf[i], scale=-SC)
            k_t[f] = gtt(K[:, f], K[:, f], x, MUL, t8, t_k)
            a_t[f] = gtt(A[:, f], A[:, f], x, MUL, t8, t1)
            tpf[i] = [a_t[f]]
            l_t[f] = act(L[:, f], L[:, f], ACT.Exp, t6, scale=SC)
            e_t[f] = act(lc, lc, ACT.Exp, t6, t8, fc_t[f], scale=SC)

        def norms(f):
            i, x = temp()
            t = act(x, H8[:, f], ACT.Square, kk_t[f], tpf[i])
            b = bank()
            t = mm(ps[:, b], bones[:, :], x, True, True, t, t_cst, bank_free[b], inc=True)
            busy.add(b)
            yield
            busy.remove(b)
            t = vts(x, ps[:, b], 1e-24, None, MAXO, None, t)
            bank_free[b] = [t]
            t = act(x, x, ACT.Sqrt, t)
            yield
            t = vrec(x, x, t)
            t = vtt(H8[:, f], H8[:, f], x, MUL, t)
            tpf[i] = [t]
            a_t[f] = gtt(A[:, f], A[:, f], H8[:, f], MUL, t, a_t[f])
            l_t[f] = vstt(L[:, f], H8[:, f], -1.0, L[:, f], MUL, MUL, l_t[f], t)
            kk_t[f] = [a_t[f], l_t[f]]

        def in_turn(gens, wide):
            live, gens = [], list(gens)
            while live or gens:
                if gens and len(live) < wide:
                    live.append(gens.pop(0))
                for x in list(live):
                    if next(x, "end") == "end":
                        live.remove(x)
                yield

        work = chain(in_turn([decays(f) for f in range(8)], 2), in_turn([norms(f) for f in range(8)], 3))

        def r_evac(nb, p, t):
            while e_t[nb] is None:
                next(work)
            r_t[nb] = vtt(R[:, nb], p, X[:, nb], MUL, t, e_t[nb], t_kdone)
            return [r_t[nb]]

        t_r = proj("wr", xm(1), m_t[0], r_evac, each=lambda: next(work, None))
        for _ in work:
            pass
        t_f = vtt(fct[:, :, 0:3], fct[:, :, 0:3], lmid[:, :, 1:4], ADD, fc_t)
        t_f = act(fct[:, :, :], fct[:, :, :], ACT.Exp, t_f, scale=SC)

        nb = lambda i, n=512: nb_[:, 512 * i:512 * i + n]
        XTb, TTb, XXb = [[nb(4 * q + i) for i in range(4)] for q in range(3)]
        Pb = [nb_[:, 6144 + 256 * i:6400 + 256 * i] for i in range(4)]
        Makb, Mkrb = [nb(14), nb(15)], [nb(16), nb(17)]
        S = nb(18)
        U = sqa[:, 2:4].rearrange("p a t -> p (a t)")
        XF = X[:, :, :].rearrange("p f t -> p (f t)")
        Wkb = [T2[:, :, :].rearrange("p a t -> p (a t)"), sqa[:, 0:2].rearrange("p a t -> p (a t)")]
        Ymb = [x[:, 0:2048].rearrange("p (g j t) -> p g j t", g=4, j=4) for x in (XF, HP)]
        Mbrb = [x[:, 2048:4096].rearrange("p (g j t) -> p g j t", g=4, j=4) for x in (XF, HP)]

        def gset(o, *w):
            return E.emit("g", lambda e: e.memset(o, 0.0), w, "g")

        for x in XXb[0:2] + Makb + Mkrb + XXb[2:4]:
            t_z = gset(x, t_r, list(spl_t.values()))
        t_z = gset(Mbrb[0], r_t, hs)
        t_z1 = gset(Mbrb[1], kk_t)
        bc = lambda m, n: m.rearrange("p (o t) -> p o t", o=1).to_broadcast([128, n, m.shape[1]])
        id4 = bc(ident[:, :], 4)
        mX, mR = bc(msk[:, 0:128].bitcast(U32), 2), bc(msk[:, 128:256].bitcast(U32), 2)
        m1 = bc(msk[:, 256:384], 4)
        q4 = lambda x: x.rearrange("p (j t) -> p j t", j=4)
        q2 = lambda x: x.rearrange("p (j t) -> p j t", j=2)

        vt_t = [None] * 8

        def turn_v():
            for f in range(8):
                b = bank()
                for c in range(4):
                    t = tr(ps[:, b, 128 * c:128 * c + 128], V[:, f, 128 * c:128 * c + 128], v_t[f], bank_free[b],
                           inc=c == 3)
                v_t[f] = t
                t = act(VT[:, :, 128 * f:128 * f + 128], ps[:, b].rearrange("p (c n) -> p c n", c=4), ACT.Copy, t, t_r)
                bank_free[b] = [t]
                vt_t[f] = t
                if f % 4 == 3:
                    yield

        def bonus():
            for f in range(8):
                x = sqt[f % 2]
                t = vstt(x, R[:, f], vc("r_k", f), K[:, f], MUL, MUL, r_t[f], k_t[f], tpf[0:2])
                b = bank()
                t = mm(ps[:, b], bones[:, :], x, True, True, t, bank_free[b], inc=True)
                tpf[f % 2] = [t]
                busy.add(b)
                yield
                busy.remove(b)
                v_t[f] = vtt(V[:, f], V[:, f], ps[:, b], MUL, t, v_t[f])
                bank_free[b] = [v_t[f]]
                yield

        def four_tr(dst, x, *w):
            b = bank()
            for j in range(4):
                t = tr(ps[:, b, 128 * j:128 * j + 128], x[:, 128 * j:128 * j + 128], w, bank_free[b], inc=j == 3)
            t = act(dst, ps[:, b], ACT.Copy, t)
            bank_free[b] = [t]
            return t

        ready = {}
        gfree = [[], []]

        dones = {-2: [kk_t, r_t], -1: [kk_t, r_t]}

        def group(c, g):
            state_done = dones[c - 2]
            t_zc = [t_z, t_z1 if c % 2 else None]
            Ym, Mbr, Wk = Ymb[c % 2], Mbrb[c % 2], Wkb[c % 2]
            Mak, Mkr = Makb[g % 2], Mkrb[g % 2]
            Xm, XT, TT, Pm = XXb[g], XTb[g], TTb[g], Pb[g]
            T = Ym[:, g].rearrange("p j t -> p (j t)")
            td = []
            cs = slice(128 * c, 128 * c + 128)
            for p in range(2):
                pp = slice(64 * p, 64 * p + 64)
                b = bank()
                for fi in range(2):
                    f = 2 * g + fi
                    t = mm(ps[:, b, 256 * fi:256 * fi + 256], A[pp, f, cs], LR[pp, :, f, cs], True, True,
                           a_t[f], l_t[f], r_t[f], bank_free[b], inc=fi == 1)
                bv = ps[:, b].rearrange("p (i r t) -> p i r t", i=2, r=2)
                m2 = slice(256 * p, 256 * p + 256)
                td.append(vpred(q2(Xm[:, m2]), mX, bv[:, :, 0], t, t_zc))
                t = vpred(Mbr[:, g, 2 * p:2 * p + 2], mR, bv[:, :, 1], t, t_zc, state_done)
                bank_free[b] = [t]
            ready[c, g, "br"] = t
            tk = []
            for p in range(2):
                pp = slice(64 * p, 64 * p + 64)
                b = bank()
                for fi in range(2):
                    f = 2 * g + fi
                    t = mm(ps[:, b, 256 * fi:256 * fi + 256], K[pp, f, cs], LR[pp, :, f, cs], True, True,
                           k_t[f], bank_free[b], inc=fi == 1)
                bv = ps[:, b].rearrange("p (i r t) -> p i r t", i=2, r=2)
                m2 = slice(256 * p, 256 * p + 256)
                vpred(q2(Mak[:, m2]), mX, bv[:, :, 0], t, gfree[g % 2])
                t = vpred(q2(Mkr[:, m2]), mR, bv[:, :, 1], t)
                bank_free[b] = [t]
                tk.append(t)
            t_x = four_tr(XT, Xm, td)
            t = vtt(q4(T), q4(Xm), m1, MUL, td, state_done)
            t_t = vtt(q4(T), q4(T), id4, ADD, t)
            yield
            b = bank()
            for j in range(4):
                p, fi = j // 2, j % 2
                hc = (2 * g + fi) * 128 + 64 * p
                t = mm(ps[:, b, 64 * j:64 * j + 64], Mak[:, 128 * j:128 * j + 128], VT[:, c, hc:hc + 64], True, True,
                       tk, vt_t[2 * g:2 * g + 2], bank_free[b], inc=j == 3)
            wd = Wk.rearrange("p (q n) -> p q n", q=2)[:, :, 128 * g:128 * g + 128]
            t = act(wd, q2(ps[:, b, 0:256]), ACT.Copy, t, state_done, tpf if c == 1 else tpf[3:5])
            bank_free[b] = [t]
            ready[c, g, "w"] = t
            b = bank()
            for j in range(4):
                p, fi = j // 2, j % 2
                hc = (2 * g + fi) * 128 + 64 * p
                t = mm(ps[64 * p:64 * p + 64, b, 128 * fi:128 * fi + 128], VT[:, c, hc:hc + 64],
                       Mkr[:, 128 * j:128 * j + 128], True, True, bank_free[b], inc=j == 3)
            gfree[g % 2] = [t]
            t = act(YT[:, 2 * g:2 * g + 2, cs], q2(ps[:, b, 0:256]), ACT.Copy, t, t_r)
            bank_free[b] = [t]
            ready[c, g, "y"] = t
            t_tt = four_tr(TT, T, t_t)
            yield
            n = 2
            for lv in range(6):
                odd = lambda x: x.rearrange("p (n two b) -> p n two b", two=2, b=n)[:, :, 1]
                b = bank()
                for j in range(4):
                    t = mm(ps[:, b, 64 * j:64 * j + 64], XT[:, 128 * j:128 * j + 128], odd(T[:, 128 * j:128 * j + 128]),
                           True, True, t_x, t_t, bank_free[b], inc=j == 3)
                t = vtt(q4(Pm), q4(ps[:, b, 0:256]), bc(msk[:, 384 + 64 * lv:448 + 64 * lv], 4), MUL, t)
                bank_free[b] = [t]
                yield
                b = bank()
                for j in range(4):
                    t = mm(ps[:, b, 64 * j:64 * j + 64], TT[:, 128 * j:128 * j + 128], Pm[:, 64 * j:64 * j + 64],
                           True, True, t_tt, t, bank_free[b], inc=j == 3)
                t_t = vtt(odd(T), odd(T), ps[:, b, 0:256].rearrange("p (n b) -> p n b", b=n), ADD, t)
                bank_free[b] = [t_t]
                yield
                if lv < 5:
                    t_tt = four_tr(TT, T, t_t)
                    yield
                n *= 2
            ready[c, g, "T"] = t_t

        s_t = [None]

        def through(c):
            cs = slice(128 * c, 128 * c + 128)
            Ym, Mbr, Wk = Ymb[c % 2], Mbrb[c % 2], Wkb[c % 2]
            done = dones[c - 1]
            tk_t = []
            w_t = []
            for p in range(2):
                pp = slice(64 * p, 64 * p + 64)
                wt = [ready[c, g, "w"] for g in range(4)]
                if c:
                    b = bank()
                    for f in range(8):
                        t = mm(ps[:, b, 64 * f:64 * f + 64], L[pp, f, cs], S[pp, 64 * f:64 * f + 64], True, True,
                               s_t, bank_free[b], inc=f == 7)
                    t = vtt(Wk[:, 512 * p:512 * p + 512], Wk[:, 512 * p:512 * p + 512], ps[:, b], ADD, t, wt)
                    bank_free[b] = [t]
                    w_t.append([t])
                else:
                    w_t.append(wt)
            yield
            if c < 3:
                for x, xt in ((A, a_t), (K, k_t)):
                    for hf in range(2):
                        b = bank()
                        for f in range(4 * hf, 4 * hf + 4):
                            t = tr(ps[:, b, 128 * (f % 4):128 * (f % 4) + 128], x[:, f, cs], bank_free[b], inc=f % 4 == 3)
                        t = act(x[:, 4 * hf:4 * hf + 4, cs], q4(ps[:, b]), ACT.Copy, t, v_t)
                        bank_free[b] = [t]
                        tk_t.append(t)
                    yield
            u_t = []
            for p in range(2):
                b = bank()
                for f in range(8):
                    t = mm(ps[:, b, 64 * f:64 * f + 64], Ym[:, f // 2, 2 * p + f % 2],
                           Wk[:, 512 * p + 64 * f:512 * p + 64 * f + 64], True, True,
                           w_t[p], [ready[c, g, "T"] for g in range(4)], bank_free[b], inc=f == 7)
                if p:
                    t = vcopy(U[:, 512:1024], ps[:, b], t, done, t_cu)
                else:
                    t = act(U[:, 0:512], ps[:, b], ACT.Copy, t, done, t_cu)
                bank_free[b] = [t]
                u_t.append(t)
            yield
            y_t = []
            for hf in range(2):
                b = bank()
                for f in range(4 * hf, 4 * hf + 4):
                    for p in range(2):
                        pp = slice(64 * p, 64 * p + 64)
                        o = ps[pp, b, 128 * (f % 4):128 * (f % 4) + 128]
                        if c:
                            mm(o, S[pp, 64 * f:64 * f + 64], R[pp, f, cs], True, False, bank_free[b], s_t)
                        t = mm(o, U[:, 512 * p + 64 * f:512 * p + 64 * f + 64], Mbr[:, f // 2, 2 * p + f % 2],
                               c == 0, True, u_t, bank_free[b], [ready[c, g, "br"] for g in range(4)],
                               inc=f % 4 == 3 and p == 1)
                yv = YT[:, 4 * hf:4 * hf + 4, cs]
                t = vtt(yv, yv, q4(ps[:, b]), ADD, t, [ready[c, g, "y"] for g in range(4)])
                bank_free[b] = [t]
                y_t.append(t)
                yield
            dones[c] = y_t
            if c < 3:
                b = bank()
                for f in range(8):
                    for p in range(2):
                        o = ps[64 * p:64 * p + 64, b, 64 * f:64 * f + 64]
                        n = slice(64 * p, 64 * p + 64)
                        mm(o, A[:, f, 128 * c + 64 * p:128 * c + 64 * p + 64], U[:, 512 * p + 64 * f:512 * p + 64 * f + 64],
                           True, False, tk_t, bank_free[b])
                        t = mm(o, K[:, f, 128 * c + 64 * p:128 * c + 64 * p + 64],
                               VT[:, c, 128 * f + 64 * p:128 * f + 64 * p + 64], False, True, inc=f == 7 and p == 1)
                fb = fct[:, :, c:c + 1].to_broadcast([128, 8, 64])
                s3 = S.rearrange("p (f v) -> p f v", v=64)
                p3 = ps[:, b].rearrange("p (f v) -> p f v", v=64)
                if c:
                    t2 = vtt(S, S, ps[:, b], ADD, t)
                    s_t[0] = vtt(s3, s3, fb, MUL, t2, t_f)
                else:
                    s_t[0] = vtt(s3, p3, fb, MUL, t, t_f, t_r)
                bank_free[b] = [s_t[0]]
                dones[c] = y_t + [s_t[0]]

        t_cu = [kk_t, t_f, tpf]
        for c in range(5):
            live = [turn_v(), bonus()] if c == 0 else [through(c - 1)]
            if c == 4:
                early = [("v", E.count["v"]), ("a", E.count["a"]), ("pe", E.count["pe"])]
                nx["stop"] = len(want)
                raw_free[:] = [list(early) for _ in range(NRAW)]
                for _ in range(NRAW):
                    dma_piece()
                x_t = [dma("sp", X[:, :, :], D["x_keep"], "cx", t_xout, early)] * 8
            else:
                live += [group(c, g) for g in range(2)]
                for _ in range(2):
                    for x in list(live):
                        if next(x, "end") == "end":
                            live.remove(x)
                live += [group(c, g) for g in range(2, 4)]
                if c:
                    live.append(live.pop(0))
            while live:
                for x in list(live):
                    if next(x, "end") == "end":
                        live.remove(x)
        y_t = dones[3]
        after = [("v", E.count["v"]), ("a", E.count["a"]), ("pe", E.count["pe"])]
        for i in range(NSPLIT):
            spl_free[i] = list(after)

        o_t = [None] * 8
        g4 = [sqa[:, i] for i in range(4)]
        g4f = [[after] for _ in range(4)]

        def group_norm(f):
            i = f % 4
            b = bank()
            t = mm(ps[:, b], bones[:, :], YT[:, f], True, True, y_t, bank_free[b], inc=True)
            busy.add(b)
            yield
            busy.remove(b)
            t = vstt(YT[:, f], ps[:, b], -1.0 / 64, YT[:, f], MUL, ADD, t)
            bank_free[b] = [t]
            t1 = act(g4[i], YT[:, f], ACT.Square, t, g4f[i])
            b = bank()
            t2 = mm(ps[:, b], bones[:, :], g4[i], True, True, t1, bank_free[b], inc=True)
            busy.add(b)
            yield
            busy.remove(b)
            t3 = act(g4[i], ps[:, b], ACT.Sqrt, t2, t_e1, scale=1.0 / 64, bias=eps6[:, 1:2])
            bank_free[b] = [t3]
            yield
            t4 = vrec(g4[i], g4[i], t3)
            t5 = vstt(YT[:, f], YT[:, f], vc("ln_w", f), g4[i], MUL, MUL, t4, t1)
            g4f[i] = [t5]
            o_t[f] = vstt(YT[:, f], YT[:, f], vc("ln_b", f), V[:, f], ADD, ADD, t5)

        for n, _ in enumerate(in_turn([group_norm(f) for f in range(8)], 4)):
            if n == 4:
                ghs = [split(GHs[:, 0, j], GHs[:, 1, j], GH[:, j], gk, after) for j in range(2)]
            if n == 6:
                ahead()
        sq_free[:] = [g4f[0], g4f[1]]
        sq_n["acc"] = g4f[2]
        rstd_read["t"] = g4f[3]

        def gate_evac(nb, p, t):
            t1 = vtt(YT[:, nb], YT[:, nb], p, MUL, t, o_t[nb])
            o_t[nb] = split(MX[0][0][:, nb], MX[0][1][:, nb], YT[:, nb], t1, after, eng="vg"[nb % 2])
            return [t1]
        proj("gw2", lambda k: (GHs[:, 0, k], GHs[:, 1, k]), ghs, gate_evac)
        proj("w_o", xm(0), o_t, residual(lambda m: md(1, 2, m), mod_t[8]))
        h_free = [x_t[7]]
        tmf = [[after] for _ in range(4)]
        fg1 = stat[:, 0:8]
        t_fg = vtt(fg1, vc("final_g", 0, 8), vc("ffn1_norm", 0, 8), MUL, t_cst)
        acc2, r1 = T2[:, 0], T2[:, 1]
        sq2 = {"t": after}

        def both(g, m, p, t):
            out = g(m, p, t)
            t2 = act(r1, X[:, m], ACT.Square, x_t[m], sq2["t"], scale=vc("final_g", m))
            if m == 0:
                sq2["t"] = vcopy(acc2, r1, t2)
            else:
                sq2["t"] = vtt(acc2, acc2, r1, ADD, t2)
            return out
        t_prev = mlp(1, None, (fg1, [t_fg, after]))

        def last_norm():
            nonlocal t_prev
            t = finish_norm(ones[:, :], 1024.0, eps6[:, 0:1], r1, w=sq2["t"])
            b = bank()
            t2 = mm(ps[:, b], ones[:, :], acc2, True, True, sq2["t"], bank_free[b], inc=True)
            t1 = vtt(rstd, r1, r1, MUL, t, rstd_read["t"])
            t1 = vtt(rstd, rstd, ps[:, b], MUL, t2, t1)
            bank_free[b] = [t1]
            t1 = act(rstd, rstd, ACT.Sqrt, t1, scale=1.0 / 1024, bias=eps6[:, 0:1])
            t1 = vrec(rstd, rstd, t1)
            t_r = vtt(rstd, rstd, r1, MUL, t1)
            rstd_read["t"] = t_r
            for f in range(8):
                x_t[f] = vstt(X[:, f], X[:, f], vc("final_g", f), r1, MUL, MUL, t_r, x_t[f])
            return [t_r, x_t[7]]

        def ffn(n, t_r):
            nonlocal h_free, t_prev
            hs = [later[m] for m in range(8)]
            pr = [tmp_[:, i] for i in range(4)] + [T2[:, 0], T2[:, 1], GH[:, 0], GH[:, 1]]
            prf = [[t_prev, t_r] for _ in range(8)]
            sgf = [[sq_free[0], sq_free[1]], [sq_free[0], sq_free[1]]]
            hid_t = [None] * 22
            keep = {"base": 0}

            def evac(nb, p, t):
                j, e = keep["base"] + nb // 2, nb % 2
                i = 2 * (j % 4) + e
                keep[j, e] = vtt(pr[i], p, rstd, MUL, t, prf[i], t_r)
                if e == 1:
                    a_, b_, c_ = pr[i - 1], pr[i], sqt[j % 2]
                    t1 = act(c_, a_, ACT.Sigmoid, keep[j, 0], sgf[j % 2])
                    t2 = gtt(a_, a_, c_, MUL, t1)
                    sgf[j % 2] = [t2]
                    waiting.append((j, i, a_, b_, t2, keep[j, 1]))
                    if len(waiting) > 1:
                        finish()
                return [keep[j, e]]

            waiting = []

            def finish():
                j, i, a_, b_, t2, t1 = waiting.pop(0)
                t3 = vtt(b_, b_, a_, MUL, t2, t1)
                prf[i - 1] = [t3]
                hid_t[j] = split(HID[:, 0, j], HID[:, 1, j], b_, t3, t_prev)
                prf[i] = hid_t[j]

            warm(ACT.Sigmoid)
            proj("f%dgu" % n, h, hs, evac)
            keep["base"] = 20
            h_free = [proj("f%dgux" % n, h, hs, evac)]
            while waiting:
                finish()
            rstd_read["t"] = [keep[21, 1]]
            sq_free[:] = [sgf, sgf]
            nxt = (vc("mix_norm", 0, 8), t_cst) if n == 1 else None
            t_prev = proj("f%dd" % n, hid, hid_t, residual(lambda m: 0.5, None, follow=nxt))

        ffn(1, last_norm())

        t_rs = finish_norm(ones[:, :], 1024.0, eps6[:, 0:1], rstd)
        hs = [later[m] for m in range(8)]
        P = lambda k: Pq[:, k]
        p_t = [None] * 24
        dec = att[:, 0:2048].rearrange("p (h t) -> p h t", h=4)
        rot = att[:, 2048:3072].rearrange("p (h t) -> p h t", h=2)
        perm = att[:, 3072:3200]
        lq = att[:, 3200:3456]
        t_at = dma("sp", att[:, 0:3200], D["att"], "cst", t_prev, h_free)
        t_at = dma("sp", lq, D["lq"], "cst", t_prev)

        def p_evac(nb, p, t):
            p_t[nb] = vtt(P(nb), p, rstd, MUL, t, t_rs, t_prev)
            return [p_t[nb]]
        h_free = [proj("w_in", h, hs, p_evac)]
        rstd_read["t"] = p_t[23]
        lqj = att[:, 3456:3584]
        ta = vdot(lqj[:, 0:64], lq[:, 0:64], lq[:, 64:128], st[:, 0:1], t_at)
        tb = vdot(lqj[:, 64:128], lq[:, 128:192], lq[:, 192:256], st[:, 1:2], t_at)
        ta = act(st[:, 2:4], st[:, 0:2], ACT.Exp, ta, tb)
        ta = vtt(st[:, 4:5], st[:, 3:4], st[:, 2:3], SUB, ta)
        t_lam = vts(st[:, 4:5], st[:, 4:5], -(0.8 - 0.6 * math.exp(-0.3 * 0)), None, ADD, None, ta)
        for k in range(4):
            b = bank()
            t = mm(ps[:, b], perm, P(k), True, True, p_t[k], t_at, bank_free[b], inc=True)
            t1 = vtt(sqt[k % 2], ps[:, b], rot[:, 1], MUL, t, sq_free[k % 2])
            bank_free[b] = [t1]
            t2 = vtt(P(k), P(k), rot[:, 0], MUL, t)
            p_t[k] = vtt(P(k), P(k), sqt[k % 2], ADD, t1, t2)
            sq_free[k % 2] = p_t[k]
        rvT, dvT = rdT[:, 0], rdT[:, 1]
        vv = []
        for dst, k0 in ((rvT, 4), (dvT, 20)):
            for k in range(4):
                b = bank()
                for c in range(4):
                    t = tr(ps[:, b, 128 * c:128 * c + 128], P(k0 + k)[:, 128 * c:128 * c + 128], p_t[k0 + k], bank_free[b],
                           inc=c == 3)
                t = act(dst[:, :, 128 * k:128 * k + 128], q4(ps[:, b]), ACT.Copy, t, t_prev)
                bank_free[b] = [t]
                vv.append(t)
        O = lambda k: (HH[:, k], HL[:, k])
        o_t = [None] * 8
        pb_ = [P(20), P(21), P(22), P(23)]
        pf = [[vv] for _ in range(4)]
        late = []

        def then():
            for x in list(late):
                if next(x, "end") == "end":
                    late.remove(x)

        def head_norm(o_bank, t, fin):
            i = sq_n["n"] % 2
            sq_n["n"] += 1
            t1 = act(sqt[i], ps[:, o_bank], ACT.Square, t, sq_free[i])
            sq_free[i] = t1

            def rest():
                b = free_bank(obs.values())
                t2 = mm(ps[:, b], ones[:, :], sqt[i], True, True, t1, bank_free[b], inc=True)
                busy.add(b)
                yield
                busy.remove(b)
                t3 = act(sqt[i], ps[:, b], ACT.Sqrt, t2, scale=1.0 / 128, bias=eps6[:, 0:1])
                bank_free[b] = [t3]
                yield
                sq_free[i] = fin(sqt[i], vrec(sqt[i], sqt[i], t3))
            late.append(rest())

        for hh in range(4):
            i = hh
            t = act(tmp2[:, i], P(8 + hh), ACT.Sigmoid, p_t[8 + hh], t_prev)
            p_t[8 + hh] = gtt(P(8 + hh), tmp2[:, i], P(8 + hh), MUL, t)
        warm(ACT.Sqrt)
        items = [(hh, q) for hh in range(4) for q in range(4)]
        sc_t, obs = {}, {}

        def ret_scores(n):
            hh, q = items[n]
            pp = slice(64 * (hh % 2), 64 * (hh % 2) + 64)
            w = 512 - 128 * q
            b = free_bank(obs.values())
            t = mm(ps[:, b, 0:w], P(2 + hh // 2)[pp, 128 * q:128 * q + 128], P(hh // 2)[pp, 128 * q:512], True, True,
                   p_t[hh // 2], p_t[2 + hh // 2], bank_free[b], inc=True)
            i = n % 4
            t = vtt(pb_[i][:, 0:w], ps[:, b, 0:w], dec[:, hh, 0:w], MUL, t, pf[i], t_at)
            bank_free[b] = [t]
            sc_t[n] = t

        def free_bank(busy):
            b = bank()
            while b in busy:
                b = bank()
            return b

        ret_scores(0)
        ret_scores(1)
        for n, (hh, q) in enumerate(items):
            if n + 2 < 16:
                ret_scores(n + 2)
            if q == 0:
                obs[hh] = free_bank(obs.values())
            w = 512 - 128 * q
            i = n % 4
            t = mm(ps[:, obs[hh], 128 * q:512], rvT[:, q, 128 * hh:128 * hh + 128], pb_[i][:, 0:w], q == 0, q == 3,
                   sc_t[n], vv, bank_free[obs[hh]] if q == 0 else None, inc=True)
            pf[i] = [t]
            if q < 3:
                then()
            if q == 3:
                def fin(r, t4, hh=hh, ob=obs[hh]):
                    t5 = vstt(r, ps[:, ob], vc("ret_norm", hh), r, MUL, MUL, t4)
                    bank_free[ob] = [t5]
                    t6 = vtt(r, r, P(8 + hh), MUL, t5, p_t[8 + hh])
                    o_t[hh] = split(HH[:, hh], HL[:, hh], r, t6, h_free)
                    del obs[hh]
                    return o_t[hh]
                head_norm(obs[hh], t, fin)

        EB = [P(4 + i) for i in range(4)] + [P(20 + i) for i in range(4)]
        ebf = [[vv] for _ in range(4)] + [[pf[i]] for i in range(4)]
        atf = [[t_prev, h_free, p_t[8:12]], [t_prev, h_free]]
        es_of, evs = {}, {}
        n_s = [0]

        def diff_scores(n):
            hh, i = items[n]
            w = 128 * (i + 1)
            es = []
            for cc in range(2):
                pp = slice(64 * cc, 64 * cc + 64)
                b = free_bank(obs.values())
                mm(ps[:, b, 0:w], P(12 + hh)[pp, 128 * i:128 * i + 128], P(16 + hh)[pp, 0:w], True, False,
                   p_t[12 + hh], p_t[16 + hh], bank_free[b])
                t = mm(ps[:, b, w - 128:w], ident[:, :], negm[:, :], False, True, inc=True)
                x = n_s[0] % 8
                n_s[0] += 1
                sc = stat[:, 4 * x:4 * x + 4]
                t1 = vmax(sc[:, 0:1], ps[:, b, 0:w], t, ebf[x])
                t2 = vts(sc[:, 1:2], sc[:, 0:1], -0.125, None, MUL, None, t1)
                t3 = act(EB[x][:, 0:w], ps[:, b, 0:w], ACT.Exp, t2, ebf[x], scale=0.125, bias=sc[:, 1:2], accum=sc[:, 2:3])
                bank_free[b] = [t3]
                es.append((x, sc, t3))
            if shares:
                shares.pop()()
            shares.append(lambda: diff_shares(n, w, es))

        shares = []

        def diff_shares(n, w, es):
            (x0, s0_, ta), (x1, s1_, tb) = es
            ta, tb = vrec(s0_[:, 3:4], s0_[:, 2:3], ta), vrec(s1_[:, 3:4], s1_[:, 2:3], tb)
            t5 = vts(EB[x0][:, 0:w], EB[x0][:, 0:w], s0_[:, 3:4], None, MUL, None, ta)
            t6 = vtt(s1_[:, 3:4], s1_[:, 3:4], st[:, 4:5], MUL, tb, t_lam)
            t7 = vstt(EB[x0][:, 0:w], EB[x1][:, 0:w], s1_[:, 3:4], EB[x0][:, 0:w], MUL, ADD, t5, t6)
            es_of[n] = (x0, x1, t7)

        diff_scores(0)
        diff_scores(1)
        diff_scores(2)
        warm(ACT.Exp)
        for n, (hh, i) in enumerate(items):
            w = 128 * (i + 1)
            if n not in es_of:
                shares.pop()()
            x0, x1, t7 = es_of[n]
            b = free_bank(obs.values())
            for j in range(i + 1):
                t = tr(ps[:, b, 128 * j:128 * j + 128], EB[x0][:, 128 * j:128 * j + 128], t7, bank_free[b], inc=j == i)
            ebf[x0], ebf[x1] = [t], [t7]
            t = act(atb[:, hh % 2, 0:i + 1, 128 * i:128 * i + 128], ps[:, b, 0:w].rearrange("p (j q) -> p j q", q=128),
                    ACT.Copy, t, atf[hh % 2])
            bank_free[b] = [t]
            evs.setdefault(hh, []).append(t)
            if n + 3 < 16:
                diff_scores(n + 3)
            if i < 3:
                then()
            if i == 3:
                ob = free_bank(obs.values())
                obs[hh] = ob
                for j in range(4):
                    t = mm(ps[:, ob, 128 * j:512], dvT[:, j, 128 * hh:128 * hh + 128], atb[:, hh % 2, j, 128 * j:512],
                           j == 0, j == 3, evs[hh], vv, bank_free[ob], inc=j == 3)
                atf[hh % 2] = [t]

                def fin(r, t4, hh=hh, ob=ob):
                    t5 = vstt(r, ps[:, ob], vc("diff_norm", hh), r, MUL, MUL, t4)
                    bank_free[ob] = [t5]
                    t6 = vts(r, r, 1.0 - (0.8 - 0.6 * math.exp(-0.3 * 0)), None, MUL, None, t5)
                    o_t[4 + hh] = split(HH[:, 4 + hh], HL[:, 4 + hh], r, t6, h_free)
                    del obs[hh]
                    return o_t[4 + hh]
                head_norm(ob, t, fin)
        while late:
            then()
        t = proj("w_out", O, o_t, residual(lambda m: 1.0, None))
        h_free = [t]
        t_prev = [t, atf, ("g", E.count["g"]), ("v", E.count["v"]), ("a", E.count["a"])]

        t_m = dma("sp", MEM[:, :, :], D["memT"], "cx", t_prev)
        hs = plain_norm("xattn_norm", w=h_free)
        q_t = [None] * 8
        kv_t = [None] * 16
        ms = []

        def mem_norm():
            for f in range(8):
                sumsq(MEM[:, f], f == 0, t_m, n=256)
                yield
            t_r2 = finish_norm(ones[:, :], 1024.0, eps6[:, 0:1], rstd[:, 0:256], 256)
            yield
            for f in range(8):
                i = f % 2
                t = vstt(sqt[i][:, 0:256], MEM[:, f], vc("mem_norm", f), rstd[:, 0:256], MUL, MUL, t_r2, t_m, sq_free[i])
                r = split(MNs[:, 0, f], MNs[:, 1, f], sqt[i][:, 0:256], t, t_prev)
                sq_free[i] = r[1]
                ms.append(r)
                if f % 2:
                    yield
            rstd_read["t"] = ms[-1]

        memory = mem_norm()
        h_free = [proj("wq", h, hs, copy_evac(Qx, q_t, t_prev), each=lambda: next(memory, None))]
        for _ in memory:
            pass

        def kv_evac(nb, p, t):
            o = KTm[:, nb] if nb < 8 else VFm[:, nb - 8]
            kv_t[nb] = act(o, p, ACT.Copy, t, t_prev) if nb % 2 else vcopy(o, p, t, t_prev)
            return [kv_t[nb]]
        t_kv = proj("wkv", lambda k: (MNs[:, 0, k], MNs[:, 1, k]), ms, kv_evac, n=256)
        mv_t = []
        for k in range(8):
            b = bank()
            for c in range(2):
                t = tr(ps[:, b, 128 * c:128 * c + 128], VFm[:, k, 128 * c:128 * c + 128], kv_t[8 + k], bank_free[b], inc=c == 1)
            t = act(MV[:, :, 128 * k:128 * k + 128], q2(ps[:, b, 0:256]), ACT.Copy, t, t_prev)
            bank_free[b] = [t]
            mv_t.append(t)
        ptf = [[t_prev], [t_prev]]
        ebf = [[t_prev] for _ in range(4)]
        es_of, evs = {}, {}

        def x_scores(n):
            hh, i = items[n]
            b = bank()
            for e in range(2):
                t = mm(ps[:, b, 0:256], Qx[:, 2 * hh + e, 128 * i:128 * i + 128], KTm[:, 2 * hh + e], e == 0, e == 1,
                       q_t[2 * hh + e], kv_t[2 * hh + e], bank_free[b], inc=e == 1)
            x = n % 4
            sc = stat[:, 4 * x:4 * x + 4]
            t1 = vmax(sc[:, 0:1], ps[:, b, 0:256], t, ebf[x])
            t2 = vts(sc[:, 1:2], sc[:, 0:1], -0.0625, None, MUL, None, t1)
            t3 = act(EBx[:, x], ps[:, b, 0:256], ACT.Exp, t2, ebf[x], scale=0.0625, bias=sc[:, 1:2], accum=sc[:, 2:3])
            bank_free[b] = [t3]
            if shares:
                shares.pop()()
            shares.append(lambda: x_shares(n, x, sc, t3))

        shares = []

        def x_shares(n, x, sc, t3):
            t4 = vrec(sc[:, 3:4], sc[:, 2:3], t3)
            es_of[n] = vts(EBx[:, x], EBx[:, x], sc[:, 3:4], None, MUL, None, t4)

        for n in range(3):
            x_scores(n)
        for n, (hh, i) in enumerate(items):
            x = n % 4
            if n not in es_of:
                shares.pop()()
            b = bank()
            for j in range(2):
                t = tr(ps[:, b, 128 * j:128 * j + 128], EBx[:, x, 128 * j:128 * j + 128], es_of[n], bank_free[b], inc=j == 1)
            ebf[x] = [t]
            t = act(PTx[:, hh % 2, :, 128 * i:128 * i + 128], q2(ps[:, b, 0:256]), ACT.Copy, t, ptf[hh % 2])
            bank_free[b] = [t]
            evs.setdefault(hh, []).append(t)
            if n + 3 < 16:
                x_scores(n + 3)
            if i == 3:
                for e in range(2):
                    b = bank()
                    for j in range(2):
                        t = mm(ps[:, b], MV[:, j, 256 * hh + 128 * e:256 * hh + 128 * e + 128], PTx[:, hh % 2, j], j == 0, j == 1,
                               evs[hh], mv_t, bank_free[b], inc=j == 1)
                    k = 2 * hh + e
                    th = act(OX[0][:, k], ps[:, b], ACT.Copy, t, t_kv)
                    o_t[k] = [th, vtt(OX[1][:, k], ps[:, b], OX[0][:, k].bitcast(F32), SUB, th)]
                    bank_free[b] = [o_t[k][1]]
                ptf[hh % 2] = [t]
        t = proj("wo", lambda k: (OX[0][:, k], OX[1][:, k]), o_t,
                 residual(lambda m: 1.0, None, follow=(vc("ffn2_norm", 0, 8), t_cst)))
        t_prev = [t, ("g", E.count["g"]), ("v", E.count["v"]), ("a", E.count["a"])]

        ffn(2, finish_norm(ones[:, :], 1024.0, eps6[:, 0:1], rstd))
        tr_ = finish_norm(ones[:, :], 1024.0, eps6[:, 0:1], rstd)
        for f in range(8):
            t = vstt(OUT[:, f], X[:, f], vc("final_norm", f), rstd, MUL, MUL, tr_, x_t[f], t_prev)
            t_out = dma("sp", out[:, f, :], OUT[:, f], "out", t)
        E.emit("sp", lambda e: e.nop(), [t_out])

        block = ctx.enter_context(nc.Block())

        @block.sync
        def _(eng):
            E.play("sp", eng)

        @block.gpsimd
        def _(eng):
            E.play("g", eng)

        @block.scalar
        def _(eng):
            E.play("a", eng)

        @block.vector
        def _(eng):
            E.play("v", eng)

        @block.tensor
        def _(eng):
            E.play("pe", eng)


def kernel(**inp):
    import numpy as np
    import concourse.bacc as bacc
    from concourse import mybir as mb
    from concourse.bass_utils import run_bass_kernel_spmd as run

    a = {k: np.asarray(v) for k, v in inp.items()}

    def blocks(w, m=128):
        K, N = w.shape
        return w.reshape(K // 128, 128, N // m, m).transpose(2, 1, 0, 3).reshape(N // m, 128, K // 128 * m)

    def feat(v):
        return v.reshape(-1, 128).T

    d = {}
    d["xT"] = a["x"][0].T.reshape(8, 128, 512).transpose(1, 0, 2)
    d["memT"] = a["mem_2"][0].T.reshape(8, 128, 256).transpose(1, 0, 2)
    d["cb"] = np.broadcast_to(a["c"], (128, 1024))
    d["adab"] = feat(a["ada_b"].reshape(-1))
    d["adaw"] = a["ada_w"].transpose(0, 2, 1).reshape(96, 128, 1024)
    pad = np.zeros((128, 4), np.float32)
    cols = {"g00": a["norm_g"][0, 0], "g01": a["norm_g"][0, 1], "g10": a["norm_g"][1, 0], "g11": a["norm_g"][1, 1],
            "final_g": a["final_g"], "cw0": a["conv_w"][0, 0], "cw1": a["conv_w"][0, 1], "cw2": a["conv_w"][0, 2],
            "w0": a["rw_w0"], "a0": a["rw_a0"], "k_k": a["rw_k_k"], "k_a": a["rw_k_a"], "r_k": a["rw_r_k"],
            "ln_w": a["rw_ln_w"], "ln_b": a["rw_ln_b"], "ffn1_norm": a["ffn1_norm_2"], "mix_norm": a["mix_norm_2"],
            "xattn_norm": a["xattn_norm_2"], "mem_norm": a["mem_norm_2"], "ffn2_norm": a["ffn2_norm_2"],
            "final_norm": a["final_norm_2"], "ret_norm": a["ret_out_norm_2"], "diff_norm": a["diff_out_norm_2"]}
    for i in range(6):
        cols["mu%d" % i] = a["rw_mu"][0, i]
    d["vec"] = np.concatenate([x for n in VECS for x in ([feat(cols[n].reshape(-1))] +
                                                         ([pad] if cols[n].size == 512 else []))], axis=1)
    def kpieces(w, per=8):
        K, N = w.shape
        return w.reshape(K // 128, 128, N // (128 * per), 128 * per).transpose(2, 0, 1, 3)

    def woven(*ws):
        K = ws[0].shape[0]
        return np.stack([w.reshape(K, -1, 128) for w in ws], axis=2).reshape(K, -1)

    def padded(w, K, N):
        out = np.zeros((K, N), w.dtype)
        out[0:w.shape[0], 0:w.shape[1]] = w
        return out

    wb, wc, wh = np.split(a["conv_w_in"][0], 3, axis=1)
    d["cw_in"] = kpieces(woven(wc, wh, wb))
    d["cw_out"] = blocks(a["conv_w_out"][0])
    for i in range(2):
        for j in range(2):
            x = "%d%s" % (i, "ab"[j])
            d["mw1_" + x] = kpieces(a["mlp_w1"][i][:, 2048 * j:2048 * j + 2048])
            d["mw2_" + x] = blocks(a["mlp_w2"][i][2048 * j:2048 * j + 2048])
    d["wr"], d["wk"], d["wv"] = [kpieces(a["rw_w_rkv"][0, i], WIDE[k]) for i, k in enumerate("hkk")]
    d["w_o"] = blocks(a["rw_w_o"][0])
    d["dw1"] = blocks(padded(a["rw_w1"][0], 1024, 128))
    d["aw1"] = blocks(padded(a["rw_a1"][0], 1024, 128))
    d["gw1"] = blocks(padded(a["rw_g1"][0], 1024, 256))
    d["dw2"] = kpieces(padded(a["rw_w2"][0], 128, 1024))
    d["aw2"] = kpieces(padded(a["rw_a2"][0], 128, 1024))
    d["gw2"] = kpieces(padded(a["rw_g2"][0], 256, 1024))
    for i in (1, 2):
        w = woven(a["ffn%d_w_gate_2" % i][0], a["ffn%d_w_up_2" % i][0])
        d["f%dgu" % i] = kpieces(w[:, 0:5120])
        d["f%dgux" % i] = kpieces(w[:, 5120:], 4)
        d["f%dd" % i] = blocks(a["ffn%d_w_down_2" % i][0])
    d["w_in"] = kpieces(a["w_in_2"][0])
    d["w_out"] = blocks(a["w_out_2"][0])
    d["wq"] = kpieces(a["xattn_wq_2"][0], WIDE["h"])
    d["wkv"] = kpieces(a["xattn_wkv_2"][0])
    d["wo"] = blocks(a["xattn_wo_2"][0])
    d["lq"] = np.broadcast_to(np.concatenate([a["diff_lq1_2"], a["diff_lk1_2"], a["diff_lq2_2"], a["diff_lk2_2"]], 1), (128, 256))

    i = np.arange(128)
    d["ident"] = np.eye(128, dtype=np.float32)
    d["bones"] = (i[:, None] // 64 == i[None, :] // 64).astype(np.float32)
    d["negm"] = np.where(i[None, :] > i[:, None], np.float32(-1e30), np.float32(0))
    m = [i[:, None] < i[None, :], i[:, None] <= i[None, :], (i[:, None] // 2 == i[None, :] // 2) & (i[:, None] < i[None, :])]
    b = 2
    while b < 128:
        t = i[(i // b) % 2 == 1]
        m.append((i[:, None] // (2 * b) == t[None, :] // (2 * b)) & ((i[:, None] // b) % 2 == 0))
        b *= 2
    d["msk"] = np.concatenate(m, axis=1).astype(np.float32)
    rel = np.arange(512)[None, :] - i[:, None]
    dec = []
    for hh in range(4):
        lg = np.log(1.0 - 2.0 ** (-5.0 - hh))
        dec.append(np.where(rel >= 0, np.exp(np.maximum(rel, 0) * lg), 0.0) * 64.0 ** -0.5)
    inv = (1.0 / (np.float32(10000.0) ** (np.arange(0, 64, 2, dtype=np.float32) / np.float32(64)))).astype(np.float32)
    ang = (np.arange(512, dtype=np.float32)[None, :] * inv[i % 32][:, None]).astype(np.float32).astype(np.float64)
    perm = np.zeros((128, 128))
    for m in range(128):
        if m % 64 < 32:
            perm[m + 32, m] = -1.0
        else:
            perm[m - 32, m] = 1.0
    d["att"] = np.concatenate(dec + [np.cos(ang), np.sin(ang), perm], axis=1).astype(np.float32)

    nc = bacc.Bacc("TRN2", target_bir_lowering=False, num_devices=1)
    arrays, D = {}, {}
    for n, v in d.items():
        v = np.ascontiguousarray(v)
        arrays["in_" + n] = v
        D[n] = nc.dram_tensor("in_" + n, v.shape, mb.dt.from_np(v.dtype), kind="ExternalInput").ap()
    D["x_keep"] = nc.dram_tensor("x_keep", (128, 8, 512), mb.dt.float32, kind="Internal").ap()
    o = nc.dram_tensor("out_dram", (128, 8, 512), mb.dt.float32, kind="ExternalOutput").ap()
    build(nc, D, o)
    r = run(nc, [arrays], core_ids=[0])
    got = r.results[0]["out_dram"]
    return np.ascontiguousarray(got.transpose(2, 1, 0).reshape(1, 512, 1024))
```
